# Optimizing a Trainium2 kernel written in Bass

```python
import math
import jax
import jax.numpy as jnp
from jax import lax
import numpy as np

D_MODEL = 1024
BATCH = 1
SEQ = 256
DEPTH = 2
DEC_BATCH = 1
DEC_SEQ = 512
PAST_LEN = 128

PLE_DIM = 256
HG_WIDTH = D_MODEL // 2
HG_HEADS = 4
HG_DK = HG_WIDTH // HG_HEADS
HG_DV = HG_WIDTH // HG_HEADS
HG_CHUNK = 64
LB_FLOOR = 1e-30
DA_WIDTH = D_MODEL // 2
DA_HEADS = 4
DA_DV = DA_WIDTH // DA_HEADS
DA_DH = DA_DV // 2
Q_BLOCK = 128
D_FF = 2816
CONV_W = 3
ROPE_THETA = 10000.0
EPS = 1e-6
IN_COLS = 5 * HG_WIDTH + 3 * DA_WIDTH + 2 * D_MODEL

kernel_name = "hybrid_hgrn2_diffattn_encoder"

def rms_norm(x, w):
    xf = x.astype(jnp.float32)
    y = xf * lax.rsqrt(jnp.mean(xf * xf, axis=-1, keepdims=True) + EPS)
    return (y * w.astype(jnp.float32)).astype(x.dtype)

def rms_unit(x):
    xf = x.astype(jnp.float32)
    return (xf * lax.rsqrt(jnp.mean(xf * xf, axis=-1, keepdims=True) + EPS)).astype(x.dtype)

def rope_tables(L, dtype):
    inv = 1.0 / (ROPE_THETA ** (jnp.arange(0, DA_DH, 2, dtype=jnp.float32) / DA_DH))
    ang = jnp.arange(L, dtype=jnp.float32)[:, None] * inv[None, :]
    ang = jnp.concatenate([ang, ang], axis=-1)
    return jnp.cos(ang).astype(dtype), jnp.sin(ang).astype(dtype)

def apply_rope(x, cos, sin):
    x1, x2 = jnp.split(x, 2, axis=-1)
    return x * cos + jnp.concatenate([-x2, x1], axis=-1) * sin

def gla_chunk_scan(q, k, v, log_f):
    B, H, L, dk = q.shape
    dv = v.shape[-1]
    n = L // HG_CHUNK

    def to_chunks(a):
        return jnp.moveaxis(a.reshape(B, H, n, HG_CHUNK, a.shape[-1]), 2, 0)

    causal = jnp.tril(jnp.ones((HG_CHUNK, HG_CHUNK), dtype=bool))[:, :, None]

    def step(S, inp):
        qc, kc, vc, gc = inp
        b = jnp.cumsum(gc, axis=-2)
        diff = b[..., :, None, :] - b[..., None, :, :]
        decay = jnp.where(causal, jnp.exp(jnp.where(causal, diff, 0.0)), 0.0)
        A = jnp.einsum('bhtk,bhsk,bhtsk->bhts', qc, kc, decay)
        o = (jnp.einsum('bhts,bhsv->bhtv', A, vc)
             + jnp.einsum('bhtk,bhkv->bhtv', qc * jnp.exp(b), S))
        b_last = b[..., -1:, :]
        S = (jnp.exp(b_last[..., 0, :])[..., None] * S
             + jnp.einsum('bhsk,bhsv->bhkv', kc * jnp.exp(b_last - b), vc))
        return S, o

    S0 = jnp.zeros((B, H, dk, dv), jnp.float32)
    _, o = lax.scan(step, S0, (to_chunks(q), to_chunks(k), to_chunks(v), to_chunks(log_f)))
    return jnp.moveaxis(o, 0, 2).reshape(B, H, L, dv)

def hgrn2_mixer(q_raw, f_fw_raw, f_bw_raw, i_raw, g_raw, lb, gnorm_w):
    B, L, _ = q_raw.shape
    dt = q_raw.dtype

    def heads(a):
        return a.reshape(B, L, HG_HEADS, -1).transpose(0, 2, 1, 3)

    q = heads(jax.nn.silu(q_raw.astype(jnp.float32))) * (HG_DK ** -0.5)
    v = heads(i_raw.astype(jnp.float32))

    def gates(f_raw, lb_d):
        z = f_raw.astype(jnp.float32)
        log_f = jnp.logaddexp(jnp.log(jnp.maximum(lb_d, LB_FLOOR)),
                              jnp.log1p(-lb_d) + jax.nn.log_sigmoid(z))
        k = (1.0 - lb_d) * jax.nn.sigmoid(-z)
        return heads(k), heads(log_f)

    k_fw, g_fw = gates(f_fw_raw, lb[0])
    k_bw, g_bw = gates(f_bw_raw, lb[1])
    o_fw = gla_chunk_scan(q, k_fw, v, g_fw)
    o_bw = jnp.flip(gla_chunk_scan(jnp.flip(q, 2), jnp.flip(k_bw, 2), jnp.flip(v, 2), jnp.flip(g_bw, 2)), 2)
    o = (o_fw + o_bw).transpose(0, 2, 1, 3)
    gate = jax.nn.silu(g_raw.astype(jnp.float32).reshape(B, L, HG_HEADS, HG_DV))
    o = rms_norm(o, gnorm_w) * gate
    return o.reshape(B, L, HG_WIDTH).astype(dt)

def diff_attention(q_raw, k_raw, v_raw, lam_params, lambda_init, subln_w, cos, sin):
    B, L, _ = q_raw.shape
    q = q_raw.reshape(B, L, DA_HEADS, 2, DA_DH).transpose(0, 2, 3, 1, 4)
    k = k_raw.reshape(B, L, DA_HEADS, 2, DA_DH).transpose(0, 2, 3, 1, 4)
    v = v_raw.reshape(B, L, DA_HEADS, DA_DV).transpose(0, 2, 1, 3)
    q = apply_rope(q, cos, sin) * (DA_DH ** -0.5)
    k = apply_rope(k, cos, sin)
    lp = lam_params.astype(jnp.float32)
    lam = jnp.exp(jnp.sum(lp[0] * lp[1])) - jnp.exp(jnp.sum(lp[2] * lp[3])) + lambda_init
    nb = L // Q_BLOCK
    qb = jnp.moveaxis(q.reshape(B, DA_HEADS, 2, nb, Q_BLOCK, DA_DH), 3, 0)

    def block(q_blk):
        s = jnp.einsum('bhmqd,bhmkd->bhmqk', q_blk, k).astype(jnp.float32)
        p = jax.nn.softmax(s, axis=-1)
        a = p[:, :, 0] - lam * p[:, :, 1]
        return jnp.einsum('bhqk,bhkv->bhqv', a.astype(v.dtype), v)

    o = lax.map(block, qb)
    o = jnp.moveaxis(o, 0, 2).reshape(B, DA_HEADS, L, DA_DV)
    o = rms_norm(o, subln_w) * (1.0 - lambda_init)
    return o.transpose(0, 2, 1, 3).reshape(B, L, DA_WIDTH)

def conv_ffn(h, w_up, conv_w, conv_b, w_down):
    u = h @ w_up
    up = jnp.pad(u, ((0, 0), (1, 1), (0, 0)))
    c = up[:, :-2] * conv_w[0] + up[:, 1:-1] * conv_w[1] + up[:, 2:] * conv_w[2] + conv_b
    gate, val = jnp.split(c, 2, axis=-1)
    return (jax.nn.gelu(gate, approximate=True) * val) @ w_down

def _trunk(x, p, w_in, hgrn_lb_logits, hgrn_gnorm, diff_lambda, diff_subln,
           w_branch_a, w_branch_b, w_out, norm_mix_pre, norm_mix_post,
           w_up, conv_w, conv_b, w_down, norm_ffn_pre, norm_ffn_post,
           w_ple, w_ple_gate, norm_ple):
    L = x.shape[1]
    cos, sin = rope_tables(L, x.dtype)
    lb = jax.nn.softmax(hgrn_lb_logits.astype(jnp.float32), axis=0)
    lb = jnp.cumsum(lb, axis=0) - lb[0]
    splits = ([HG_WIDTH * i for i in range(1, 6)]
              + [5 * HG_WIDTH + DA_WIDTH * i for i in range(1, 4)]
              + [5 * HG_WIDTH + 3 * DA_WIDTH + D_MODEL])
    for l in range(DEPTH):
        lambda_init = 0.8 - 0.6 * math.exp(-0.3 * l)
        h = rms_norm(x, norm_mix_pre[l])
        z = h @ w_in[l]
        q_h, f_fw, f_bw, i_h, g_h, q_d, k_d, v_d, gate_a, gate_b = jnp.split(z, splits, axis=-1)
        a = hgrn2_mixer(q_h, f_fw, f_bw, i_h, g_h, lb[l], hgrn_gnorm[l])
        b = diff_attention(q_d, k_d, v_d, diff_lambda[l], lambda_init, diff_subln[l], cos, sin)
        m = jax.nn.sigmoid(gate_a) * (a @ w_branch_a[l]) + jax.nn.sigmoid(gate_b) * (b @ w_branch_b[l])
        x = x + rms_norm(m @ w_out[l], norm_mix_post[l])
        f = conv_ffn(rms_norm(x, norm_ffn_pre[l]), w_up[l], conv_w[l], conv_b[l], w_down[l])
        x = x + rms_norm(f, norm_ffn_post[l])
        e = p[l] @ w_ple[l]
        g = jax.nn.sigmoid(rms_unit(x) @ w_ple_gate[l])
        x = x + rms_norm(g * e, norm_ple[l])
    return x

def setup_inputs(seed: int = 0) -> dict:
    key = jax.random.key(seed)
    ks = jax.random.split(key, 24)

    def nrm(k, shape, s):
        return s * jax.random.normal(k, shape, jnp.float32)

    def gain(k, shape):
        return 1.0 + 0.05 * jax.random.normal(k, shape, jnp.float32)

    return {
        "x_prompt": nrm(ks[0], (BATCH, SEQ, D_MODEL), 1.0),
        "x_sample": nrm(ks[1], (DEC_BATCH, DEC_SEQ, D_MODEL), 1.0),
        "p_prompt": nrm(ks[2], (DEPTH, BATCH, SEQ, PLE_DIM), 1.0),
        "p_sample": nrm(ks[3], (DEPTH, DEC_BATCH, DEC_SEQ, PLE_DIM), 1.0),
        "w_in": nrm(ks[4], (DEPTH, D_MODEL, IN_COLS), D_MODEL ** -0.5),
        "hgrn_lb_logits": nrm(ks[5], (DEPTH, 2, HG_WIDTH), 0.1),
        "hgrn_gnorm": gain(ks[6], (DEPTH, HG_DV)),
        "diff_lambda": nrm(ks[7], (DEPTH, 4, DA_DH), 0.1),
        "diff_subln": gain(ks[8], (DEPTH, DA_DV)),
        "w_branch_a": nrm(ks[9], (DEPTH, HG_WIDTH, D_MODEL), HG_WIDTH ** -0.5),
        "w_branch_b": nrm(ks[10], (DEPTH, DA_WIDTH, D_MODEL), DA_WIDTH ** -0.5),
        "w_out": nrm(ks[11], (DEPTH, D_MODEL, D_MODEL), D_MODEL ** -0.5),
        "norm_mix_pre": gain(ks[12], (DEPTH, D_MODEL)),
        "norm_mix_post": gain(ks[13], (DEPTH, D_MODEL)),
        "w_up": nrm(ks[14], (DEPTH, D_MODEL, 2 * D_FF), D_MODEL ** -0.5),
        "conv_w": nrm(ks[15], (DEPTH, CONV_W, 2 * D_FF), CONV_W ** -0.5),
        "conv_b": nrm(ks[16], (DEPTH, 2 * D_FF), 0.01),
        "w_down": nrm(ks[17], (DEPTH, D_FF, D_MODEL), D_FF ** -0.5),
        "norm_ffn_pre": gain(ks[18], (DEPTH, D_MODEL)),
        "norm_ffn_post": gain(ks[19], (DEPTH, D_MODEL)),
        "w_ple": nrm(ks[20], (DEPTH, PLE_DIM, D_MODEL), PLE_DIM ** -0.5),
        "w_ple_gate": nrm(ks[21], (DEPTH, D_MODEL, D_MODEL), D_MODEL ** -0.5),
        "norm_ple": gain(ks[22], (DEPTH, D_MODEL)),
    }

def reference(x_prompt, x_sample, p_prompt, p_sample, w_in, hgrn_lb_logits, hgrn_gnorm,
              diff_lambda, diff_subln, w_branch_a, w_branch_b, w_out, norm_mix_pre,
              norm_mix_post, w_up, conv_w, conv_b, w_down, norm_ffn_pre, norm_ffn_post,
              w_ple, w_ple_gate, norm_ple):
    y_prompt = _trunk(x_prompt, p_prompt, w_in, hgrn_lb_logits, hgrn_gnorm, diff_lambda,
                      diff_subln, w_branch_a, w_branch_b, w_out, norm_mix_pre, norm_mix_post,
                      w_up, conv_w, conv_b, w_down, norm_ffn_pre, norm_ffn_post,
                      w_ple, w_ple_gate, norm_ple)
    y_sample = _trunk(x_sample, p_sample, w_in, hgrn_lb_logits, hgrn_gnorm, diff_lambda,
                      diff_subln, w_branch_a, w_branch_b, w_out, norm_mix_pre, norm_mix_post,
                      w_up, conv_w, conv_b, w_down, norm_ffn_pre, norm_ffn_post,
                      w_ple, w_ple_gate, norm_ple)
    return (y_prompt, y_sample)


_drawn_inputs = setup_inputs


def setup_inputs(seed=0):
    import zlib

    import numpy as np

    out = dict(_drawn_inputs(seed))
    spreads = {}
    factors = {'hgrn_lb_logits': 21.666, 'conv_b': 5.339}
    for name, (base, spread) in spreads.items():
        noise = np.random.default_rng([zlib.crc32(name.encode()), seed]).standard_normal(out[name].shape)
        drawn = base * np.exp(spread * noise) if base else spread * noise
        out[name] = jnp.asarray(drawn.astype(out[name].dtype))
    for name, factor in factors.items():
        out[name] = (out[name] * factor).astype(out[name].dtype)
    return out
```

```python
import math
from contextlib import ExitStack

import concourse.bass as bass
from concourse import mybir

ALU = mybir.AluOpType
ACT = mybir.ActivationFunctionType
F32 = mybir.dt.float32
F32R = mybir.dt.float32r
U8 = mybir.dt.uint8
AX_X = mybir.AxisListType.X

P = 128
DEPTH = 2
TP, TS = 256, 512
T = TP + TS
NT = T // P
D = 1024
KD = D // P
HW = 512
NH = 4
DA_DH = 64
PLE = 256
FF = 2816
NFF = FF // P
EPS = 1e-6
LB_FLOOR = 1e-30
LN_SPLIT = 2.0 ** -60
HALVES = ((0, TP), (TP, TS))
LEVELS = (64, 32, 16, 8, 4, 2, 1)
STATES = ((0, 0), (0, 2), (0, 3), (0, 4), (1, 1), (1, 5), (1, 4), (1, 3))
CARRIES = ((0, 0, 1), (0, 1, 3), (0, 2, 4), (0, 3, 5), (1, 4, 0), (1, 5, 4), (1, 6, 3), (1, 7, 2))
SEQ_OF = [(0, TP)] * (TP // P) + [(TP, TS)] * (TS // P)
ISLOTS = 2048

U_PB, N_PB = 0, 14
U_PA, N_PA = 14, 10
U_BR = 24
U_WO = 28
U_UP = 32
U_DN = 54
U_PE = 76
U_PG = 78
N_UNITS = 82
CREDIT = 2


def lambda_init(l):
    return 0.8 - 0.6 * math.exp(-0.3 * l)


class Steps:

    def __init__(self, sem, names, credit=0):
        self.sem, self.names, self.n, self.credit = sem, list(names), len(names), credit
        self.index = {s: i for i, s in enumerate(self.names)}
        assert len(self.index) == self.n
        self.next = 0

    def step(self, name):
        assert self.names[self.next] == name, (self.names[self.next], name)
        self.next = (self.next + 1) % self.n
        return self.sem, 1

    def at(self, it, name):
        return it * self.n + (self.index[name] + 1 + self.credit)

    def before(self, it, name):
        return it * self.n + (self.index[name] + 1 + self.credit - self.n)

    def last(self, it):
        return self.at(it, self.names[-1])


def view(ap, offset, dims):
    return bass.AP(tensor=ap.tensor, offset=ap.offset + offset, ap=[list(ap.ap[0])] + [list(d) for d in dims])


def norm_names(engine, residual):
    out = []
    for s in range(NT + 2):
        r, n, h = s, s - 1, s - 2
        if r < NT and residual:
            out += {"act": [f"sqy{r}"], "dve": [f"ra{r}", f"rb{r}", f"rx{r}"],
                    "pool": [f"sy{r}", f"my{r}", f"ry{r}"], "pe": []}[engine]
        if 0 <= n < NT:
            out += {"act": [f"sqx{n}"], "dve": [f"hn{n}"], "pool": [f"mx{n}", f"rs{n}"],
                    "pe": [f"tr{n}_0", f"tr{n}_1"]}[engine]
        if h >= 0:
            out += {"act": [f"hi{h}_0", f"hi{h}_1"], "dve": [f"lo{h}_0", f"lo{h}_1"], "pool": [], "pe": []}[engine]
    return out


def gla_names():
    act = ["silu_q", "silu_g", "sig", "sig_neg", "ln1", "ln2", "exp_b", "exp_l", "kht0", "kht1", "kht2"]
    dve = ["lb", "qs", "k0", "k1", "f0", "f1", "fa", "fb", "g", "scan0", "scan1", "gw", "D0"]
    dve += ["dec", "qh", "dl", "kh", "D1", "at0", "at1"]
    pe = ["trk0", "trk1", "trk2", "diag", "ds"]
    n = len(LEVELS)
    for l in range(n):
        act += [f"xk{l}", f"xq{l}"]
        dve += [f"mk{l}", f"mq{l}"] + ([f"D{l + 2}"] if l + 2 < n else []) + (["s0", "s1", "s2", "s3", "s4", "s5"] if l == 0 else [])
        dve += [f"cp{l - 1}_0", f"cp{l - 1}_1"] if l else []
        pe += [f"lv{l}"]
    dve += [f"cp{n - 1}_0", f"cp{n - 1}_1", "o0", "o1", "ss"] + [f"on{c}" for c in range(NT)]
    act += ["sq0", "sq1", "ab0", "ab1"]
    pe += ["o0", "o1", "tro0", "tro1"]
    return act, dve, pe


def att_names():
    act, dve, pe = ["qk0", "qk1", "qk2"], ["cqk", "s_q", "s_k", "radd"], ["trq0", "trq1", "trq2"]
    for q in range(-1, NT):
        if q + 1 < NT:
            pe += [f"sc{q + 1}"]
            dve += [f"mx{q + 1}", f"nb{q + 1}"]
            act += [f"e{q + 1}_0", f"e{q + 1}_1"]
        if q >= 0:
            dve += [f"rc{q}", f"lr{q}", f"a{q}", f"al{q}"]
            act += [f"at{q}"]
            pe += [f"tra{q}"] + ([f"av{q - 1}"] if q else [])
    pe += [f"av{NT - 1}", "tro0", "tro1"]
    act += ["sq0", "sq1", "ab0", "ab1"]
    dve += ["o0", "o1", "ss"] + [f"on{c}" for c in range(NT)]
    return act, dve, pe


def build(nc, x_in, p_in, w_in, lb_logits, gnorm, lam_in, subln, w_a, w_b, w_out, n_mix_pre, n_mix_post,
          w_up, conv_p, w_down, n_ffn_pre, n_ffn_post, w_ple, w_ple_gate, n_ple, ident_in, masks_in,
          rope_in, out):
    with ExitStack() as ctx:
        place = [(nc.sbuf_base + 31) // 32 * 32]

        def put(name, shape, dt, offset=None):
            size = mybir.dt.size(dt)
            for s in shape[1:]:
                size *= s
            if offset is None:
                offset = place[0]
                place[0] += (size + 31) // 32 * 32
            return nc.alloc_sbuf_tensor_at(name, shape, dt, offset=offset), offset, offset + (size + 31) // 32 * 32

        def keep(name, shape, dt=F32):
            return put(name, shape, dt)[0]

        ident = keep("ident", [P, P])
        masks = keep("masks", [P, 2 * len(LEVELS), 64], U8)
        rmask = keep("rmask", [P, T], U8)
        lbl = keep("lbl", [P, NH * 2 * DEPTH])
        lbtab = keep("lbtab", [P, DEPTH * NH * 4])
        lb_now = keep("lb_now", [P, 4])
        lbs = keep("lbs", [P, 64])
        laytab = keep("laytab", [P, DEPTH * 2])
        lay_now = keep("lay_now", [P, 2])
        lams = keep("lams", [P, 16])
        conv_all = keep("conv_all", [P, NFF, 8])
        conv_now = keep("conv_now", [P, 2, 8])
        gn_row = keep("gn_row", [P, P])
        sl_row = keep("sl_row", [P, P])
        ssx = keep("ssx", [P, NT])
        rsx = keep("rsx", [P, NT])
        ssy = keep("ssy", [P, 2 * NT])
        rsy = keep("rsy", [P, NT])
        msx = keep("msx", [P, NT])
        msy = keep("msy", [P, NT])
        half_neg = keep("half_neg", [P, NT])
        decay = keep("decay", [P, 2, NT])
        st_g = keep("st_g", [P, 4, NT])
        st_t = keep("st_t", [P, 4, NT])
        mx = keep("mx", [P, 2, 2])
        nb = keep("nb", [P, 2, 2])
        sm = keep("sm", [P, 2, 2])
        rc = keep("rc", [P, 2, 2])
        lr = keep("lr", [P, 2])
        wrows, wr_off, _ = put("wrows", [P, 2, D], F32)
        rope = put("rope", [P, 2, T], F32, wr_off)[0]
        hn = keep("hn", [P, D])
        raw = keep("raw", [P, 2, ISLOTS])
        whi = keep("whi", [P, 2, ISLOTS], F32R)
        wlo = keep("wlo", [P, 2, ISLOTS], F32R)
        X, x_off, _ = put("X", [P, NT, D], F32)
        hT_hi, h_off, _ = put("hT_hi", [P, KD, T], F32R)
        hT_lo, _, h_end = put("hT_lo", [P, KD, T], F32R)
        m_off = place[0]
        prod, _, m_end = put("prod", [P, NFF, T], F32)
        assert place[0] <= nc.sbuf_usable_end, (place[0], nc.sbuf_usable_end)

        def stack(start, end, items):
            got, at = [], start
            for name, shape, dt in items:
                t, _, at = put(name, shape, dt, at)
                got.append(t)
            assert at <= end, (at, end)
            return got

        stT, stN = stack(m_off, m_end, [("stT", [P, 2, 2, T], F32), ("stN", [P, NT, 512], F32)])
        abT = put("abT", [P, 2 * NH, T], F32, x_off)[0]
        Qb, Kb, B, LB0, LB1, QH, AT, vN, gN, S, FZ = stack(m_off, m_end, [
            ("Qb", [P, T], F32), ("Kb", [P, 2, T], F32), ("B", [P, 2, T], F32), ("LB0", [P, 2, T], F32),
            ("LB1", [P, 2, T], F32), ("QH", [P, 2, T], F32), ("AT", [P, NT, P], F32), ("vN", [P, NT, P], F32),
            ("gN", [P, NT, P], F32), ("S", [P, 8, P], F32), ("FZ", [P, 3, T], F32)])
        LB2 = put("LB2", [P, 2, T], F32, m_end - 2 * T * 4)[0]
        khT = FZ[:, 0:2, :].rearrange("p a (c k) -> p (a c) k", k=P)
        O1 = FZ[:, 2, :].rearrange("p (c v) -> p c v", v=P)
        SQ1 = FZ[:, 0, :].rearrange("p (c v) -> p c v", v=P)
        QK, vD, T1, T2, qkT, PR, At, O2 = stack(h_off, h_end, [
            ("QK", [P, 2, NT, P], F32), ("vD", [P, NT, P], F32), ("T1", [P, 2, NT, P], F32),
            ("T2", [P, 2, NT, P], F32), ("qkT", [P, 2, T], F32), ("PR", [P, 2, 2, TS], F32),
            ("At", [P, 2, TS], F32), ("O2", [P, NT, P], F32)])
        SQ2 = put("SQ2", [P, NT, P], F32, h_off)[0]
        mT_hi, mT_lo, GT, BT1, BT2 = stack(m_off, m_end, [
            ("mT_hi", [P, KD, T], F32R), ("mT_lo", [P, KD, T], F32R), ("GT", [P, 2, 2, T], F32),
            ("BT1", [P, T], F32), ("BT2", [P, T], F32)])
        Y0w = put("Y0w", [P, NT, 512], F32, m_off + 2 * KD * T * 4)[0]
        TMP = put("TMP", [P, D], F32, m_off + 2 * KD * T * 4 + NT * 512 * 4)[0]
        CG, CV, Y0d = stack(x_off, h_off, [("CG", [P, 2, T], F32), ("CV", [P, 2, T], F32), ("Y0d", [P, NT, 512], F32)])
        PH_hi, PH_lo = stack(h_off, h_end, [("PH_hi", [P, 2, 2, T], F32R), ("PH_lo", [P, 2, 2, T], F32R)])
        XM, PT_hi, PT_lo, Pn, SG = stack(m_off, m_off + 2 * KD * T * 4, [
            ("XM", [P, NT, D], F32), ("PT_hi", [P, 2, T], F32R), ("PT_lo", [P, 2, T], F32R),
            ("Pn", [P, NT, PLE], F32), ("SG", [P, 2, 512], F32)])
        E = put("E", [P, 2, NT, 512], F32, x_off)[0]
        LB = (LB0, LB1, LB2)
        JK = put("JK", [P, 512], F32, m_end - 2048)[0]
        JX = put("JX", [P, D], F32, m_off + 2 * KD * T * 4)[0]
        JY = put("JY", [P, D], F32, m_off)[0]

        ps = ctx.enter_context(nc.psum_tensor("ps", [P, 8, 512], F32))
        zT = nc.dram_tensor("zT", [28 * P, T], F32, kind="Internal").ap()
        zN = nc.dram_tensor("zN", [T, 5 * 512], F32, kind="Internal").ap()

        def sem(name):
            return ctx.enter_context(nc.semaphore(name))

        const_ld = sem("constants_loaded")
        const_ok = sem("constants_ready")
        lam_exp = sem("lambda_exponentials")
        waited = sem("waited")
        w_loaded = [sem("unit_loaded_slot0"), sem("unit_loaded_slot1")]
        w_hi = sem("unit_high_part")
        w_lo = sem("unit_low_part")
        w_used = sem("unit_used")
        s_x = [sem(f"x_tiles_loaded_{n}") for n in range(3)]
        s_xm = sem("x_loaded_for_ple")
        s_wr = sem("rows_loaded")
        s_lay = sem("layer_constants_loaded")
        s_out = sem("x_stored")
        s_p = sem("p_loaded")
        zt_st = [sem("zT_stored_stage0"), sem("zT_stored_stage1")]
        zn_st = sem("zN_stored")
        s_fz, s_v, s_g, s_qk, s_vd = (sem(n) for n in ("gla_qf_loaded", "gla_v_loaded", "gla_g_loaded", "att_qk_loaded", "att_v_loaded"))
        s_gt = [sem("gates_loaded_0"), sem("gates_loaded_1")]

        def steps(name, names, credit=False):
            return Steps(sem(name), names, len(names) if credit else 0)

        lay_dve = steps("layer_dve", ["lay", "slw"])
        n1 = {e: steps(f"norm1_{e}", norm_names(e, False)) for e in ("act", "dve", "pool", "pe")}
        nr = {e: steps(f"resnorm_{e}", norm_names(e, True)) for e in ("act", "dve", "pool", "pe")}
        pb_act = steps("pb_act", [f"ev{u}_{b}_{h}" for u in range(2) for b in range(2) for h in range(2)], credit=True)
        pb_pe = steps("pb_pe", ["blk0", "blk1"])
        pa_pe = steps("pa_pe", [f"a{t}" for t in range(NT - 1)])
        pa_dve = steps("pa_dve", [f"ev{t}" for t in range(NT)], credit=True)
        ga, gd, gp = gla_names()
        G_act, G_dve, G_pe = steps("gla_act", ga, True), steps("gla_dve", gd, True), steps("gla_pe", gp, True)
        G_pool = steps("gla_pool", ["ms", "rs"])
        ta, td, tp = att_names()
        A_act, A_dve, A_pe = steps("att_act", ta, True), steps("att_dve", td, True), steps("att_pe", tp, True)
        A_pool = steps("att_pool", ["ms", "rs"])
        ab_act = steps("ab_act", [f"h{c}" for c in range(KD)])
        ab_dve = steps("ab_dve", [f"l{c}" for c in range(KD)])
        br_pe = steps("br_pe", ["blk0", "blk1"])
        br_act = steps("br_act", [f"{k}{u}_{b}" for u in range(2) for b in range(2) for k in ("sg", "mh")])
        br_dve = steps("br_dve", [f"{k}{u}_{b}" for u in range(2) for b in range(2) for k in ("ta0", "ta1", "tb0", "tb1", "m", "ml")], True)
        wo_pe = steps("wo_pe", [f"a{c}_{t}" for c in range(2) for t in range(NT - 1)])
        wo_act = steps("wo_act", [f"sq{t}" for t in range(NT)])
        wo_dve = steps("wo_dve", [f"y{t}" for t in range(NT)])
        up_pe = steps("up_pe", ["blk0", "blk1"])
        up_act = steps("up_act", [f"{k}{u}" for u in range(2) for k in ("cg0_", "cg1_", "cv0_", "cv1_", "ge")], True)
        up_dve = steps("up_dve", [f"{k}{u}" for u in range(2) for k in
                                  ("cp", "g0l", "g0r", "g1l", "g1r", "v0l", "v0r", "v1l", "v1r", "pr")], True)
        dn_pe = steps("dn_pe", [f"a{c}_{t}" for c in range(2) for t in range(NT - 1)])
        dn_act = steps("dn_act", [f"ph{j}" for j in range(12)] + [f"sq{t}" for t in range(NT)] + [f"ph{j}" for j in range(12, 22)])
        dn_dve = steps("dn_dve", [f"pl{j}" for j in range(12)] + [f"y{t}" for t in range(NT)] + [f"pl{j}" for j in range(12, 22)])
        pt_pe = steps("pt_pe", ["tr0", "tr1", "tr2"])
        pt_act = steps("pt_act", ["h0", "h1", "h2"])
        pt_dve = steps("pt_dve", ["l0", "l1", "l2"])
        pe_pe = steps("ple_pe", [f"e{c}_{t}" for c in range(2) for t in range(NT - 1)])
        pe_act = steps("ple_act", [f"e{c}_{t}" for c in range(2) for t in range(NT)])
        pg_pe = steps("gate_pe", [f"g{c}_{t}" for c in range(2) for t in range(NT - 1)])
        pg_act = steps("gate_act", [x for c in range(2) for t in range(NT + 1)
                                    for x in ([f"s{c}_{t}"] if t < NT else []) + ([f"q{c}_{t - 1}"] if t else [])])
        pg_dve = steps("gate_dve", [f"m{c}_{t}" for c in range(2) for t in range(NT)])
        fin_pool = steps("fin_pool", [f"{k}{t}" for t in range(NT) for k in ("s", "m", "r")])
        fin_dve = steps("fin_dve", [f"{k}{t}" for t in range(NT) for k in ("a", "b", "x")], True)

        def unit(L, j, i=None):
            n, half = L * N_UNITS + j, L * (N_UNITS // 2) + j // 2
            return (n, half, j % 2) if i is None else (n + i * 2, half + i, j % 2)

        block = ctx.enter_context(nc.Block())

        @block.sync
        def _(sp):
            for dst, src in ((ident[:], ident_in), (X[:, 0, 0:len(LEVELS) * P], masks_in), (lbl[:], lb_logits)):
                sp.dma_start(dst, src).then_inc(const_ld, 16)
            sp.dma_start(hn[:, 0:2 * DEPTH * 2 * DA_DH], lam_in.partition_broadcast(P)).then_inc(const_ld, 16)
            sp.dma_start(out, x_in).then_inc(s_out, 16)
            for s in (pb_act, pa_dve, G_act, G_dve, G_pe, A_act, A_dve, A_pe, br_dve, up_act, up_dve, fin_dve):
                sp.sem_inc(s.sem, s.credit)
            for s in (w_lo, w_used):
                sp.sem_inc(s, CREDIT)
            for s in (*zt_st, zn_st):
                sp.sem_inc(s, 16)

            def load(u, parts, width=ISLOTS):
                n, _, s = u
                sp.wait_ge(w_lo, n + 1)
                at = 0
                for src in parts:
                    cols = width // len(parts)
                    sp.dma_start(raw[:, s, at:at + cols].rearrange("p (k n) -> p k n", n=src.shape[-1]), src)\
                        .then_inc(w_loaded[s], 16 * 2 // len(parts))
                    at += cols

            def rows(w, L, k0, nk, c0, nc_):
                return w[bass.ds(L, 1), k0 * P:(k0 + nk) * P, bass.ds(c0, nc_)].rearrange("o (k p) n -> p (o k) n", p=P)

            with sp.Fori(0, DEPTH) as L:
                with sp.Fori(0, 3) as i:
                    for u in range(2):
                        load(unit(L, U_PB + u, i), [rows(w_in, L, 0, KD, i * 512 + u * 256, 256)])
                with sp.Fori(0, 4) as i:
                    for u in range(2):
                        load(unit(L, U_PB + 6 + u, i), [rows(w_in, L, 0, KD, i * 512 + (8 * HW + u * 256), 256)])
                with sp.Fori(0, 5) as i:
                    for u in range(2):
                        load(unit(L, U_PA + u, i), [rows(w_in, L, 4 * u, 4, i * 512 + 3 * HW, 512)])
                with sp.Fori(0, 2) as i:
                    for u in range(2):
                        load(unit(L, U_BR + u, i), [rows(w, L, 0, 4, i * 512 + u * 256, 256) for w in (w_a, w_b)])
                with sp.Fori(0, 2) as i:
                    for u in range(2):
                        load(unit(L, U_WO + u, i), [rows(w_out, L, 4 * u, 4, i * 512, 512)])
                with sp.Fori(0, NFF // 2) as i:
                    for u in range(2):
                        load(unit(L, U_UP + u, i), [rows(w_up, L, 0, KD, i * 256 + (u * P + half), P) for half in (0, FF)])
                for c in range(2):
                    for j in range(11):
                        load(unit(L, U_DN + c * 11 + j), [rows(w_down, L, 2 * j, 2, c * 512, 512)], 1024)
                for c in range(2):
                    load(unit(L, U_PE + c), [rows(w_ple, L, 0, 2, c * 512, 512)], 1024)
                for c in range(2):
                    for u in range(2):
                        load(unit(L, U_PG + 2 * c + u), [rows(w_ple_gate, L, 4 * u, 4, c * 512, 512)])

        @block.tensor
        def _(pe):
            mm = nc.tensor.matmul
            pe.wait_ge(const_ld, 64)
            PASSES = ((0, 0), (0, 1), (1, 0))
            hT, mT, PH, PT, W = (hT_hi, hT_lo), (mT_hi, mT_lo), (PH_hi, PH_lo), (PT_hi, PT_lo), (whi, wlo)

            def unit_ready(u):
                pe.wait_ge(w_lo, u[0] + (1 + CREDIT))

            def feature_block(rhs, s, chunks, banks):
                n = len(chunks) * 3
                i = 0
                for w0, k in chunks:
                    for a, b in PASSES:
                        for (t0, tn), bank in zip(HALVES, banks):
                            ins = mm(ps[:, bank, 0:tn], W[b][:, s, w0:w0 + P], rhs[a][:, k, t0:t0 + tn],
                                     start=(i == 0), stop=(i == n - 1))
                        i += 1
                return ins

            def token_chunks(lhs, s, chunks, first, last, counter, names, free=None):
                for i, (w, k) in enumerate(chunks):
                    for t in range(NT):
                        if free and first and i == 0:
                            free(t)
                        for q, (a, b) in enumerate(PASSES):
                            end = last and i == len(chunks) - 1 and q == 2
                            ins = mm(ps[:, t, :], lhs[a][:, k, t * P:(t + 1) * P] if not callable(k) else k(a, t),
                                     W[b][:, s, w * 512:(w + 1) * 512], start=(first and i == 0 and q == 0), stop=end)
                        if end and t < NT - 1:
                            ins.then_inc(*counter.step(names[t]))
                ins.then_inc(w_used, 1)

            def norm_transposes(c, it, ahead=None):
                for t in range(NT):
                    if ahead and t == 0:
                        ahead(0)
                    if ahead and t + 1 < NT:
                        ahead(t + 1)
                    pe.wait_ge(c["dve"].sem, c["dve"].at(it, f"hn{t}"))
                    for h in range(2):
                        if t:
                            pe.wait_ge(c["dve"].sem, c["dve"].at(it, f"lo{t - 1}_{h}"))
                        for k in range(4):
                            ins = nc.tensor.transpose(ps[:, 6 + h, k * P:(k + 1) * P],
                                                      hn[:, (4 * h + k) * P:(4 * h + k + 1) * P], ident[:])
                        ins.then_inc(*c["pe"].step(f"tr{t}_{h}"))

            def gla(it):
                pe.wait_ge(G_dve.sem, G_dve.at(it, "kh"))
                pe.wait_ge(A_act.sem, A_act.before(it, "ab1"))
                for b in range(3):
                    for i in range(4):
                        d, c = divmod(4 * b + i, NT)
                        ins = nc.tensor.transpose(ps[:, b, i * P:(i + 1) * P], LB2[:, d, c * P:(c + 1) * P], ident[:])
                    ins.then_inc(*G_pe.step(f"trk{b}"))
                for c in range(NT):
                    o = ps[:, 3 + c // 4, (c % 4) * P:(c % 4 + 1) * P]
                    mm(o, Kb[:, 0, c * P:(c + 1) * P], Qb[:, c * P:(c + 1) * P], start=True, stop=False)
                    ins = mm(o, Kb[:, 1, c * P:(c + 1) * P], Qb[:, c * P:(c + 1) * P], start=False, stop=True)
                ins.then_inc(*G_pe.step("diag"))
                pe.wait_ge(G_act.sem, G_act.at(it, "kht2"))
                pe.wait_ge(s_v, it * 16 + 16)
                for n, (d, c) in enumerate(STATES):
                    ins = mm(ps[:, 5 + n // 4, (n % 4) * P:(n % 4 + 1) * P], khT[:, d * NT + c, :], vN[:, c, :],
                             start=True, stop=True)
                ins.then_inc(*G_pe.step("ds"))
                for l, h in enumerate(LEVELS):
                    buf, b0 = LB[l % 3], 2 * (l % 2)
                    pe.wait_ge(G_dve.sem, G_dve.at(it, f"mq{l}"))
                    if l == 1:
                        pe.wait_ge(G_dve.sem, G_dve.at(it, "at0"))
                    if l >= 2:
                        pe.wait_ge(G_dve.sem, G_dve.at(it, f"cp{l - 2}_1"))
                    for d in range(2):
                        for c in range(NT):
                            ins = mm(ps[:, b0 + d, c * 64:(c + 1) * 64], buf[:, d, c * P:(c + 1) * P],
                                     view(buf[:], d * T + c * P + (0 if d else h), [[2 * h, 64 // h], [1, h]]),
                                     start=True, stop=True)
                    ins.then_inc(*G_pe.step(f"lv{l}"))
                pe.wait_ge(G_dve.sem, G_dve.at(it, f"cp{len(LEVELS) - 1}_1"))
                for c in range(NT):
                    o = ps[:, 4 + c // 4, (c % 4) * P:(c % 4 + 1) * P]
                    carried = [(d, n) for d, n, cc in CARRIES if cc == c]
                    mm(o, AT[:, c, :], vN[:, c, :], start=True, stop=False)
                    for i, (d, n) in enumerate(carried):
                        ins = mm(o, QH[:, d, c * P:(c + 1) * P], S[:, n, :], start=False, stop=(i == len(carried) - 1))
                    if c in (3, 5):
                        ins.then_inc(*G_pe.step(f"o{c // 4}"))
                out_transposes(G_dve, G_pe, it, O1, (6, 7))

            def out_transposes(dve_steps, pe_steps, it, o, banks):
                for c in range(NT):
                    if c in (0, 4):
                        pe.wait_ge(dve_steps.sem, dve_steps.at(it, f"on{3 if c == 0 else 5}"))
                    ins = nc.tensor.transpose(ps[:, banks[c // 4], (c % 4) * P:(c % 4 + 1) * P], o[:, c, :], ident[:])
                    if c in (3, 5):
                        ins.then_inc(*pe_steps.step(f"tro{c // 4}"))

            def attention(it):
                pe.wait_ge(A_dve.sem, A_dve.at(it, "radd"))
                for b in range(3):
                    for i in range(4):
                        a, t = divmod(4 * b + i, NT)
                        ins = nc.tensor.transpose(ps[:, b, i * P:(i + 1) * P], T1[:, a, t, :], ident[:])
                    ins.then_inc(*A_pe.step(f"trq{b}"))
                pe.wait_ge(A_act.sem, A_act.at(it, "qk2"))

                def values(q):
                    ok = SEQ_OF[q]
                    pe.wait_ge(A_act.sem, A_act.at(it, f"at{q}"))
                    if q == 0:
                        pe.wait_ge(s_vd, it * 16 + 16)
                        pe.wait_ge(G_act.sem, G_act.at(it, "ab1"))
                    n = ok[1] // P
                    for j in range(n):
                        ins = mm(ps[:, 6 + q // 4, (q % 4) * P:(q % 4 + 1) * P], At[:, q % 2, j * P:(j + 1) * P],
                                 vD[:, ok[0] // P + j, :], start=(j == 0), stop=(j == n - 1))
                    ins.then_inc(*A_pe.step(f"av{q}"))

                for q in range(-1, NT):
                    if q + 1 < NT:
                        k0, kn = SEQ_OF[q + 1]
                        if q >= 1:
                            pe.wait_ge(A_act.sem, A_act.at(it, f"e{q - 1}_1"))
                        for m in range(2):
                            rows_ = slice(m * DA_DH, (m + 1) * DA_DH)
                            ins = mm(ps[:, 2 * ((q + 1) % 2) + m, 0:kn], qkT[rows_, 0, (q + 1) * P:(q + 2) * P],
                                     qkT[rows_, 1, k0:k0 + kn], start=True, stop=True)
                        ins.then_inc(*A_pe.step(f"sc{q + 1}"))
                    if q >= 0:
                        pe.wait_ge(A_dve.sem, A_dve.at(it, f"al{q}"))
                        for j in range(SEQ_OF[q][1] // P):
                            ins = nc.tensor.transpose(ps[:, 4 + q % 2, j * P:(j + 1) * P], PR[:, q % 2, 0, j * P:(j + 1) * P], ident[:])
                        ins.then_inc(*A_pe.step(f"tra{q}"))
                        if q:
                            values(q - 1)
                values(NT - 1)
                pe.wait_ge(A_act.sem, A_act.at(it, f"at{NT - 1}"))
                out_transposes(A_dve, A_pe, it, O2, (4, 5))

            with pe.Fori(0, DEPTH) as L:
                norm_transposes(n1, L)
                pe.wait_ge(n1["dve"].sem, n1["dve"].last(L))
                pe.sem_inc(waited, 1)
                with pe.Fori(0, N_PB // 2) as i:
                    it = L * (N_PB // 2) + i
                    for u in range(2):
                        w = unit(L, U_PB + u, i)
                        unit_ready(w)
                        for b in range(2):
                            pe.wait_ge(pb_act.sem, pb_act.before(it, f"ev{u}_{b}_1"))
                            ins = feature_block(hT, w[2], [(k * 256 + b * P, k) for k in range(KD)],
                                                (4 * u + 2 * b, 4 * u + 2 * b + 1))
                            ins.then_inc(*(pb_pe.step(f"blk{u}") if b == 0 else (w_used, 1)))
                pe.wait_ge(pb_act.sem, pb_act.last(L * (N_PB // 2) + (N_PB // 2 - 1)))
                pe.sem_inc(waited, 1)
                with pe.Fori(0, 5) as g:
                    it = L * 5 + g
                    for u in range(2):
                        w = unit(L, U_PA + u, g)
                        unit_ready(w)
                        token_chunks(hT, w[2], [(k, 4 * u + k) for k in range(4)], u == 0, u == 1, pa_pe,
                                     [f"a{t}" for t in range(NT - 1)],
                                     lambda t: pe.wait_ge(pa_dve.sem, pa_dve.before(it, f"ev{t}")))
                pe.wait_ge(pa_dve.sem, pa_dve.last(L * 5 + 4))
                pe.sem_inc(waited, 1)
                with pe.Fori(0, NH) as h:
                    gla(L * NH + h)
                    attention(L * NH + h)
                pe.sem_inc(waited, 1)
                with pe.Fori(0, 2) as i:
                    it = L * 2 + i
                    for u in range(2):
                        w = unit(L, U_BR + u, i)
                        unit_ready(w)
                        pe.wait_ge(ab_dve.sem, ab_dve.last(L))
                        for b in range(2):
                            pe.wait_ge(br_dve.sem, br_dve.at(it, f"tb10_{b}") if u else br_dve.before(it, f"tb11_{b}"))
                            feature_block(hT, w[2], [(k * 256 + b * P, k) for k in range(4)], (4 * b, 4 * b + 1))
                            ins = feature_block(hT, w[2], [(1024 + k * 256 + b * P, 4 + k) for k in range(4)], (4 * b + 2, 4 * b + 3))
                            ins.then_inc(*(br_pe.step(f"blk{u}") if b == 0 else (w_used, 1)))
                pe.wait_ge(br_dve.sem, br_dve.last(L * 2 + 1))
                for c in range(2):
                    for u in range(2):
                        w = unit(L, U_WO + 2 * c + u)
                        unit_ready(w)
                        token_chunks(mT, w[2], [(k, 4 * u + k) for k in range(4)], u == 0, u == 1, wo_pe,
                                     [f"a{c}_{t}" for t in range(NT - 1)],
                                     (lambda t: pe.wait_ge(wo_dve.sem, wo_dve.at(L, f"y{t}"))) if c else None)
                norm_transposes(nr, L * 2)
                pe.wait_ge(nr["dve"].sem, nr["dve"].last(L * 2))
                pe.sem_inc(waited, 1)
                with pe.Fori(0, NFF // 2) as i:
                    it = L * (NFF // 2) + i
                    for u in range(2):
                        w = unit(L, U_UP + u, i)
                        unit_ready(w)
                        for b in range(2):
                            pe.wait_ge(up_dve.sem, up_dve.before(it, f"{'gv'[b]}1r{u}"))
                            ins = feature_block(hT, w[2], [(b * 1024 + k * P, k) for k in range(KD)],
                                                (4 * u + 2 * b, 4 * u + 2 * b + 1))
                            ins.then_inc(*(up_pe.step(f"blk{u}") if b == 0 else (w_used, 1)))
                pe.wait_ge(up_dve.sem, up_dve.last(L * (NFF // 2) + (NFF // 2 - 1)))
                for c in range(2):
                    for j in range(11):
                        n = 11 * c + j
                        w = unit(L, U_DN + n)
                        unit_ready(w)
                        pe.wait_ge(dn_dve.sem, dn_dve.at(L, f"pl{n}"))
                        token_chunks(PH, w[2], [(k, (lambda a, t, k=k: PH[a][:, n % 2, k, t * P:(t + 1) * P])) for k in range(2)],
                                     j == 0, j == 10, dn_pe, [f"a{c}_{t}" for t in range(NT - 1)],
                                     (lambda t: pe.wait_ge(dn_dve.sem, dn_dve.at(L, f"y{t}"))) if c else None)
                pe.wait_ge(s_p, L * 16 + 16)
                for b in range(3):
                    if b == 2:
                        pe.wait_ge(pt_dve.sem, pt_dve.at(L, "l0"))
                    for i in range(4):
                        k, t = divmod(4 * b + i, NT)
                        ins = nc.tensor.transpose(ps[:, 6 + b % 2, i * P:(i + 1) * P], Pn[:, t, k * P:(k + 1) * P], ident[:])
                    ins.then_inc(*pt_pe.step(f"tr{b}"))
                pe.wait_ge(pt_dve.sem, pt_dve.last(L))
                def e_tile(c, t):
                    if c:
                        pe.wait_ge(pe_act.sem, pe_act.at(L, f"e0_{t}"))
                    else:
                        pe.wait_ge(nr["dve"].sem, nr["dve"].at(L * 2 + 1, f"ra{t}"))
                    for k in range(2):
                        for q, (a, b) in enumerate(PASSES):
                            ins = mm(ps[:, t, :], PT[a][:, k, t * P:(t + 1) * P], W[b][:, (U_PE + c) % 2, k * 512:(k + 1) * 512],
                                     start=(k == 0 and q == 0), stop=(k == 1 and q == 2))
                    ins.then_inc(*(pe_pe.step(f"e{c}_{t}") if t < NT - 1 else (w_used, 1)))

                unit_ready(unit(L, U_PE))
                norm_transposes(nr, L * 2 + 1, lambda t: e_tile(0, t))
                unit_ready(unit(L, U_PE + 1))
                for t in range(NT):
                    e_tile(1, t)
                pe.wait_ge(nr["dve"].sem, nr["dve"].last(L * 2 + 1))
                for c in range(2):
                    for u in range(2):
                        w = unit(L, U_PG + 2 * c + u)
                        unit_ready(w)
                        token_chunks(hT, w[2], [(k, 4 * u + k) for k in range(4)], u == 0, u == 1, pg_pe,
                                     [f"g{c}_{t}" for t in range(NT - 1)],
                                     (lambda t: pe.wait_ge(pg_act.sem, pg_act.at(L, f"s0_{t}"))) if c else
                                     (lambda t: pe.wait_ge(pe_act.sem, pe_act.at(L, f"e1_{t}"))))

        mark = {}

        @block.vector
        def _(dve):
            v = nc.vector
            count = [0]

            def link(ins, name=None):
                count[0] += 1
                ins.then_inc(const_ok, 1)
                dve.wait_ge(const_ok, count[0])
                if name:
                    mark[name] = count[0]

            def done(c, it, name):
                dve.wait_ge(c.sem, c.at(it, name))

            link(v.memset(rmask[:], 1))
            link(v.memset(view(rmask[:], 0, [[P, NT]]), 0))
            link(v.memset(half_neg[:], -0.5))
            dve.wait_ge(const_ld, 64)
            link(v.tensor_copy(masks[:].rearrange("p a j -> p (a j)"), X[:, 0, 0:len(LEVELS) * P]))
            link(v.tensor_tensor(view(hn[:], 512, [[128, 2], [64, 2], [1, 64]]), view(hn[:], 0, [[256, 2], [128, 2], [1, 64]]),
                                 view(hn[:], 64, [[256, 2], [128, 2], [1, 64]]), ALU.mult))
            link(v.tensor_reduce(lams[:, 0:4], view(hn[:], 512, [[64, 4], [1, 64]]), AX_X, ALU.add))
            l0, l1 = view(lbl[:], 0, [[2, 8]]), view(lbl[:], 1, [[2, 8]])
            link(v.tensor_tensor(lbs[:, 0:8], l0, l1, ALU.max))
            link(v.tensor_tensor(view(lbs[:], 8, [[2, 8], [1, 2]]), view(lbl[:], 0, [[2, 8], [1, 2]]),
                                 view(lbs[:], 0, [[1, 8], [0, 2]]), ALU.subtract), "exponents")
            dve.wait_ge(lam_exp, 2)
            e0, e1 = view(lbs[:], 24, [[2, 8]]), view(lbs[:], 25, [[2, 8]])
            link(v.tensor_tensor(lbs[:, 40:48], e0, e1, ALU.add))
            link(v.reciprocal(lbs[:, 48:56], lbs[:, 40:48]))
            link(v.tensor_tensor(view(lbs[:], 8, [[2, 8], [1, 2]]), view(lbs[:], 24, [[2, 8], [1, 2]]),
                                 view(lbs[:], 48, [[1, 8], [0, 2]]), ALU.mult))
            p0, p1 = view(lbs[:], 8, [[2, 8]]), view(lbs[:], 9, [[2, 8]])
            link(v.tensor_tensor(lbs[:, 40:48], p0, p1, ALU.add))
            link(v.tensor_tensor(lbs[:, 56:64], lbs[:, 40:48], p0, ALU.subtract))
            link(v.tensor_tensor(lbs[:, 48:56], p0, p0, ALU.subtract))
            for l in range(DEPTH):
                lb = lbs[:, 48 + 8 * l:56 + 8 * l]
                link(v.tensor_scalar(view(lbtab[:], 16 * l, [[2, 8]]), lb, -1.0, 1.0, ALU.mult, ALU.add))
                link(v.tensor_scalar(view(lbtab[:], 16 * l + 1, [[2, 8]]), lb, LB_FLOOR, None, ALU.max))
                link(v.tensor_tensor(lams[:, 8 + l:9 + l], lams[:, 5 + 2 * l:6 + 2 * l], lams[:, 4 + 2 * l:5 + 2 * l], ALU.subtract))
                link(v.tensor_scalar(laytab[:, 2 * l:2 * l + 1], lams[:, 8 + l:9 + l], -lambda_init(l), None, ALU.add))
                link(v.memset(laytab[:, 2 * l + 1:2 * l + 2], 1.0 - lambda_init(l)), "all")

            def low(u, width=ISLOTS):
                n, _, s = u
                dve.wait_ge(w_hi, n + 1)
                v.tensor_tensor(wlo[:, s, 0:width], raw[:, s, 0:width], whi[:, s, 0:width].bitcast(F32), ALU.subtract)\
                    .then_inc(w_lo, 1)

            def norm_stage(c, it, x, weight, residual=None, bank_ready=None, extra=None):
                for s in range(NT + 2):
                    r, n, h = s, s - 1, s - 2
                    if r < NT and residual is not None:
                        bank_ready(r)
                        done(c["pool"], it, f"ry{r}")
                        if r:
                            done(c["dve"], it, f"rx{r - 1}")
                        v.scalar_tensor_tensor(TMP[:, 512:D], ps[:, r, :], rsy[:, r:r + 1], wrows[:, 1, 512:D], ALU.mult, ALU.mult)\
                            .then_inc(*c["dve"].step(f"ra{r}"))
                        v.scalar_tensor_tensor(TMP[:, 0:512], residual[:, r, :], rsy[:, r:r + 1], wrows[:, 1, 0:512], ALU.mult, ALU.mult)\
                            .then_inc(*c["dve"].step(f"rb{r}"))
                        done(c["dve"], it, f"rb{r}")
                        v.tensor_tensor(x[:, r, :], x[:, r, :], TMP[:], ALU.add).then_inc(*c["dve"].step(f"rx{r}"))
                    if 0 <= n < NT:
                        done(c["pool"], it, f"rs{n}")
                        if n:
                            done(c["pe"], it, f"tr{n - 1}_1")
                        if weight:
                            v.scalar_tensor_tensor(hn[:], x[:, n, :], rsx[:, n:n + 1], wrows[:, 0, :], ALU.mult, ALU.mult)\
                                .then_inc(*c["dve"].step(f"hn{n}"))
                        else:
                            v.tensor_scalar(hn[:], x[:, n, :], rsx[:, n:n + 1], None, ALU.mult).then_inc(*c["dve"].step(f"hn{n}"))
                    if h >= 0:
                        for k in range(2):
                            done(c["act"], it, f"hi{h}_{k}")
                            v.tensor_tensor(hT_lo[:, 4 * k:4 * k + 4, h * P:(h + 1) * P],
                                            ps[:, 6 + k, :].rearrange("p (k t) -> p k t", k=4),
                                            hT_hi[:, 4 * k:4 * k + 4, h * P:(h + 1) * P].bitcast(F32), ALU.subtract)\
                                .then_inc(*c["dve"].step(f"lo{h}_{k}"))

            def head_out(it, c_act, c_dve, c_pool, c_pe, o, sq, st, banks, weight):
                for k, n in ((0, 4), (1, 2)):
                    done(c_act, it, f"sq{k}")
                    v.tensor_copy(o[:, 4 * k:4 * k + n, :],
                                  ps[:, banks[k], 0:n * P].rearrange("p (c v) -> p c v", v=P)).then_inc(*c_dve.step(f"o{k}"))
                v.tensor_reduce(st[:, 0, :], sq[:], AX_X, ALU.add).then_inc(*c_dve.step("ss"))
                done(c_pool, it, "rs")
                done(c_dve, it, "o1")
                for c in range(NT):
                    v.scalar_tensor_tensor(o[:, c, :], o[:, c, :], st[:, 2, c:c + 1], weight(c), ALU.mult, ALU.mult)\
                        .then_inc(*c_dve.step(f"on{c}"))

            def gla(it):
                G = G_dve
                dve.wait_ge(G_pe.sem, G_pe.before(it, "tro1"))
                v.tensor_copy(lb_now[:], lbtab[:, bass.ds(it * 4, 4)]).then_inc(*G.step("lb"))
                done(G_act, it, "silu_q")
                v.tensor_scalar(Qb[:], FZ[:, 0, :], float(P) ** -0.5, None, ALU.mult).then_inc(*G.step("qs"))
                done(G_act, it, "sig_neg")
                done(G, it, "lb")
                for d in range(2):
                    v.tensor_scalar(Kb[:, d, :], FZ[:, 1 + d, :], lb_now[:, 2 * d:2 * d + 1], None, ALU.mult).then_inc(*G.step(f"k{d}"))
                for d in range(2):
                    v.tensor_scalar(LB0[:, d, :], LB0[:, d, :], lb_now[:, 2 * d:2 * d + 1], lb_now[:, 2 * d + 1:2 * d + 2],
                                    ALU.mult, ALU.add).then_inc(*G.step(f"f{d}"))
                done(G, it, "f1")
                v.tensor_scalar(LB1[:], LB0[:], LN_SPLIT, None, ALU.max).then_inc(*G.step("fa"))
                v.tensor_scalar(LB2[:], LB0[:], 1.0 / LN_SPLIT, 1.0, ALU.mult, ALU.min).then_inc(*G.step("fb"))
                done(G_act, it, "ln2")
                done(G, it, "fb")
                v.tensor_tensor(LB0[:], LB1[:], LB2[:], ALU.add).then_inc(*G.step("g"))
                done(G, it, "g")
                v.tensor_tensor_scan(B[:, 0, :], rmask[:], LB0[:, 0, :], 0.0, ALU.mult, ALU.add).then_inc(*G.step("scan0"))
                v.tensor_tensor_scan(B[:, 1, ::-1], rmask[:], LB0[:, 1, ::-1], 0.0, ALU.mult, ALU.add).then_inc(*G.step("scan1"))
                done(G_act, it, "silu_g")
                v.tensor_tensor(gN[:], gN[:], view(gn_row[:], 0, [[0, NT], [1, P]]), ALU.mult).then_inc(*G.step("gw"))
                done(G, it, "scan1")

                def differences(l):
                    h, out = LEVELS[l], LB[l % 3]
                    nb_ = T // (2 * h)
                    full = [[T, 2], [2 * h, nb_], [1, 2 * h]]
                    v.tensor_tensor(view(out[:], 0, full), view(B[:], 0, full),
                                    view(B[:], h - 1, [[T + 1, 2], [2 * h, nb_], [0, 2 * h]]), ALU.subtract).then_inc(*G.step(f"D{l}"))

                def copy_level(l):
                    h = LEVELS[l]
                    done(G_pe, it, f"lv{l}")
                    done(G, it, f"cp{l - 1}_1" if l else "at1")
                    dve.sem_inc(waited, 1)
                    for d in range(2):
                        v.copy_predicated(view(AT[:], 0 if d else h, [[P, NT], [2 * h, 64 // h], [1, h]]),
                                          view(masks[:], (d * len(LEVELS) + l) * 64, [[0, NT], [h, 64 // h], [1, h]]),
                                          view(ps[:], (2 * (l % 2) + d) * 512, [[64, NT], [h, 64 // h], [1, h]]))\
                            .then_inc(*G.step(f"cp{l}_{d}"))
                        if d == 0:
                            done(G, it, f"cp{l}_0")
                            dve.sem_inc(waited, 1)

                differences(0)
                done(G_act, it, "exp_b")
                ends = [[T - P + 1, 2], [P, NT]]
                v.tensor_copy(decay[:], view(LB1[:], P - 1, ends)).then_inc(*G.step("dec"))
                v.tensor_tensor(QH[:], view(Qb[:], 0, [[0, 2], [1, T]]), LB1[:], ALU.mult).then_inc(*G.step("qh"))
                v.tensor_tensor(view(LB2[:], 0, [[T, 2], [P, NT], [1, P]]), view(B[:], 0, [[T, 2], [P, NT], [1, P]]),
                                view(B[:], P - 1, ends + [[0, P]]), ALU.subtract).then_inc(*G.step("dl"))
                done(G_act, it, "exp_l")
                v.tensor_tensor(LB2[:], LB2[:], Kb[:], ALU.mult).then_inc(*G.step("kh"))
                done(G, it, "qh")
                differences(1)
                done(G_pe, it, "diag")
                for k, n in ((0, 4), (1, 2)):
                    v.tensor_tensor(AT[:, 4 * k:4 * k + n, :], ps[:, 3 + k, 0:n * P].rearrange("p (c t) -> p c t", t=P),
                                    view(ident[:], 0, [[0, n], [1, P]]), ALU.mult).then_inc(*G.step(f"at{k}"))
                for l, h in enumerate(LEVELS):
                    nb_ = T // (2 * h)
                    keys, queries = [[T + h, 2], [2 * h, nb_], [1, h]], [[T - h, 2], [2 * h, nb_], [1, h]]
                    buf = LB[l % 3]
                    done(G_act, it, f"xk{l}")
                    v.tensor_tensor(view(buf[:], 0, keys), view(buf[:], 0, keys), view(Kb[:], 0, keys), ALU.mult).then_inc(*G.step(f"mk{l}"))
                    done(G_act, it, f"xq{l}")
                    v.tensor_tensor(view(buf[:], h, queries), view(buf[:], h, queries),
                                    view(Qb[:], h, [[-h, 2], [2 * h, nb_], [1, h]]), ALU.mult).then_inc(*G.step(f"mq{l}"))
                    if l + 2 < len(LEVELS):
                        if l == 0:
                            done(G_pe, it, "trk2")
                            done(G, it, "kh")
                        else:
                            done(G_pe, it, f"lv{l - 1}")
                        differences(l + 2)
                    if l == 0:
                        done(G_pe, it, "ds")
                        v.tensor_copy(S[:, 0:4, :], ps[:, 5, :].rearrange("p (n v) -> p n v", v=P)).then_inc(*G.step("s0"))
                        v.tensor_copy(S[:, 4:8, :], ps[:, 6, :].rearrange("p (n v) -> p n v", v=P)).then_inc(*G.step("s1"))
                        done(G, it, "s1")
                        for i, (n, d, c) in enumerate(((2, 0, 3), (3, 0, 4), (6, 1, 4), (7, 1, 3))):
                            v.scalar_tensor_tensor(S[:, n, :], S[:, n - 1, :], decay[:, d, c:c + 1], S[:, n, :], ALU.mult, ALU.add)\
                                .then_inc(*G.step(f"s{2 + i}"))
                            done(G, it, f"s{2 + i}")
                    else:
                        copy_level(l - 1)
                copy_level(len(LEVELS) - 1)
                head_out(it, G_act, G, G_pool, G_pe, O1, SQ1, st_g, (4, 5), lambda c: gN[:, c, :])

            def attention(it, L):
                A = A_dve
                dve.wait_ge(s_qk, it * 32 + 32)
                dve.wait_ge(s_wr, L * 96 + 32)
                v.tensor_tensor(view(T1[:], 0, [[T, 2], [1, T]]), view(QK[:], 0, [[T, 2], [1, T]]),
                                view(rope[:], 0, [[0, 2], [1, T]]), ALU.mult).then_inc(*A.step("cqk"))
                for a, n in ((0, "s_q"), (1, "s_k")):
                    half = DA_DH // 2
                    v.tensor_tensor(view(T2[:], a * T, [[DA_DH, 2 * NT], [half, 2], [1, half]]),
                                    view(QK[:], a * T + half, [[DA_DH, 2 * NT], [-half, 2], [1, half]]),
                                    view(rope[:], T, [[DA_DH, 2 * NT], [half, 2], [1, half]]), ALU.mult).then_inc(*A.step(n))
                done(A, it, "s_k")
                v.tensor_tensor(T1[:], T1[:], T2[:], ALU.add).then_inc(*A.step("radd"))
                for q in range(-1, NT):
                    if q + 1 < NT:
                        n, p = q + 1, (q + 1) % 2
                        done(A_pe, it, f"sc{n}")
                        v.tensor_reduce(mx[:, p, :], ps[:, 2 * p:2 * p + 2, 0:SEQ_OF[n][1]], AX_X, ALU.max, negate=True)\
                            .then_inc(*A.step(f"mx{n}"))
                        done(A, it, f"mx{n}")
                        v.tensor_scalar(nb[:, p, :], mx[:, p, :], DA_DH ** -0.5, None, ALU.mult).then_inc(*A.step(f"nb{n}"))
                    if q >= 0:
                        p, kn = q % 2, SEQ_OF[q][1]
                        done(A_act, it, f"e{q}_1")
                        v.reciprocal(rc[:, p, :], sm[:, p, :]).then_inc(*A.step(f"rc{q}"))
                        done(A, it, f"rc{q}")
                        v.tensor_tensor(lr[:, p:p + 1], rc[:, p, 1:2], lay_now[:, 0:1], ALU.mult).then_inc(*A.step(f"lr{q}"))
                        done(A, it, f"lr{q}")
                        v.tensor_scalar(PR[:, p, 1, 0:kn], PR[:, p, 1, 0:kn], lr[:, p:p + 1], None, ALU.mult).then_inc(*A.step(f"a{q}"))
                        done(A, it, f"a{q}")
                        v.scalar_tensor_tensor(PR[:, p, 0, 0:kn], PR[:, p, 0, 0:kn], rc[:, p, 0:1], PR[:, p, 1, 0:kn],
                                               ALU.mult, ALU.add).then_inc(*A.step(f"al{q}"))
                head_out(it, A_act, A, A_pool, A_pe, O2, SQ2, st_t, (6, 7), lambda c: sl_row[:])

            with dve.Fori(0, DEPTH) as L:
                dve.wait_ge(s_lay, L * 48 + 48)
                v.tensor_copy(lay_now[:], laytab[:, bass.ds(L * 2, 2)]).then_inc(*lay_dve.step("lay"))
                done(lay_dve, L, "lay")
                v.tensor_scalar(sl_row[:], sl_row[:], lay_now[:, 1:2], None, ALU.mult).then_inc(*lay_dve.step("slw"))
                low(unit(L, 0))
                dve.wait_ge(s_wr, L * 96 + 16)
                norm_stage(n1, L, X, True)
                with dve.Fori(0, N_PB // 2) as i:
                    for u in range(2):
                        low(unit(L, U_PB + u + 1, i))
                with dve.Fori(0, 5) as g:
                    it = L * 5 + g
                    low(unit(L, U_PA + 1, g))
                    low(unit(L, U_PA + 2, g))
                    dve.wait_ge(zn_st, it * 16 + 16)
                    for t in range(NT):
                        if t < NT - 1:
                            done(pa_pe, it, f"a{t}")
                        else:
                            dve.wait_ge(w_used, unit(L, U_PA + 1, g)[0] + 3)
                        v.tensor_copy(stN[:, t, :], ps[:, t, :]).then_inc(*pa_dve.step(f"ev{t}"))
                with dve.Fori(0, NH) as h:
                    gla(L * NH + h)
                    attention(L * NH + h, L)
                for c in range(KD):
                    done(ab_act, L, f"h{c}")
                    v.tensor_tensor(hT_lo[:, c, :], abT[:, c, :], hT_hi[:, c, :].bitcast(F32), ALU.subtract).then_inc(*ab_dve.step(f"l{c}"))
                with dve.Fori(0, 2) as i:
                    it = L * 2 + i
                    for u in range(2):
                        low(unit(L, U_BR + u + 1, i))
                        for b in range(2):
                            n = f"{u}_{b}"
                            if b == 0:
                                done(br_pe, it, f"blk{u}")
                            else:
                                dve.wait_ge(w_used, unit(L, U_BR + u, i)[0] + 3)
                            done(br_act, it, f"sg{n}")
                            if (u, b) != (0, 0):
                                done(br_dve, it, f"ml{(2 * u + b - 1) // 2}_{(b + 1) % 2}")
                            else:
                                dve.wait_ge(br_dve.sem, br_dve.before(it, "ml1_1"))
                            for k, name, dst in ((0, "ta", BT1), (1, "tb", BT2)):
                                for hf, (t0, tn) in enumerate(HALVES):
                                    v.tensor_tensor(dst[:, t0:t0 + tn], GT[:, b, k, t0:t0 + tn], ps[:, 4 * b + 2 * k + hf, 0:tn], ALU.mult)\
                                        .then_inc(*br_dve.step(f"{name}{hf}{n}"))
                            done(br_dve, it, f"tb1{n}")
                            v.tensor_tensor(BT1[:], BT1[:], BT2[:], ALU.add).then_inc(*br_dve.step(f"m{n}"))
                            done(br_act, it, f"mh{n}")
                            blk = i * 4 + (2 * u + b)
                            v.tensor_tensor(mT_lo[:, bass.ds(blk, 1), :].rearrange("p o t -> p (o t)"), BT1[:],
                                            mT_hi[:, bass.ds(blk, 1), :].rearrange("p o t -> p (o t)").bitcast(F32), ALU.subtract)\
                                .then_inc(*br_dve.step(f"ml{n}"))
                low(unit(L, U_WO + 1))
                low(unit(L, U_WO + 2))
                for t in range(NT):
                    done(wo_act, L, f"sq{t}")
                    v.tensor_copy(Y0w[:, t, :], ps[:, t, :]).then_inc(*wo_dve.step(f"y{t}"))
                low(unit(L, U_WO + 3))
                low(unit(L, U_UP))
                dve.wait_ge(s_wr, L * 96 + 64)
                done(wo_dve, L, f"y{NT - 1}")
                for n in range(3):
                    dve.wait_ge(s_x[n], L * 32 + 32)
                norm_stage(nr, L * 2, X, True, Y0w, lambda t: None)
                with dve.Fori(0, NFF // 2) as i:
                    it = L * (NFF // 2) + i
                    for u in range(2):
                        low(unit(L, U_UP + u + 1, i))
                        if u == 0:
                            dve.wait_ge(up_dve.sem, up_dve.before(it, "pr1"))
                        dve.wait_ge(up_act.sem, up_act.before(it, f"cv1_{u}"))
                        v.tensor_copy(conv_now[:, u, :], conv_all[:, bass.ds(i * 2 + u, 1), :].rearrange("p o c -> p (o c)"))\
                            .then_inc(*up_dve.step(f"cp{u}"))
                        done(up_dve, it, f"cp{u}")
                        for gv, C in enumerate((CG, CV)):
                            nm = "gv"[gv]
                            done(up_act, it, f"c{nm}1_{u}")
                            for hf, (t0, tn) in enumerate(HALVES):
                                bank = 4 * u + 2 * gv + hf
                                left, right = C[:, u, t0 + 1:t0 + tn], C[:, u, t0:t0 + tn - 1]
                                v.scalar_tensor_tensor(left, ps[:, bank, 0:tn - 1], conv_now[:, u, 4 * gv:4 * gv + 1], left,
                                                       ALU.mult, ALU.add).then_inc(*up_dve.step(f"{nm}{hf}l{u}"))
                                done(up_dve, it, f"{nm}{hf}l{u}")
                                v.scalar_tensor_tensor(right, ps[:, bank, 1:tn], conv_now[:, u, 4 * gv + 2:4 * gv + 3], right,
                                                       ALU.mult, ALU.add).then_inc(*up_dve.step(f"{nm}{hf}r{u}"))
                        done(up_act, it, f"ge{u}")
                        done(up_dve, it, f"v1r{u}")
                        v.tensor_tensor(prod[:, bass.ds(i * 2 + u, 1), :].rearrange("p o t -> p (o t)"), CG[:, u, :], CV[:, u, :], ALU.mult)\
                            .then_inc(*up_dve.step(f"pr{u}"))

                def prod_low(n):
                    done(dn_act, L, f"ph{n}")
                    j = n % 11
                    v.tensor_tensor(PH_lo[:, n % 2], prod[:, 2 * j:2 * j + 2, :], PH_hi[:, n % 2].bitcast(F32), ALU.subtract)\
                        .then_inc(*dn_dve.step(f"pl{n}"))

                prod_low(0)
                for n in range(22):
                    low(unit(L, U_DN + n + 1), 1024)
                    if n + 1 < 22:
                        prod_low(n + 1)
                    if n == 10:
                        for t in range(NT):
                            done(dn_act, L, f"sq{t}")
                            v.tensor_copy(Y0d[:, t, :], ps[:, t, :]).then_inc(*dn_dve.step(f"y{t}"))
                for b in range(3):
                    done(pt_act, L, f"h{b}")
                    v.tensor_tensor(view(PT_lo[:], b * 512, [[1, 512]]), ps[:, 6 + b % 2, :],
                                    view(PT_hi[:], b * 512, [[1, 512]]).bitcast(F32), ALU.subtract).then_inc(*pt_dve.step(f"l{b}"))
                low(unit(L, U_PE + 1), 1024)
                dve.wait_ge(s_wr, L * 96 + 80)
                dve.wait_ge(s_xm, L * 16 + 16)
                norm_stage(nr, L * 2 + 1, XM, False, Y0d, lambda t: None)
                for j in range(4):
                    low(unit(L, U_PG + j))
                for c in range(2):
                    for t in range(NT):
                        done(pg_act, L, f"s{c}_{t}")
                        v.tensor_tensor(E[:, c, t, :], SG[:, t % 2, :], E[:, c, t, :], ALU.mult).then_inc(*pg_dve.step(f"m{c}_{t}"))
                dve.wait_ge(s_wr, L * 96 + 96)
                for t in range(NT):
                    done(fin_pool, L, f"r{t}")
                    if t:
                        done(fin_dve, L, f"x{t - 1}")
                    for c, n in ((0, "a"), (1, "b")):
                        v.scalar_tensor_tensor(TMP[:, c * 512:(c + 1) * 512], E[:, c, t, :], rsy[:, t:t + 1],
                                               wrows[:, 1, c * 512:(c + 1) * 512], ALU.mult, ALU.mult).then_inc(*fin_dve.step(f"{n}{t}"))
                    done(fin_dve, L, f"b{t}")
                    v.tensor_tensor(XM[:, t, :], XM[:, t, :], TMP[:], ALU.add).then_inc(*fin_dve.step(f"x{t}"))

        @block.gpsimd
        def _(pool):
            g = nc.gpsimd
            pool.wait_ge(const_ok, 3)

            def done(c, it, name):
                pool.wait_ge(c.sem, c.at(it, name))

            def rstd(c, it, out, ms, ss, width, m, r, n=1, col=0):
                pool.sem_inc(waited, 1)
                g.tensor_scalar(ms, ss, 1.0 / width, EPS, ALU.mult, ALU.add).then_inc(*c.step(m))
                done(c, it, m)
                g.tensor_tensor(out, ms, half_neg[:, 0:n], ALU.pow).then_inc(*c.step(r))

            def norm_stage(c, it, residual=None):
                for s in range(NT + 2):
                    r, n = s, s - 1
                    if r < NT and residual:
                        done(c["act"], it, f"sqy{r}")
                        g.tensor_tensor(msy[:, r:r + 1], ssy[:, r:r + 1], ssy[:, NT + r:NT + r + 1], ALU.add).then_inc(*c["pool"].step(f"sy{r}"))
                        done(c["pool"], it, f"sy{r}")
                        rstd(c["pool"], it, rsy[:, r:r + 1], msy[:, r:r + 1], msy[:, r:r + 1], D, f"my{r}", f"ry{r}")
                    if 0 <= n < NT:
                        done(c["act"], it, f"sqx{n}")
                        rstd(c["pool"], it, rsx[:, n:n + 1], msx[:, n:n + 1], ssx[:, n:n + 1], D, f"mx{n}", f"rs{n}")

            with pool.Fori(0, DEPTH) as L:
                norm_stage(n1, L)
                with pool.Fori(0, NH) as h:
                    it = L * NH + h
                    for c_dve, c_pool, st in ((G_dve, G_pool, st_g), (A_dve, A_pool, st_t)):
                        done(c_dve, it, "ss")
                        rstd(c_pool, it, st[:, 2, :], st[:, 1, :], st[:, 0, :], P, "ms", "rs", NT)
                norm_stage(nr, L * 2, True)
                norm_stage(nr, L * 2 + 1, True)
                for t in range(NT):
                    done(pg_act, L, f"q1_{t}")
                    g.tensor_tensor(msy[:, t:t + 1], ssy[:, t:t + 1], ssy[:, NT + t:NT + t + 1], ALU.add).then_inc(*fin_pool.step(f"s{t}"))
                    done(fin_pool, L, f"s{t}")
                    rstd(fin_pool, L, rsy[:, t:t + 1], msy[:, t:t + 1], msy[:, t:t + 1], D, f"m{t}", f"r{t}")

        @block.scalar
        def _(act):
            a = nc.scalar.activation

            def done(c, it, name):
                act.wait_ge(c.sem, c.at(it, name))

            def high(u, width=ISLOTS):
                n, half, s = u
                act.wait_ge(w_loaded[s], half * 32 + 32)
                act.wait_ge(w_used, n + 1)
                a(whi[:, s, 0:width], raw[:, s, 0:width], ACT.Copy).then_inc(w_hi, 1)

            def used(u):
                act.wait_ge(w_used, u[0] + (1 + CREDIT))

            def norm_stage(c, it, x, junk, hT_free, residual=None, extra=None):
                for s in range(NT + 2):
                    r, n, h = s, s - 1, s - 2
                    if r < NT and residual is not None:
                        residual(r)
                        if r:
                            done(c["act"], it, f"sqy{r - 1}")
                        a(JK[:], ps[:, r, :], ACT.Square, accum_out=ssy[:, NT + r:NT + r + 1]).then_inc(*c["act"].step(f"sqy{r}"))
                    if 0 <= n < NT:
                        if residual is not None:
                            done(c["dve"], it, f"rx{n}")
                        if n == 0:
                            hT_free()
                        else:
                            done(c["act"], it, f"sqx{n - 1}")
                        a(junk[:], x[:, n, :], ACT.Square, accum_out=ssx[:, n:n + 1]).then_inc(*c["act"].step(f"sqx{n}"))
                    if h >= 0:
                        for k in range(2):
                            done(c["pe"], it, f"tr{h}_{k}")
                            a(hT_hi[:, 4 * k:4 * k + 4, h * P:(h + 1) * P], ps[:, 6 + k, :].rearrange("p (k t) -> p k t", k=4), ACT.Copy)\
                                .then_inc(*c["act"].step(f"hi{h}_{k}"))
                    if extra:
                        extra(s)

            def row(dst, w, L, s):
                act.dma_start(dst, w[bass.ds(L, 1), :].partition_broadcast(P)).then_inc(s, 16)

            def load_x(dst_of, L):
                for n in range(3):
                    act.dma_start(X[:, 2 * n:2 * n + 2, :], out[n * 2 * P:(n + 1) * 2 * P, :].rearrange("(t p) d -> p t d", p=P))\
                        .then_inc(s_x[n], 16)

            def head_out(it, c_act, c_pe, sq, first, last, av, slot):
                for k, n in ((0, 4), (1, 2)):
                    done(c_pe, it, av[k])
                    a(sq[:, 4 * k:4 * k + n, :], ps[:, first + k, 0:n * P].rearrange("p (c v) -> p c v", v=P), ACT.Square)\
                        .then_inc(*c_act.step(f"sq{k}"))
                for k, n in ((0, 4), (1, 2)):
                    done(c_pe, it, f"tro{k}")
                    a(abT[:, bass.ds(slot, 1), 4 * k * P:(4 * k + n) * P].rearrange("p o t -> p (o t)"), ps[:, last + k, 0:n * P], ACT.Copy)\
                        .then_inc(*c_act.step(f"ab{k}"))

            def gla(it, h):
                act.wait_ge(s_fz, it * 16 + 16)
                a(FZ[:, 0, :], FZ[:, 0, :], ACT.Silu).then_inc(*G_act.step("silu_q"))
                act.wait_ge(s_g, it * 16 + 16)
                a(gN[:], gN[:], ACT.Silu).then_inc(*G_act.step("silu_g"))
                a(LB0[:], FZ[:, 1:3, :], ACT.Sigmoid).then_inc(*G_act.step("sig"))
                done(G_act, it, "sig")
                a(FZ[:, 1:3, :], FZ[:, 1:3, :], ACT.Sigmoid, scale=-1.0).then_inc(*G_act.step("sig_neg"))
                done(G_dve, it, "fa")
                a(LB1[:], LB1[:], ACT.Ln).then_inc(*G_act.step("ln1"))
                done(G_dve, it, "fb")
                a(LB2[:], LB2[:], ACT.Ln).then_inc(*G_act.step("ln2"))
                done(G_dve, it, "scan1")
                a(LB1[:], B[:], ACT.Exp).then_inc(*G_act.step("exp_b"))
                done(G_dve, it, "dl")
                a(LB2[:], LB2[:], ACT.Exp, scale=-1.0).then_inc(*G_act.step("exp_l"))
                for b in range(3):
                    done(G_pe, it, f"trk{b}")
                    a(view(FZ[:], b * 512, [[1, 512]]), ps[:, b, :], ACT.Copy).then_inc(*G_act.step(f"kht{b}"))
                for l, h_ in enumerate(LEVELS):
                    nb_ = T // (2 * h_)
                    keys, queries = [[T + h_, 2], [2 * h_, nb_], [1, h_]], [[T - h_, 2], [2 * h_, nb_], [1, h_]]
                    buf = LB[l % 3]
                    done(G_dve, it, f"D{l}")
                    a(view(buf[:], 0, keys), view(buf[:], 0, keys), ACT.Exp, scale=-1.0).then_inc(*G_act.step(f"xk{l}"))
                    a(view(buf[:], h_, queries), view(buf[:], h_, queries), ACT.Exp).then_inc(*G_act.step(f"xq{l}"))
                head_out(it, G_act, G_pe, SQ1, 4, 6, ("o0", "o1"), h)

            def attention(it, h):
                for b in range(3):
                    done(A_pe, it, f"trq{b}")
                    a(view(qkT[:], b * 512, [[1, 512]]), ps[:, b, :], ACT.Copy).then_inc(*A_act.step(f"qk{b}"))
                for q in range(-1, NT):
                    if q + 1 < NT:
                        n, p, kn = q + 1, (q + 1) % 2, SEQ_OF[q + 1][1]
                        done(A_dve, it, f"nb{n}")
                        if n >= 2:
                            done(A_pe, it, f"tra{n - 2}")
                        for m in range(2):
                            a(PR[:, p, m, 0:kn], ps[:, 2 * p + m, 0:kn], ACT.Exp, bias=nb[:, p, m:m + 1], scale=DA_DH ** -0.5,
                              accum_out=sm[:, p, m:m + 1]).then_inc(*A_act.step(f"e{n}_{m}"))
                    if q >= 0:
                        done(A_pe, it, f"tra{q}")
                        if q >= 2:
                            done(A_pe, it, f"av{q - 2}")
                        kn = SEQ_OF[q][1]
                        a(At[:, q % 2, 0:kn], ps[:, 4 + q % 2, 0:kn], ACT.Copy).then_inc(*A_act.step(f"at{q}"))
                head_out(it, A_act, A_pe, SQ2, 6, 4, ("av3", "av5"), h + 4)

            act.wait_ge(const_ok, mark["exponents"])
            a(lams[:, 4:8], lams[:, 0:4], ACT.Exp).then_inc(lam_exp, 1)
            a(lbs[:, 24:40], lbs[:, 8:24], ACT.Exp).then_inc(lam_exp, 1)
            act.wait_ge(const_ok, mark["all"])

            with act.Fori(0, DEPTH) as L:
                act.wait_ge(s_out, L * 192 + 16)
                act.wait_ge(fin_dve.sem, fin_dve.before(L, f"x{NT - 1}"))
                load_x(X, L)
                row(wrows[:, 0, :], n_mix_pre, L, s_wr)
                row(gn_row[:], gnorm, L, s_lay)
                row(sl_row[:], subln, L, s_lay)
                act.dma_start(conv_all[:], conv_p[bass.ds(L, 1), :, :].rearrange("o p (u c) -> p (o u) c", c=8)).then_inc(s_lay, 16)
                high(unit(L, 0))

                act.wait_ge(s_x[0], L * 32 + 16)
                act.wait_ge(s_x[1], L * 32 + 16)
                act.wait_ge(s_x[2], L * 32 + 16)
                norm_stage(n1, L, X, JX, lambda: None)
                done(n1["dve"], L, f"hn{NT - 1}")
                act.dma_start(rope[:], rope_in.rearrange("p (a t) -> p a t", a=2)).then_inc(s_wr, 16)
                with act.Fori(0, N_PB // 2) as i:
                    it = L * (N_PB // 2) + i
                    for u in range(2):
                        w = unit(L, U_PB + u, i)
                        high(unit(L, U_PB + u + 1, i))
                        act.wait_ge(zt_st[u], it * 16 + 16)
                        for b in range(2):
                            if b == 0:
                                done(pb_pe, it, f"blk{u}")
                            else:
                                used(w)
                            for hf, (t0, tn) in enumerate(HALVES):
                                a(stT[:, u, b, t0:t0 + tn], ps[:, 4 * u + 2 * b + hf, 0:tn], ACT.Copy)\
                                    .then_inc(*pb_act.step(f"ev{u}_{b}_{hf}"))
                        done(pb_act, it, f"ev{u}_1_1")
                        act.dma_start(zT[bass.ds(i * 4 * P + u * 2 * P, 2 * P), :].rearrange("(b p) t -> p b t", p=P), stT[:, u])\
                            .then_inc(zt_st[u], 16)
                with act.Fori(0, 5) as g:
                    it = L * 5 + g
                    high(unit(L, U_PA + 1, g))
                    high(unit(L, U_PA + 2, g))
                    done(pa_dve, it, f"ev{NT - 1}")
                    act.dma_start(zN[:, bass.ds(g * 512, 512)].rearrange("(t p) c -> p t c", p=P), stN[:]).then_inc(zn_st, 16)
                for u in range(2):
                    act.wait_ge(zt_st[u], L * (16 * N_PB // 2) + 16 * (N_PB // 2 + 1))
                act.wait_ge(zn_st, L * (16 * 5) + 16 * 6)
                heads = zT.rearrange("(a h p) t -> h p a t", a=7, p=P)
                cols = zN.rearrange("(t p) (g h c) -> g h p t c", p=P, g=5, h=NH)
                with act.Fori(0, NH) as h:
                    it = L * NH + h
                    act.wait_ge(G_pe.sem, G_pe.before(it, "tro1"))
                    act.wait_ge(A_act.sem, A_act.before(it, "ab1"))
                    act.dma_start(FZ[:], heads[bass.ds(h, 1), :, 0:3, :].rearrange("o p a t -> p (o a) t")).then_inc(s_fz, 16)
                    for n, (dst, s) in enumerate(((vN[:], s_v), (gN[:], s_g), (QK[:, 0], s_qk), (QK[:, 1], s_qk), (vD[:], s_vd))):
                        act.dma_start(dst, cols[n, bass.ds(h, 1)].rearrange("o p t c -> p (o t) c")).then_inc(s, 16)
                    gla(it, h)
                    attention(it, h)
                row(wrows[:, 0, :], n_ffn_pre, L, s_wr)
                row(wrows[:, 1, :], n_mix_post, L, s_wr)
                done(A_act, L * NH + (NH - 1), "ab1")
                for c in range(KD):
                    a(hT_hi[:, c, :], abT[:, c, :], ACT.Copy).then_inc(*ab_act.step(f"h{c}"))
                gates = zT[12 * P:28 * P, :].rearrange("(g b p) t -> b p g t", g=2, p=P)
                with act.Fori(0, 2) as i:
                    it = L * 2 + i
                    for u in range(2):
                        for b in range(2):
                            act.wait_ge(br_dve.sem, br_dve.at(it, f"tb10_{b}") if u else br_dve.before(it, f"tb11_{b}"))
                            act.dma_start(GT[:, b], gates[bass.ds(i * 4 + (2 * u + b), 1)].rearrange("o p g t -> p (o g) t")).then_inc(s_gt[b], 16)
                        high(unit(L, U_BR + u + 1, i))
                        for b in range(2):
                            act.wait_ge(s_gt[b], it * 32 + (16 * u + 16))
                            a(GT[:, b], GT[:, b], ACT.Sigmoid).then_inc(*br_act.step(f"sg{u}_{b}"))
                            done(br_dve, it, f"m{u}_{b}")
                            a(mT_hi[:, bass.ds(i * 4 + (2 * u + b), 1), :].rearrange("p o t -> p (o t)"), BT1[:], ACT.Copy)\
                                .then_inc(*br_act.step(f"mh{u}_{b}"))
                done(ab_dve, L, f"l{KD - 1}")
                load_x(X, L)
                high(unit(L, U_WO + 1))
                high(unit(L, U_WO + 2))
                for t in range(NT):
                    if t < NT - 1:
                        done(wo_pe, L, f"a0_{t}")
                    else:
                        used(unit(L, U_WO + 1))
                    if t == 0:
                        done(br_dve, L * 2 + 1, "ml1_1")
                    else:
                        done(wo_act, L, f"sq{t - 1}")
                    a(JK[:], ps[:, t, :], ACT.Square, accum_out=ssy[:, t:t + 1]).then_inc(*wo_act.step(f"sq{t}"))
                high(unit(L, U_WO + 3))
                high(unit(L, U_UP))

                def wo_bank(t):
                    if t == 0:
                        done(wo_act, L, f"sq{NT - 1}")
                    if t < NT - 1:
                        done(wo_pe, L, f"a1_{t}")
                    else:
                        used(unit(L, U_WO + 3))

                def store_x(x):
                    def f(s):
                        if 1 <= s <= NT:
                            act.dma_start(out[(s - 1) * P:s * P, :], x[:, s - 1, :]).then_inc(s_out, 16)
                    return f

                norm_stage(nr, L * 2, X, JY, lambda: used(unit(L, U_WO + 3)), wo_bank, store_x(X))
                done(nr["dve"], L * 2, f"hn{NT - 1}")
                row(wrows[:, 1, :], n_ffn_post, L, s_wr)
                act.wait_ge(s_out, L * 192 + (16 + 96))
                with act.Fori(0, NFF // 2) as i:
                    it = L * (NFF // 2) + i
                    for u in range(2):
                        high(unit(L, U_UP + u + 1, i))
                        act.wait_ge(up_dve.sem, up_dve.before(it, f"pr{u}"))
                        done(up_dve, it, f"cp{u}")
                        for gv, C in enumerate((CG, CV)):
                            if gv == 0:
                                done(up_pe, it, f"blk{u}")
                            else:
                                used(unit(L, U_UP + u, i))
                            for hf, (t0, tn) in enumerate(HALVES):
                                a(C[:, u, t0:t0 + tn], ps[:, 4 * u + 2 * gv + hf, 0:tn], ACT.Identity,
                                  scale=conv_now[:, u, 4 * gv + 1:4 * gv + 2], bias=conv_now[:, u, 4 * gv + 3:4 * gv + 4])\
                                    .then_inc(*up_act.step(f"c{'gv'[gv]}{hf}_{u}"))
                        done(up_dve, it, f"g1r{u}")
                        a(CG[:, u, :], CG[:, u, :], ACT.Gelu_apprx_tanh).then_inc(*up_act.step(f"ge{u}"))

                def prod_high(n):
                    act.wait_ge(w_used, unit(L, U_DN + n)[0] + 1)
                    j = n % 11
                    a(PH_hi[:, n % 2], prod[:, 2 * j:2 * j + 2, :], ACT.Copy).then_inc(*dn_act.step(f"ph{n}"))

                done(up_dve, L * (NFF // 2) + (NFF // 2 - 1), "pr1")
                act.wait_ge(w_used, unit(L, U_DN)[0] + 2)
                prod_high(0)
                for n in range(22):
                    high(unit(L, U_DN + n + 1), 1024)
                    if n + 1 < 22:
                        prod_high(n + 1)
                    if n == 10:
                        for t in range(NT):
                            if t < NT - 1:
                                done(dn_pe, L, f"a0_{t}")
                            else:
                                used(unit(L, U_DN + 10))
                            if t:
                                done(dn_act, L, f"sq{t - 1}")
                            a(CG[:, 0, 0:512], ps[:, t, :], ACT.Square, accum_out=ssy[:, t:t + 1]).then_inc(*dn_act.step(f"sq{t}"))
                done(dn_dve, L, "pl21")
                act.dma_start(XM[:], out.rearrange("(t p) d -> p t d", p=P)).then_inc(s_xm, 16)
                act.dma_start(Pn[:], p_in[bass.ds(L, 1), :, :].rearrange("o (t p) c -> p (o t) c", p=P)).then_inc(s_p, 16)
                for b in range(3):
                    done(pt_pe, L, f"tr{b}")
                    a(view(PT_hi[:], b * 512, [[1, 512]]), ps[:, 6 + b % 2, :], ACT.Copy).then_inc(*pt_act.step(f"h{b}"))
                high(unit(L, U_PE + 1), 1024)

                def dn_bank(t):
                    if t < NT - 1:
                        done(dn_pe, L, f"a1_{t}")

                def e_out(c, t):
                    if t < NT - 1:
                        done(pe_pe, L, f"e{c}_{t}")
                    else:
                        used(unit(L, U_PE + c))
                    a(E[:, c, t, :], ps[:, t, :], ACT.Copy).then_inc(*pe_act.step(f"e{c}_{t}"))

                norm_stage(nr, L * 2 + 1, XM, JX, lambda: None, dn_bank, lambda s: e_out(0, s - 1) if 1 <= s <= NT else None)
                row(wrows[:, 1, :], n_ple, L, s_wr)
                high(unit(L, U_PG))
                for t in range(NT):
                    e_out(1, t)
                for j in (1, 2, 3):
                    high(unit(L, U_PG + j))
                for c in range(2):
                    for t in range(NT + 1):
                        if t < NT:
                            if t < NT - 1:
                                done(pg_pe, L, f"g{c}_{t}")
                            else:
                                used(unit(L, U_PG + 1 + 2 * c))
                            n = c * NT + t
                            if n >= 2:
                                done(pg_dve, L, f"m{(n - 2) // NT}_{(n - 2) % NT}")
                            a(SG[:, t % 2, :], ps[:, t, :], ACT.Sigmoid).then_inc(*pg_act.step(f"s{c}_{t}"))
                        if t:
                            done(pg_dve, L, f"m{c}_{t - 1}")
                            if t > 1:
                                done(pg_act, L, f"q{c}_{t - 2}")
                            elif c:
                                done(pg_act, L, f"q0_{NT - 1}")
                            else:
                                done(nr["act"], L * 2 + 1, f"sqy{NT - 1}")
                            a(JK[:], E[:, c, t - 1, :], ACT.Square, accum_out=ssy[:, c * NT + t - 1:c * NT + t]).then_inc(*pg_act.step(f"q{c}_{t - 1}"))
                for t in range(NT):
                    done(fin_dve, L, f"x{t}")
                    act.dma_start(out[t * P:(t + 1) * P, :], XM[:, t, :]).then_inc(s_out, 16)
            act.wait_ge(s_out, DEPTH * 192 + 16)



def kernel(**inputs):
    import numpy as np
    import concourse.bacc as bacc
    from concourse.bass_utils import run_bass_kernel_spmd

    i = {k: np.asarray(v) for k, v in inputs.items()}
    lay = {
        "x_in": np.concatenate([i["x_prompt"][0], i["x_sample"][0]], axis=0),
        "p_in": np.concatenate([i["p_prompt"][:, 0], i["p_sample"][:, 0]], axis=1),
        "w_in": i["w_in"],
        "lb_logits": i["hgrn_lb_logits"].reshape(DEPTH, 2, NH, P).transpose(3, 2, 1, 0).reshape(P, -1),
        "gnorm": i["hgrn_gnorm"],
        "lam_in": i["diff_lambda"].reshape(1, -1),
        "subln": i["diff_subln"],
        "w_a": i["w_branch_a"], "w_b": i["w_branch_b"], "w_out": i["w_out"],
        "n_mix_pre": i["norm_mix_pre"], "n_mix_post": i["norm_mix_post"],
        "w_up": i["w_up"],
        "conv_p": np.concatenate([i["conv_w"], i["conv_b"][:, None]], axis=1).reshape(DEPTH, 4, 2, NFF, P)
        .transpose(0, 4, 3, 2, 1).reshape(DEPTH, P, NFF * 8),
        "w_down": i["w_down"],
        "n_ffn_pre": i["norm_ffn_pre"], "n_ffn_post": i["norm_ffn_post"],
        "w_ple": i["w_ple"], "w_ple_gate": i["w_ple_gate"], "n_ple": i["norm_ple"],
    }
    lay["ident_in"] = np.eye(P, dtype=np.float32)
    masks = np.zeros((P, 2, len(LEVELS), 64), np.float32)
    for l, h in enumerate(LEVELS):
        for j in range(64):
            block = j // h * 2 * h
            masks[block:block + h, 0, l, j] = 1
            masks[block + h:block + 2 * h, 1, l, j] = 1
    lay["masks_in"] = masks.reshape(P, -1)
    inv = (1.0 / (10000.0 ** (np.arange(0, DA_DH, 2) / DA_DH))).astype(np.float32)
    pos = np.concatenate([np.arange(TP), np.arange(TS)]).astype(np.float32)
    ang = (pos[:, None] * inv[None, :]).astype(np.float32)
    cos, sin = np.cos(ang), np.sin(ang)
    rope = np.stack([np.concatenate([cos, cos] * 2, 1), np.concatenate([-sin, sin] * 2, 1)])
    lay["rope_in"] = rope.reshape(2, NT, P, P).transpose(2, 0, 1, 3).reshape(P, -1).astype(np.float32)

    nc = bacc.Bacc("TRN2", target_bir_lowering=False, num_devices=1)
    arrays, args = {}, {}
    for name, arr in lay.items():
        arr = np.ascontiguousarray(arr)
        arrays[name + "_dram"] = arr
        args[name] = nc.dram_tensor(name + "_dram", arr.shape, mybir.dt.from_np(arr.dtype), kind="ExternalInput").ap()
    args["out"] = nc.dram_tensor("out_dram", (T, D), F32, kind="ExternalOutput").ap()
    build(nc, **args)
    y = run_bass_kernel_spmd(nc, [arrays], core_ids=[0]).results[0]["out_dram"]
    return y[None, :TP], y[None, TP:]
```

```python
import math
from contextlib import ExitStack

import concourse.bass as bass
from concourse import mybir

ALU = mybir.AluOpType
ACT = mybir.ActivationFunctionType
F32 = mybir.dt.float32
F32R = mybir.dt.float32r
U8 = mybir.dt.uint8
AX_X = mybir.AxisListType.X

P = 128
DEPTH = 2
TP, TS = 256, 512
T = TP + TS
NT = T // P
D = 1024
KD = D // P
HW = 512
NH = 4
DA_DH = 64
PLE = 256
FF = 2816
NFF = FF // P
EPS = 1e-6
LB_FLOOR = 1e-30
LN_SPLIT = 2.0 ** -60
HALVES = ((0, TP), (TP, TS))
LEVELS = (64, 32, 16, 8, 4, 2, 1)
STATES = ((0, 0), (0, 2), (0, 3), (0, 4), (1, 1), (1, 5), (1, 4), (1, 3))
CARRIES = ((0, 0, 1), (0, 1, 3), (0, 2, 4), (0, 3, 5), (1, 4, 0), (1, 5, 4), (1, 6, 3), (1, 7, 2))
SEQ_OF = [(0, TP)] * (TP // P) + [(TP, TS)] * (TS // P)
ISLOTS = 2048

U_PB, N_PB = 0, 6
U_PA = 6
U_GT = 16
U_BR = 24
U_WO = 28
U_UP = 32
U_DN = 54
U_PE = 76
U_PG = 78
N_UNITS = 82
CREDIT = 2


def lambda_init(l):
    return 0.8 - 0.6 * math.exp(-0.3 * l)


class Steps:

    def __init__(self, sem, names, credit=0):
        self.sem, self.names, self.n, self.credit = sem, list(names), len(names), credit
        self.index = {s: i for i, s in enumerate(self.names)}
        assert len(self.index) == self.n
        self.next = 0

    def step(self, name):
        assert self.names[self.next] == name, (self.names[self.next], name)
        self.next = (self.next + 1) % self.n
        return self.sem, 1

    def at(self, it, name):
        return it * self.n + (self.index[name] + 1 + self.credit)

    def before(self, it, name):
        return it * self.n + (self.index[name] + 1 + self.credit - self.n)

    def last(self, it):
        return self.at(it, self.names[-1])


def view(ap, offset, dims):
    return bass.AP(tensor=ap.tensor, offset=ap.offset + offset, ap=[list(ap.ap[0])] + [list(d) for d in dims])


def norm_names(engine, residual):
    out = []
    for s in range(NT + 2):
        r, n, h = s, s - 1, s - 2
        if r < NT and residual:
            out += {"act": [f"sqy{r}"], "dve": [f"ra{r}", f"rb{r}", f"rx{r}"],
                    "pool": [f"sy{r}", f"my{r}", f"ry{r}"], "pe": []}[engine]
        if 0 <= n < NT:
            out += {"act": [f"sqx{n}"], "dve": [f"hn{n}"], "pool": [f"mx{n}", f"rs{n}"],
                    "pe": [f"tr{n}_0", f"tr{n}_1"]}[engine]
        if h >= 0:
            out += {"act": [f"hi{h}_0", f"hi{h}_1"], "dve": [f"lo{h}_0", f"lo{h}_1"], "pool": [], "pe": []}[engine]
    return out


def gla_names():
    act = ["silu_q", "silu_g", "sig", "sig_neg", "ln1", "ln2", "exp_b", "exp_l", "xk0", "xq0", "kht0", "kht1", "kht2"]
    dve = ["lb", "qs", "k0", "k1", "f0", "f1", "fa", "fb", "g", "scan0", "scan1", "gw", "D0"]
    dve += ["dec", "qh", "dl", "kh", "D1", "at0", "at1"]
    pe = ["trk0", "trk1", "trk2", "diag", "ds"]
    n = len(LEVELS)
    for l in range(n):
        act += [f"xk{l}", f"xq{l}"] if l else []
        dve += [f"mk{l}", f"mq{l}"] + ([f"D{l + 2}"] if l + 2 < n else []) + (["s0", "s1", "s2", "s3", "s4", "s5"] if l == 0 else [])
        dve += [f"cp{l - 1}_0", f"cp{l - 1}_1"] if l else []
        pe += [f"lv{l}_0", f"lv{l}_1"]
    dve += [f"cp{n - 1}_0", f"cp{n - 1}_1", "o0", "o1", "ss"] + [f"on{c}" for c in range(NT)]
    act += ["sq0", "sq1", "ab0", "ab1"]
    pe += ["o0", "o1", "tro0", "tro1"]
    return act, dve, pe


def att_names():
    act, dve, pe = ["qk0", "qk1", "qk2"], ["cqk", "s_q", "s_k", "radd"], ["trq0", "trq1", "trq2"]
    act += ["e0_0", "e0_1"]
    dve += ["mx0", "nb0"]
    pe += ["sc0"]
    for k in range(NT + 1):
        if k < NT:
            dve += [f"rc{k}", f"lr{k}", f"a{k}", f"al{k}"]
        if k + 1 < NT:
            pe += [f"sc{k + 1}"]
            dve += [f"mx{k + 1}", f"nb{k + 1}"]
        pe += ([f"av{k - 1}"] if k else []) + ([f"tra{k}"] if k < NT else [])
        act += ([f"e{k + 1}_0", f"e{k + 1}_1"] if k + 1 < NT else []) + ([f"oc{k - 1}"] if k else []) + ([f"at{k}"] if k < NT else [])
    pe += ["tro0", "tro1"]
    act += ["sq", "ab0", "ab1"]
    dve += ["ss"] + [f"on{c}" for c in range(NT)]
    return act, dve, pe


def build(nc, x_in, p_in, w_in, lb_logits, gnorm, lam_in, subln, w_a, w_b, w_out, n_mix_pre, n_mix_post,
          w_up, conv_p, w_down, n_ffn_pre, n_ffn_post, w_ple, w_ple_gate, n_ple, ident_in, masks_in,
          rope_in, out):
    with ExitStack() as ctx:
        place = [(nc.sbuf_base + 31) // 32 * 32]

        def put(name, shape, dt, offset=None):
            size = mybir.dt.size(dt)
            for s in shape[1:]:
                size *= s
            if offset is None:
                offset = place[0]
                place[0] += (size + 31) // 32 * 32
            return nc.alloc_sbuf_tensor_at(name, shape, dt, offset=offset), offset, offset + (size + 31) // 32 * 32

        def keep(name, shape, dt=F32):
            return put(name, shape, dt)[0]

        ident = keep("ident", [P, P])
        masks = keep("masks", [P, 2 * len(LEVELS), 64], U8)
        rmask = keep("rmask", [P, T], U8)
        lbl = keep("lbl", [P, NH * 2 * DEPTH])
        lbtab = keep("lbtab", [P, DEPTH * NH * 4])
        lb_now = keep("lb_now", [P, 4])
        lbs = keep("lbs", [P, 64])
        laytab = keep("laytab", [P, DEPTH * 2])
        lay_now = keep("lay_now", [P, 2])
        lams = keep("lams", [P, 16])
        conv_all = keep("conv_all", [P, NFF, 8])
        conv_now = keep("conv_now", [P, 2, 8])
        gn_row = keep("gn_row", [P, P])
        sl_row = keep("sl_row", [P, P])
        ssx = keep("ssx", [P, NT])
        rsx = keep("rsx", [P, NT])
        ssy = keep("ssy", [P, 2 * NT])
        rsy = keep("rsy", [P, NT])
        msx = keep("msx", [P, NT])
        msy = keep("msy", [P, NT])
        half_neg = keep("half_neg", [P, NT])
        decay = keep("decay", [P, 2, NT])
        st_g = keep("st_g", [P, 4, NT])
        st_t = keep("st_t", [P, 4, NT])
        mx = keep("mx", [P, 2, 2])
        nb = keep("nb", [P, 2, 2])
        sm = keep("sm", [P, 2, 2])
        rc = keep("rc", [P, 2, 2])
        lr = keep("lr", [P, 2])
        wrows, wr_off, _ = put("wrows", [P, 2, D], F32)
        rope = put("rope", [P, 2, T], F32, wr_off)[0]
        hn = keep("hn", [P, D])
        raw = keep("raw", [P, 2, ISLOTS])
        whi = keep("whi", [P, 2, ISLOTS], F32R)
        wlo = keep("wlo", [P, 2, ISLOTS], F32R)
        X, x_off, _ = put("X", [P, NT, D], F32)
        hT_hi, h_off, _ = put("hT_hi", [P, KD, T], F32R)
        hT_lo, _, h_end = put("hT_lo", [P, KD, T], F32R)
        m_off = place[0]
        prod, _, m_end = put("prod", [P, NFF, T], F32)
        assert place[0] <= nc.sbuf_usable_end, (place[0], nc.sbuf_usable_end)

        def stack(start, end, items):
            got, at = [], start
            for name, shape, dt in items:
                t, _, at = put(name, shape, dt, at)
                got.append(t)
            assert at <= end, (at, end)
            return got

        stT, stN = stack(m_off, m_end, [("stT", [P, 2, 2, T], F32), ("stN", [P, NT, 512], F32)])
        abT = put("abT", [P, 2 * NH, T], F32, x_off)[0]
        Qb, Kb, B, LB0, LB1, QH, AT, vN, gN, S, FZ, vD = stack(m_off, m_end, [
            ("Qb", [P, T], F32), ("Kb", [P, 2, T], F32), ("B", [P, 2, T], F32), ("LB0", [P, 2, T], F32),
            ("LB1", [P, 2, T], F32), ("QH", [P, 2, T], F32), ("AT", [P, NT, P], F32), ("vN", [P, NT, P], F32),
            ("gN", [P, NT, P], F32), ("S", [P, 8, P], F32), ("FZ", [P, 3, T], F32),
            ("vD", [P, NT, P], F32)])
        LB2 = put("LB2", [P, 2, T], F32, m_end - 2 * T * 4)[0]
        khT = FZ[:, 0:2, :].rearrange("p a (c k) -> p (a c) k", k=P)
        O1 = FZ[:, 2, :].rearrange("p (c v) -> p c v", v=P)
        SQ1 = FZ[:, 0, :].rearrange("p (c v) -> p c v", v=P)
        QK, T1, PR, At = stack(x_off, h_off, [
            ("QK", [P, 2, NT, P], F32), ("T1", [P, 2, NT, P], F32), ("PR", [P, 2, 2, TS], F32), ("At", [P, 2, TS], F32)])
        qkT = put("qkT", [P, 2, T], F32, x_off)[0]
        T2 = put("T2", [P, 2, NT, P], F32, x_off + 4 * T * 4)[0]
        O2, SQ2 = T1[:, 0], T1[:, 1]
        gst = hn[:, 0:T]
        mT_hi, mT_lo, GT, BT1, BT2 = stack(m_off, m_end, [
            ("mT_hi", [P, KD, T], F32R), ("mT_lo", [P, KD, T], F32R), ("GT", [P, 2, 2, T], F32),
            ("BT1", [P, T], F32), ("BT2", [P, T], F32)])
        Y0w = put("Y0w", [P, NT, 512], F32, m_off + 2 * KD * T * 4)[0]
        TMP = put("TMP", [P, D], F32, m_off + 2 * KD * T * 4 + NT * 512 * 4)[0]
        CG, CV, Y0d = stack(x_off, h_off, [("CG", [P, 2, T], F32), ("CV", [P, 2, T], F32), ("Y0d", [P, NT, 512], F32)])
        PH_hi, PH_lo = stack(h_off, h_end, [("PH_hi", [P, 2, 2, T], F32R), ("PH_lo", [P, 2, 2, T], F32R)])
        XM, PT_hi, PT_lo, Pn, SG = stack(m_off, m_off + 2 * KD * T * 4, [
            ("XM", [P, NT, D], F32), ("PT_hi", [P, 2, T], F32R), ("PT_lo", [P, 2, T], F32R),
            ("Pn", [P, NT, PLE], F32), ("SG", [P, 2, 512], F32)])
        E = put("E", [P, 2, NT, 512], F32, x_off)[0]
        LB = (LB0, LB1, LB2)
        GB, AB = (0, 1, 2), (3, 4, 5)
        JK = put("JK", [P, 512], F32, m_end - 2048)[0]
        JX = put("JX", [P, D], F32, m_off + 2 * KD * T * 4)[0]
        JY = put("JY", [P, D], F32, m_off)[0]

        ps = ctx.enter_context(nc.psum_tensor("ps", [P, 8, 512], F32))
        zT = nc.dram_tensor("zT", [28 * P, T], F32, kind="Internal").ap()
        abD = nc.dram_tensor("abD", [2 * NH * P, T], F32, kind="Internal").ap()
        zN = nc.dram_tensor("zN", [T, 5 * 512], F32, kind="Internal").ap()

        def sem(name):
            return ctx.enter_context(nc.semaphore(name))

        const_ld = sem("constants_loaded")
        const_ok = sem("constants_ready")
        lam_exp = sem("lambda_exponentials")
        waited = sem("waited")
        w_loaded = [sem("unit_loaded_slot0"), sem("unit_loaded_slot1")]
        w_hi = sem("unit_high_part")
        w_lo = sem("unit_low_part")
        w_used = sem("unit_used")
        s_x = [sem(f"x_tiles_loaded_{n}") for n in range(3)]
        s_xm = sem("x_loaded_for_ple")
        s_wr = sem("rows_loaded")
        s_lay = sem("layer_constants_loaded")
        s_out = sem("x_stored")
        s_p = sem("p_loaded")
        zt_st = [sem("zT_stored_stage0"), sem("zT_stored_stage1")]
        zn_st = sem("zN_stored")
        zg_st = sem("gate_stored")
        ab_st = [sem("gla_head_stored"), sem("att_head_stored")]
        s_ab = sem("heads_loaded")
        s_fz, s_v, s_g, s_qk, s_vd = (sem(n) for n in ("gla_qf_loaded", "gla_v_loaded", "gla_g_loaded", "att_qk_loaded", "att_v_loaded"))
        s_gt = [sem("gates_loaded_0"), sem("gates_loaded_1")]

        def steps(name, names, credit=False):
            return Steps(sem(name), names, len(names) if credit else 0)

        lay_dve = steps("layer_dve", ["lay", "slw"])
        n1 = {e: steps(f"norm1_{e}", norm_names(e, False)) for e in ("act", "dve", "pool", "pe")}
        nr = {e: steps(f"resnorm_{e}", norm_names(e, True)) for e in ("act", "dve", "pool", "pe")}
        pb_act = steps("pb_act", [f"ev{u}_{b}_{h}" for u in range(2) for b in range(2) for h in range(2)], credit=True)
        pb_pe = steps("pb_pe", ["blk0", "blk1"])
        pa_pe = steps("pa_pe", [f"a{t}" for t in range(NT - 1)])
        pa_dve = steps("pa_dve", [f"ev{t}" for t in range(NT)], credit=True)
        ga, gd, gp = gla_names()
        gt_pe = steps("gates_pe", ["b0", "b2"])
        gt_act = steps("gates_act", [f"ev{b}_{h}" for b in range(4) for h in range(2)], True)
        G_act, G_dve, G_pe = steps("gla_act", ga, True), steps("gla_dve", gd, True), steps("gla_pe", gp, True)
        G_pool = steps("gla_pool", ["ms", "rs"])
        ta, td, tp = att_names()
        A_act, A_dve, A_pe = steps("att_act", ta, True), steps("att_dve", td, True), steps("att_pe", tp, True)
        A_pool = steps("att_pool", ["ms", "rs"])
        ab_act = steps("ab_act", [f"h{c}" for c in range(KD)])
        ab_dve = steps("ab_dve", [f"l{c}" for c in range(KD)])
        br_pe = steps("br_pe", ["blk0", "blk1"])
        br_act = steps("br_act", [f"{k}{u}_{b}" for u in range(2) for b in range(2) for k in ("sg", "mh")])
        br_dve = steps("br_dve", [f"{k}{u}_{b}" for u in range(2) for b in range(2) for k in ("ta0", "ta1", "tb0", "tb1", "m", "ml")], True)
        wo_pe = steps("wo_pe", [f"a{c}_{t}" for c in range(2) for t in range(NT - 1)])
        wo_act = steps("wo_act", [f"sq{t}" for t in range(NT)])
        wo_dve = steps("wo_dve", [f"y{t}" for t in range(NT)])
        up_pe = steps("up_pe", ["blk0", "blk1"])
        up_act = steps("up_act", [f"{k}{u}" for u in range(2) for k in ("cg0_", "cg1_", "cv0_", "cv1_", "ge")], True)
        up_dve = steps("up_dve", [f"{k}{u}" for u in range(2) for k in
                                  ("cp", "g0l", "g0r", "g1l", "g1r", "v0l", "v0r", "v1l", "v1r", "pr")], True)
        dn_pe = steps("dn_pe", [f"a{c}_{t}" for c in range(2) for t in range(NT - 1)])
        dn_act = steps("dn_act", [f"ph{j}" for j in range(12)] + [f"sq{t}" for t in range(NT)] + [f"ph{j}" for j in range(12, 22)])
        dn_dve = steps("dn_dve", [f"pl{j}" for j in range(12)] + [f"y{t}" for t in range(NT)] + [f"pl{j}" for j in range(12, 22)])
        pt_pe = steps("pt_pe", ["tr0", "tr1", "tr2"])
        pt_act = steps("pt_act", ["h0", "h1", "h2"])
        pt_dve = steps("pt_dve", ["l0", "l1", "l2"])
        pe_pe = steps("ple_pe", [f"e{c}_{t}" for c in range(2) for t in range(NT - 1)])
        pe_act = steps("ple_act", [f"e{c}_{t}" for c in range(2) for t in range(NT)])
        pg_pe = steps("gate_pe", [f"g{c}_{t}" for c in range(2) for t in range(NT - 1)])
        pg_act = steps("gate_act", [x for c in range(2) for t in range(NT + 1)
                                    for x in ([f"s{c}_{t}"] if t < NT else []) + ([f"q{c}_{t - 1}"] if t else [])])
        pg_dve = steps("gate_dve", [f"m{c}_{t}" for c in range(2) for t in range(NT)])
        fin_pool = steps("fin_pool", [f"{k}{t}" for t in range(NT) for k in ("s", "m", "r")])
        fin_dve = steps("fin_dve", [f"{k}{t}" for t in range(NT) for k in ("a", "b", "x")], True)

        def unit(L, j, i=None):
            n, half = L * N_UNITS + j, L * (N_UNITS // 2) + j // 2
            return (n, half, j % 2) if i is None else (n + i * 2, half + i, j % 2)

        block = ctx.enter_context(nc.Block())

        @block.sync
        def _(sp):
            for dst, src in ((ident[:], ident_in), (X[:, 0, 0:len(LEVELS) * P], masks_in), (lbl[:], lb_logits)):
                sp.dma_start(dst, src).then_inc(const_ld, 16)
            sp.dma_start(hn[:, 0:2 * DEPTH * 2 * DA_DH], lam_in.partition_broadcast(P)).then_inc(const_ld, 16)
            sp.dma_start(out, x_in).then_inc(s_out, 16)
            for s in (pb_act, pa_dve, gt_act, G_act, G_dve, G_pe, A_act, A_dve, A_pe, br_dve, up_act, up_dve, fin_dve):
                sp.sem_inc(s.sem, s.credit)
            for s in (w_lo, w_used):
                sp.sem_inc(s, CREDIT)
            for s in (*zt_st, zn_st, zg_st, *ab_st):
                sp.sem_inc(s, 16)

            def load(u, parts, width=ISLOTS):
                n, _, s = u
                sp.wait_ge(w_lo, n + 1)
                at = 0
                for src in parts:
                    cols = width // len(parts)
                    sp.dma_start(raw[:, s, at:at + cols].rearrange("p (k n) -> p k n", n=src.shape[-1]), src)\
                        .then_inc(w_loaded[s], 16 * 2 // len(parts))
                    at += cols

            def rows(w, L, k0, nk, c0, nc_):
                return w[bass.ds(L, 1), k0 * P:(k0 + nk) * P, bass.ds(c0, nc_)].rearrange("o (k p) n -> p (o k) n", p=P)

            with sp.Fori(0, DEPTH) as L:
                with sp.Fori(0, 3) as i:
                    for u in range(2):
                        load(unit(L, U_PB + u, i), [rows(w_in, L, 0, KD, i * 512 + u * 256, 256)])
                with sp.Fori(0, 5) as i:
                    for u in range(2):
                        load(unit(L, U_PA + u, i), [rows(w_in, L, 4 * u, 4, i * 512 + 3 * HW, 512)])
                with sp.Fori(0, 4) as i:
                    for u in range(2):
                        load(unit(L, U_GT + u, i), [rows(w_in, L, 0, KD, i * 512 + (8 * HW + u * 256), 256)])
                with sp.Fori(0, 2) as i:
                    for u in range(2):
                        load(unit(L, U_BR + u, i), [rows(w, L, 0, 4, i * 512 + u * 256, 256) for w in (w_a, w_b)])
                with sp.Fori(0, 2) as i:
                    for u in range(2):
                        load(unit(L, U_WO + u, i), [rows(w_out, L, 4 * u, 4, i * 512, 512)])
                with sp.Fori(0, NFF // 2) as i:
                    for u in range(2):
                        load(unit(L, U_UP + u, i), [rows(w_up, L, 0, KD, i * 256 + (u * P + half), P) for half in (0, FF)])
                for c in range(2):
                    for j in range(11):
                        load(unit(L, U_DN + c * 11 + j), [rows(w_down, L, 2 * j, 2, c * 512, 512)], 1024)
                for c in range(2):
                    load(unit(L, U_PE + c), [rows(w_ple, L, 0, 2, c * 512, 512)], 1024)
                for c in range(2):
                    for u in range(2):
                        load(unit(L, U_PG + 2 * c + u), [rows(w_ple_gate, L, 4 * u, 4, c * 512, 512)])

        @block.tensor
        def _(pe):
            mm = nc.tensor.matmul
            pe.wait_ge(const_ld, 64)
            PASSES = ((0, 0), (0, 1), (1, 0))
            hT, mT, PH, PT, W = (hT_hi, hT_lo), (mT_hi, mT_lo), (PH_hi, PH_lo), (PT_hi, PT_lo), (whi, wlo)

            def unit_ready(u):
                pe.wait_ge(w_lo, u[0] + (1 + CREDIT))

            def feature_block(rhs, s, chunks, banks):
                n = len(chunks) * 3
                i = 0
                for w0, k in chunks:
                    for a, b in PASSES:
                        for (t0, tn), bank in zip(HALVES, banks):
                            ins = mm(ps[:, bank, 0:tn], W[b][:, s, w0:w0 + P], rhs[a][:, k, t0:t0 + tn],
                                     start=(i == 0), stop=(i == n - 1))
                        i += 1
                return ins

            def token_chunks(lhs, s, chunks, first, last, counter, names, free=None):
                for i, (w, k) in enumerate(chunks):
                    for t in range(NT):
                        if free and first and i == 0:
                            free(t)
                        for q, (a, b) in enumerate(PASSES):
                            end = last and i == len(chunks) - 1 and q == 2
                            ins = mm(ps[:, t, :], lhs[a][:, k, t * P:(t + 1) * P] if not callable(k) else k(a, t),
                                     W[b][:, s, w * 512:(w + 1) * 512], start=(first and i == 0 and q == 0), stop=end)
                        if end and t < NT - 1:
                            ins.then_inc(*counter.step(names[t]))
                ins.then_inc(w_used, 1)

            def norm_transposes(c, it, ahead=None):
                for t in range(NT):
                    if ahead and t == 0:
                        ahead(0)
                    if ahead and t + 1 < NT:
                        ahead(t + 1)
                    pe.wait_ge(c["dve"].sem, c["dve"].at(it, f"hn{t}"))
                    for h in range(2):
                        if t:
                            pe.wait_ge(c["dve"].sem, c["dve"].at(it, f"lo{t - 1}_{h}"))
                        for k in range(4):
                            ins = nc.tensor.transpose(ps[:, 6 + h, k * P:(k + 1) * P],
                                                      hn[:, (4 * h + k) * P:(4 * h + k + 1) * P], ident[:])
                        ins.then_inc(*c["pe"].step(f"tr{t}_{h}"))

            def gla_keys(it):
                pe.wait_ge(G_dve.sem, G_dve.at(it, "kh"))
                for b in range(3):
                    for i in range(4):
                        d, c = divmod(4 * b + i, NT)
                        ins = nc.tensor.transpose(ps[:, GB[b], i * P:(i + 1) * P], LB2[:, d, c * P:(c + 1) * P], ident[:])
                    ins.then_inc(*G_pe.step(f"trk{b}"))
                pe.wait_ge(G_act.sem, G_act.at(it, "kht1"))
                for c in range(NT):
                    o = ps[:, GB[c // 4], (c % 4) * P:(c % 4 + 1) * P]
                    mm(o, Kb[:, 0, c * P:(c + 1) * P], Qb[:, c * P:(c + 1) * P], start=True, stop=False)
                    ins = mm(o, Kb[:, 1, c * P:(c + 1) * P], Qb[:, c * P:(c + 1) * P], start=False, stop=True)
                ins.then_inc(*G_pe.step("diag"))
                pe.wait_ge(G_act.sem, G_act.at(it, "kht2"))
                pe.wait_ge(s_v, it * 16 + 16)
                pe.wait_ge(G_dve.sem, G_dve.at(it, "at0"))
                for n, (d, c) in enumerate(STATES):
                    ins = mm(ps[:, GB[2 - 2 * (n // 4)], (n % 4) * P:(n % 4 + 1) * P], khT[:, d * NT + c, :], vN[:, c, :],
                             start=True, stop=True)
                ins.then_inc(*G_pe.step("ds"))

            def gla_level(it, l):
                h, buf = LEVELS[l], LB[l % 3]
                pe.wait_ge(G_dve.sem, G_dve.at(it, f"mq{l}"))
                for d in range(2):
                    n = 2 * l + d
                    pe.wait_ge(G_dve.sem, G_dve.at(it, f"cp{(n - 3) // 2}_{(n - 3) % 2}" if n >= 3 else "s1"))
                    for c in range(NT):
                        ins = mm(ps[:, GB[(n + 1) % 3], c * 64:(c + 1) * 64], buf[:, d, c * P:(c + 1) * P],
                                 view(buf[:], d * T + c * P + (0 if d else h), [[2 * h, 64 // h], [1, h]]),
                                 start=True, stop=True)
                    ins.then_inc(*G_pe.step(f"lv{l}_{d}"))

            def gla_out(it):
                pe.wait_ge(G_dve.sem, G_dve.at(it, f"cp{len(LEVELS) - 1}_1"))
                for c in range(NT):
                    o = ps[:, GB[c // 4], (c % 4) * P:(c % 4 + 1) * P]
                    carried = [(d, n) for d, n, cc in CARRIES if cc == c]
                    mm(o, AT[:, c, :], vN[:, c, :], start=True, stop=False)
                    for i, (d, n) in enumerate(carried):
                        ins = mm(o, QH[:, d, c * P:(c + 1) * P], S[:, n, :], start=False, stop=(i == len(carried) - 1))
                    if c in (3, 5):
                        ins.then_inc(*G_pe.step(f"o{c // 4}"))

            def out_transposes(dve_steps, pe_steps, it, o, banks):
                for c in range(NT):
                    if c in (0, 4):
                        pe.wait_ge(dve_steps.sem, dve_steps.at(it, f"on{3 if c == 0 else 5}"))
                    ins = nc.tensor.transpose(ps[:, banks[c // 4], (c % 4) * P:(c % 4 + 1) * P], o[:, c, :], ident[:])
                    if c in (3, 5):
                        ins.then_inc(*pe_steps.step(f"tro{c // 4}"))

            def att_turn(it):
                pe.wait_ge(A_dve.sem, A_dve.at(it, "radd"))
                for b in range(3):
                    for i in range(4):
                        a, t = divmod(4 * b + i, NT)
                        ins = nc.tensor.transpose(ps[:, AB[b], i * P:(i + 1) * P], T1[:, a, t, :], ident[:])
                    ins.then_inc(*A_pe.step(f"trq{b}"))
                pe.wait_ge(A_act.sem, A_act.at(it, "qk2"))

            def att_scores(it, q):
                k0, kn = SEQ_OF[q]
                if q:
                    pe.wait_ge(A_act.sem, A_act.at(it, f"e{q - 1}_1"))
                for m in range(2):
                    rows_ = slice(m * DA_DH, (m + 1) * DA_DH)
                    ins = mm(ps[:, AB[m], 0:kn], qkT[rows_, 0, q * P:(q + 1) * P], qkT[rows_, 1, k0:k0 + kn], start=True, stop=True)
                ins.then_inc(*A_pe.step(f"sc{q}"))

            def att_turn_weights(it, q):
                pe.wait_ge(A_dve.sem, A_dve.at(it, f"al{q}"))
                if q:
                    pe.wait_ge(A_act.sem, A_act.at(it, f"oc{q - 1}"))
                for j in range(SEQ_OF[q][1] // P):
                    ins = nc.tensor.transpose(ps[:, AB[2], j * P:(j + 1) * P], PR[:, q % 2, 0, j * P:(j + 1) * P], ident[:])
                ins.then_inc(*A_pe.step(f"tra{q}"))

            def att_values(it, q):
                k0, kn = SEQ_OF[q]
                pe.wait_ge(A_act.sem, A_act.at(it, f"at{q}"))
                if q == 0:
                    pe.wait_ge(s_vd, it * 16 + 16)
                for j in range(kn // P):
                    ins = mm(ps[:, AB[2], 0:P], At[:, q % 2, j * P:(j + 1) * P], vD[:, k0 // P + j, :],
                             start=(j == 0), stop=(j == kn // P - 1))
                ins.then_inc(*A_pe.step(f"av{q}"))

            def gate_part(it, L, h, n):
                b, half = divmod(n, 2)
                w = unit(L, U_GT + b // 2, h)
                if half == 0:
                    if b % 2 == 0:
                        unit_ready(w)
                    pe.wait_ge(gt_act.sem, gt_act.at(it, f"ev{b - 1}_1") if b else gt_act.before(it, "ev3_1"))
                for k in range(4 * half, 4 * half + 4):
                    for q, (a, c) in enumerate(PASSES):
                        for (t0, tn), bank in zip(HALVES, (6, 7)):
                            ins = mm(ps[:, bank, 0:tn], W[c][:, w[2], k * 256 + (b % 2) * P:k * 256 + (b % 2 + 1) * P],
                                     hT[a][:, k, t0:t0 + tn], start=(k == 0 and q == 0), stop=(k == KD - 1 and q == 2))
                if half:
                    ins.then_inc(*(gt_pe.step(f"b{b}") if b % 2 == 0 else (w_used, 1)))

            with pe.Fori(0, DEPTH) as L:
                norm_transposes(n1, L)
                pe.wait_ge(n1["dve"].sem, n1["dve"].last(L))
                pe.sem_inc(waited, 1)
                with pe.Fori(0, N_PB // 2) as i:
                    it = L * (N_PB // 2) + i
                    for u in range(2):
                        w = unit(L, U_PB + u, i)
                        unit_ready(w)
                        for b in range(2):
                            pe.wait_ge(pb_act.sem, pb_act.before(it, f"ev{u}_{b}_1"))
                            ins = feature_block(hT, w[2], [(k * 256 + b * P, k) for k in range(KD)],
                                                (4 * u + 2 * b, 4 * u + 2 * b + 1))
                            ins.then_inc(*(pb_pe.step(f"blk{u}") if b == 0 else (w_used, 1)))
                pe.wait_ge(pb_act.sem, pb_act.last(L * (N_PB // 2) + (N_PB // 2 - 1)))
                pe.sem_inc(waited, 1)
                with pe.Fori(0, 5) as g:
                    it = L * 5 + g
                    for u in range(2):
                        w = unit(L, U_PA + u, g)
                        unit_ready(w)
                        token_chunks(hT, w[2], [(k, 4 * u + k) for k in range(4)], u == 0, u == 1, pa_pe,
                                     [f"a{t}" for t in range(NT - 1)],
                                     lambda t: pe.wait_ge(pa_dve.sem, pa_dve.before(it, f"ev{t}")))
                pe.wait_ge(pa_dve.sem, pa_dve.last(L * 5 + 4))
                pe.sem_inc(waited, 1)
                with pe.Fori(0, NH) as h:
                    it = L * NH + h
                    gate_part(it, L, h, 0)
                    att_turn(it)
                    att_scores(it, 0)
                    gate_part(it, L, h, 1)
                    gla_keys(it)
                    for k in range(len(LEVELS)):
                        if k + 1 < NT:
                            att_scores(it, k + 1)
                        gla_level(it, k)
                        if k:
                            att_values(it, k - 1)
                        if k < NT:
                            if k % 2 == 0:
                                gate_part(it, L, h, 2 + k // 2)
                            att_turn_weights(it, k)
                    gate_part(it, L, h, 5)
                    gla_out(it)
                    gate_part(it, L, h, 6)
                    out_transposes(A_dve, A_pe, it, O2, (AB[0], AB[1]))
                    gate_part(it, L, h, 7)
                    out_transposes(G_dve, G_pe, it, O1, (GB[2], GB[0]))
                with pe.Fori(0, 2) as i:
                    it = L * 2 + i
                    for u in range(2):
                        w = unit(L, U_BR + u, i)
                        unit_ready(w)
                        pe.wait_ge(ab_dve.sem, ab_dve.last(L))
                        for b in range(2):
                            pe.wait_ge(br_dve.sem, br_dve.at(it, f"tb10_{b}") if u else br_dve.before(it, f"tb11_{b}"))
                            feature_block(hT, w[2], [(k * 256 + b * P, k) for k in range(4)], (4 * b, 4 * b + 1))
                            ins = feature_block(hT, w[2], [(1024 + k * 256 + b * P, 4 + k) for k in range(4)], (4 * b + 2, 4 * b + 3))
                            ins.then_inc(*(br_pe.step(f"blk{u}") if b == 0 else (w_used, 1)))
                pe.wait_ge(br_dve.sem, br_dve.last(L * 2 + 1))
                for c in range(2):
                    for u in range(2):
                        w = unit(L, U_WO + 2 * c + u)
                        unit_ready(w)
                        token_chunks(mT, w[2], [(k, 4 * u + k) for k in range(4)], u == 0, u == 1, wo_pe,
                                     [f"a{c}_{t}" for t in range(NT - 1)],
                                     (lambda t: pe.wait_ge(wo_dve.sem, wo_dve.at(L, f"y{t}"))) if c else None)
                norm_transposes(nr, L * 2)
                pe.wait_ge(nr["dve"].sem, nr["dve"].last(L * 2))
                pe.sem_inc(waited, 1)
                with pe.Fori(0, NFF // 2) as i:
                    it = L * (NFF // 2) + i
                    for u in range(2):
                        w = unit(L, U_UP + u, i)
                        unit_ready(w)
                        for b in range(2):
                            pe.wait_ge(up_dve.sem, up_dve.before(it, f"{'gv'[b]}1r{u}"))
                            ins = feature_block(hT, w[2], [(b * 1024 + k * P, k) for k in range(KD)],
                                                (4 * u + 2 * b, 4 * u + 2 * b + 1))
                            ins.then_inc(*(up_pe.step(f"blk{u}") if b == 0 else (w_used, 1)))
                pe.wait_ge(up_dve.sem, up_dve.last(L * (NFF // 2) + (NFF // 2 - 1)))
                for c in range(2):
                    for j in range(11):
                        n = 11 * c + j
                        w = unit(L, U_DN + n)
                        unit_ready(w)
                        pe.wait_ge(dn_dve.sem, dn_dve.at(L, f"pl{n}"))
                        token_chunks(PH, w[2], [(k, (lambda a, t, k=k: PH[a][:, n % 2, k, t * P:(t + 1) * P])) for k in range(2)],
                                     j == 0, j == 10, dn_pe, [f"a{c}_{t}" for t in range(NT - 1)],
                                     (lambda t: pe.wait_ge(dn_dve.sem, dn_dve.at(L, f"y{t}"))) if c else None)
                pe.wait_ge(s_p, L * 16 + 16)
                for b in range(3):
                    if b == 2:
                        pe.wait_ge(pt_dve.sem, pt_dve.at(L, "l0"))
                    for i in range(4):
                        k, t = divmod(4 * b + i, NT)
                        ins = nc.tensor.transpose(ps[:, 6 + b % 2, i * P:(i + 1) * P], Pn[:, t, k * P:(k + 1) * P], ident[:])
                    ins.then_inc(*pt_pe.step(f"tr{b}"))
                pe.wait_ge(pt_dve.sem, pt_dve.last(L))
                def e_tile(c, t):
                    if c:
                        pe.wait_ge(pe_act.sem, pe_act.at(L, f"e0_{t}"))
                    else:
                        pe.wait_ge(nr["dve"].sem, nr["dve"].at(L * 2 + 1, f"ra{t}"))
                    for k in range(2):
                        for q, (a, b) in enumerate(PASSES):
                            ins = mm(ps[:, t, :], PT[a][:, k, t * P:(t + 1) * P], W[b][:, (U_PE + c) % 2, k * 512:(k + 1) * 512],
                                     start=(k == 0 and q == 0), stop=(k == 1 and q == 2))
                    ins.then_inc(*(pe_pe.step(f"e{c}_{t}") if t < NT - 1 else (w_used, 1)))

                unit_ready(unit(L, U_PE))
                norm_transposes(nr, L * 2 + 1, lambda t: e_tile(0, t))
                unit_ready(unit(L, U_PE + 1))
                for t in range(NT):
                    e_tile(1, t)
                pe.wait_ge(nr["dve"].sem, nr["dve"].last(L * 2 + 1))
                for c in range(2):
                    for u in range(2):
                        w = unit(L, U_PG + 2 * c + u)
                        unit_ready(w)
                        token_chunks(hT, w[2], [(k, 4 * u + k) for k in range(4)], u == 0, u == 1, pg_pe,
                                     [f"g{c}_{t}" for t in range(NT - 1)],
                                     (lambda t: pe.wait_ge(pg_act.sem, pg_act.at(L, f"s0_{t}"))) if c else
                                     (lambda t: pe.wait_ge(pe_act.sem, pe_act.at(L, f"e1_{t}"))))

        mark = {}

        @block.vector
        def _(dve):
            v = nc.vector
            count = [0]

            def link(ins, name=None):
                count[0] += 1
                ins.then_inc(const_ok, 1)
                dve.wait_ge(const_ok, count[0])
                if name:
                    mark[name] = count[0]

            def done(c, it, name):
                dve.wait_ge(c.sem, c.at(it, name))

            link(v.memset(rmask[:], 1))
            link(v.memset(view(rmask[:], 0, [[P, NT]]), 0))
            link(v.memset(half_neg[:], -0.5))
            dve.wait_ge(const_ld, 64)
            link(v.tensor_copy(masks[:].rearrange("p a j -> p (a j)"), X[:, 0, 0:len(LEVELS) * P]))
            link(v.tensor_tensor(view(hn[:], 512, [[128, 2], [64, 2], [1, 64]]), view(hn[:], 0, [[256, 2], [128, 2], [1, 64]]),
                                 view(hn[:], 64, [[256, 2], [128, 2], [1, 64]]), ALU.mult))
            link(v.tensor_reduce(lams[:, 0:4], view(hn[:], 512, [[64, 4], [1, 64]]), AX_X, ALU.add))
            l0, l1 = view(lbl[:], 0, [[2, 8]]), view(lbl[:], 1, [[2, 8]])
            link(v.tensor_tensor(lbs[:, 0:8], l0, l1, ALU.max))
            link(v.tensor_tensor(view(lbs[:], 8, [[2, 8], [1, 2]]), view(lbl[:], 0, [[2, 8], [1, 2]]),
                                 view(lbs[:], 0, [[1, 8], [0, 2]]), ALU.subtract), "exponents")
            dve.wait_ge(lam_exp, 2)
            e0, e1 = view(lbs[:], 24, [[2, 8]]), view(lbs[:], 25, [[2, 8]])
            link(v.tensor_tensor(lbs[:, 40:48], e0, e1, ALU.add))
            link(v.reciprocal(lbs[:, 48:56], lbs[:, 40:48]))
            link(v.tensor_tensor(view(lbs[:], 8, [[2, 8], [1, 2]]), view(lbs[:], 24, [[2, 8], [1, 2]]),
                                 view(lbs[:], 48, [[1, 8], [0, 2]]), ALU.mult))
            p0, p1 = view(lbs[:], 8, [[2, 8]]), view(lbs[:], 9, [[2, 8]])
            link(v.tensor_tensor(lbs[:, 40:48], p0, p1, ALU.add))
            link(v.tensor_tensor(lbs[:, 56:64], lbs[:, 40:48], p0, ALU.subtract))
            link(v.tensor_tensor(lbs[:, 48:56], p0, p0, ALU.subtract))
            for l in range(DEPTH):
                lb = lbs[:, 48 + 8 * l:56 + 8 * l]
                link(v.tensor_scalar(view(lbtab[:], 16 * l, [[2, 8]]), lb, -1.0, 1.0, ALU.mult, ALU.add))
                link(v.tensor_scalar(view(lbtab[:], 16 * l + 1, [[2, 8]]), lb, LB_FLOOR, None, ALU.max))
                link(v.tensor_tensor(lams[:, 8 + l:9 + l], lams[:, 5 + 2 * l:6 + 2 * l], lams[:, 4 + 2 * l:5 + 2 * l], ALU.subtract))
                link(v.tensor_scalar(laytab[:, 2 * l:2 * l + 1], lams[:, 8 + l:9 + l], -lambda_init(l), None, ALU.add))
                link(v.memset(laytab[:, 2 * l + 1:2 * l + 2], 1.0 - lambda_init(l)), "all")

            def low(u, width=ISLOTS):
                n, _, s = u
                dve.wait_ge(w_hi, n + 1)
                v.tensor_tensor(wlo[:, s, 0:width], raw[:, s, 0:width], whi[:, s, 0:width].bitcast(F32), ALU.subtract)\
                    .then_inc(w_lo, 1)

            def norm_stage(c, it, x, weight, residual=None, bank_ready=None, extra=None):
                for s in range(NT + 2):
                    r, n, h = s, s - 1, s - 2
                    if r < NT and residual is not None:
                        bank_ready(r)
                        done(c["pool"], it, f"ry{r}")
                        if r:
                            done(c["dve"], it, f"rx{r - 1}")
                        v.scalar_tensor_tensor(TMP[:, 512:D], ps[:, r, :], rsy[:, r:r + 1], wrows[:, 1, 512:D], ALU.mult, ALU.mult)\
                            .then_inc(*c["dve"].step(f"ra{r}"))
                        v.scalar_tensor_tensor(TMP[:, 0:512], residual[:, r, :], rsy[:, r:r + 1], wrows[:, 1, 0:512], ALU.mult, ALU.mult)\
                            .then_inc(*c["dve"].step(f"rb{r}"))
                        done(c["dve"], it, f"rb{r}")
                        v.tensor_tensor(x[:, r, :], x[:, r, :], TMP[:], ALU.add).then_inc(*c["dve"].step(f"rx{r}"))
                    if 0 <= n < NT:
                        done(c["pool"], it, f"rs{n}")
                        if n:
                            done(c["pe"], it, f"tr{n - 1}_1")
                        if weight:
                            v.scalar_tensor_tensor(hn[:], x[:, n, :], rsx[:, n:n + 1], wrows[:, 0, :], ALU.mult, ALU.mult)\
                                .then_inc(*c["dve"].step(f"hn{n}"))
                        else:
                            v.tensor_scalar(hn[:], x[:, n, :], rsx[:, n:n + 1], None, ALU.mult).then_inc(*c["dve"].step(f"hn{n}"))
                    if h >= 0:
                        for k in range(2):
                            done(c["act"], it, f"hi{h}_{k}")
                            v.tensor_tensor(hT_lo[:, 4 * k:4 * k + 4, h * P:(h + 1) * P],
                                            ps[:, 6 + k, :].rearrange("p (k t) -> p k t", k=4),
                                            hT_hi[:, 4 * k:4 * k + 4, h * P:(h + 1) * P].bitcast(F32), ALU.subtract)\
                                .then_inc(*c["dve"].step(f"lo{h}_{k}"))

            def normed(it, c_dve, c_pool, o, st, weight):
                done(c_pool, it, "rs")
                for c in range(NT):
                    v.scalar_tensor_tensor(o[:, c, :], o[:, c, :], st[:, 2, c:c + 1], weight(c), ALU.mult, ALU.mult)\
                        .then_inc(*c_dve.step(f"on{c}"))

            def gla_gates(it):
                G = G_dve
                dve.wait_ge(G_pe.sem, G_pe.before(it, "tro1"))
                v.tensor_copy(lb_now[:], lbtab[:, bass.ds(it * 4, 4)]).then_inc(*G.step("lb"))
                done(G_act, it, "silu_q")
                v.tensor_scalar(Qb[:], FZ[:, 0, :], float(P) ** -0.5, None, ALU.mult).then_inc(*G.step("qs"))
                done(G_act, it, "sig_neg")
                done(G, it, "lb")
                for d in range(2):
                    v.tensor_scalar(Kb[:, d, :], FZ[:, 1 + d, :], lb_now[:, 2 * d:2 * d + 1], None, ALU.mult).then_inc(*G.step(f"k{d}"))
                for d in range(2):
                    v.tensor_scalar(LB0[:, d, :], LB0[:, d, :], lb_now[:, 2 * d:2 * d + 1], lb_now[:, 2 * d + 1:2 * d + 2],
                                    ALU.mult, ALU.add).then_inc(*G.step(f"f{d}"))
                done(G, it, "f1")
                v.tensor_scalar(LB1[:], LB0[:], LN_SPLIT, None, ALU.max).then_inc(*G.step("fa"))
                v.tensor_scalar(LB2[:], LB0[:], 1.0 / LN_SPLIT, 1.0, ALU.mult, ALU.min).then_inc(*G.step("fb"))

            def gla_sums(it):
                G = G_dve
                done(G_act, it, "ln2")
                done(G, it, "fb")
                v.tensor_tensor(LB0[:], LB1[:], LB2[:], ALU.add).then_inc(*G.step("g"))
                done(G, it, "g")
                v.tensor_tensor_scan(B[:, 0, :], rmask[:], LB0[:, 0, :], 0.0, ALU.mult, ALU.add).then_inc(*G.step("scan0"))
                v.tensor_tensor_scan(B[:, 1, ::-1], rmask[:], LB0[:, 1, ::-1], 0.0, ALU.mult, ALU.add).then_inc(*G.step("scan1"))
                done(G_act, it, "silu_g")
                v.tensor_tensor(gN[:], gN[:], view(gn_row[:], 0, [[0, NT], [1, P]]), ALU.mult).then_inc(*G.step("gw"))
                done(G, it, "scan1")
                differences(it, 0)

            def differences(it, l):
                h, out = LEVELS[l], LB[l % 3]
                nb_ = T // (2 * h)
                full = [[T, 2], [2 * h, nb_], [1, 2 * h]]
                v.tensor_tensor(view(out[:], 0, full), view(B[:], 0, full),
                                view(B[:], h - 1, [[T + 1, 2], [2 * h, nb_], [0, 2 * h]]), ALU.subtract).then_inc(*G_dve.step(f"D{l}"))

            def gla_decayed(it):
                G = G_dve
                done(G_act, it, "exp_b")
                ends = [[T - P + 1, 2], [P, NT]]
                v.tensor_copy(decay[:], view(LB1[:], P - 1, ends)).then_inc(*G.step("dec"))
                v.tensor_tensor(QH[:], view(Qb[:], 0, [[0, 2], [1, T]]), LB1[:], ALU.mult).then_inc(*G.step("qh"))
                v.tensor_tensor(view(LB2[:], 0, [[T, 2], [P, NT], [1, P]]), view(B[:], 0, [[T, 2], [P, NT], [1, P]]),
                                view(B[:], P - 1, ends + [[0, P]]), ALU.subtract).then_inc(*G.step("dl"))
                done(G_act, it, "exp_l")
                v.tensor_tensor(LB2[:], LB2[:], Kb[:], ALU.mult).then_inc(*G.step("kh"))
                done(G, it, "qh")
                differences(it, 1)

            def gla_diagonal(it):
                done(G_pe, it, "diag")
                for k, n in ((0, 4), (1, 2)):
                    v.tensor_tensor(AT[:, 4 * k:4 * k + n, :], ps[:, GB[k], 0:n * P].rearrange("p (c t) -> p c t", t=P),
                                    view(ident[:], 0, [[0, n], [1, P]]), ALU.mult).then_inc(*G_dve.step(f"at{k}"))

            def level_keys(it, l):
                G, h = G_dve, LEVELS[l]
                nb_ = T // (2 * h)
                keys, queries = [[T + h, 2], [2 * h, nb_], [1, h]], [[T - h, 2], [2 * h, nb_], [1, h]]
                buf = LB[l % 3]
                done(G_act, it, f"xk{l}")
                v.tensor_tensor(view(buf[:], 0, keys), view(buf[:], 0, keys), view(Kb[:], 0, keys), ALU.mult).then_inc(*G.step(f"mk{l}"))
                done(G_act, it, f"xq{l}")
                v.tensor_tensor(view(buf[:], h, queries), view(buf[:], h, queries),
                                view(Qb[:], h, [[-h, 2], [2 * h, nb_], [1, h]]), ALU.mult).then_inc(*G.step(f"mq{l}"))
                if l + 2 < len(LEVELS):
                    if l == 0:
                        done(G_pe, it, "trk2")
                        done(G, it, "kh")
                    else:
                        done(G_pe, it, f"lv{l - 1}_1")
                    differences(it, l + 2)

            def carried_states(it):
                G = G_dve
                done(G_pe, it, "ds")
                for k in range(2):
                    v.tensor_copy(S[:, 4 * k:4 * k + 4, :], ps[:, GB[2 - 2 * k], :].rearrange("p (n v) -> p n v", v=P)).then_inc(*G.step(f"s{k}"))
                done(G, it, "s1")
                for i, (n, d, c) in enumerate(((2, 0, 3), (3, 0, 4), (6, 1, 4), (7, 1, 3))):
                    v.scalar_tensor_tensor(S[:, n, :], S[:, n - 1, :], decay[:, d, c:c + 1], S[:, n, :], ALU.mult, ALU.add)\
                        .then_inc(*G.step(f"s{2 + i}"))
                    done(G, it, f"s{2 + i}")

            def copy_level(it, l):
                G, h = G_dve, LEVELS[l]
                for d in range(2):
                    done(G_pe, it, f"lv{l}_{d}")
                    done(G, it, f"cp{l}_0" if d else f"cp{l - 1}_1" if l else "at1")
                    dve.sem_inc(waited, 1)
                    v.copy_predicated(view(AT[:], 0 if d else h, [[P, NT], [2 * h, 64 // h], [1, h]]),
                                      view(masks[:], (d * len(LEVELS) + l) * 64, [[0, NT], [h, 64 // h], [1, h]]),
                                      view(ps[:], GB[(2 * l + d + 1) % 3] * 512, [[64, NT], [h, 64 // h], [1, h]]))\
                        .then_inc(*G.step(f"cp{l}_{d}"))

            def gla_output(it):
                for k, n in ((0, 4), (1, 2)):
                    done(G_act, it, f"sq{k}")
                    v.tensor_copy(O1[:, 4 * k:4 * k + n, :],
                                  ps[:, GB[k], 0:n * P].rearrange("p (c v) -> p c v", v=P)).then_inc(*G_dve.step(f"o{k}"))
                v.tensor_reduce(st_g[:, 0, :], SQ1[:], AX_X, ALU.add).then_inc(*G_dve.step("ss"))

            def att_rope(it, L):
                A = A_dve
                dve.wait_ge(s_qk, it * 32 + 32)
                dve.wait_ge(s_wr, L * 96 + 32)
                dve.wait_ge(ab_st[1], it * 16 + 16)
                v.tensor_tensor(view(T1[:], 0, [[T, 2], [1, T]]), view(QK[:], 0, [[T, 2], [1, T]]),
                                view(rope[:], 0, [[0, 2], [1, T]]), ALU.mult).then_inc(*A.step("cqk"))
                for a, n in ((0, "s_q"), (1, "s_k")):
                    half = DA_DH // 2
                    v.tensor_tensor(view(T2[:], a * T, [[DA_DH, 2 * NT], [half, 2], [1, half]]),
                                    view(QK[:], a * T + half, [[DA_DH, 2 * NT], [-half, 2], [1, half]]),
                                    view(rope[:], T, [[DA_DH, 2 * NT], [half, 2], [1, half]]), ALU.mult).then_inc(*A.step(n))
                done(A, it, "s_k")
                v.tensor_tensor(T1[:], T1[:], T2[:], ALU.add).then_inc(*A.step("radd"))

            def att_max(it, n):
                A, p = A_dve, n % 2
                done(A_pe, it, f"sc{n}")
                v.tensor_reduce(mx[:, p, :], ps[:, AB[0]:AB[0] + 2, 0:SEQ_OF[n][1]], AX_X, ALU.max, negate=True).then_inc(*A.step(f"mx{n}"))
                done(A, it, f"mx{n}")
                v.tensor_scalar(nb[:, p, :], mx[:, p, :], DA_DH ** -0.5, None, ALU.mult).then_inc(*A.step(f"nb{n}"))

            def att_weights(it, q):
                A, p, kn = A_dve, q % 2, SEQ_OF[q][1]
                done(A_act, it, f"e{q}_1")
                v.reciprocal(rc[:, p, :], sm[:, p, :]).then_inc(*A.step(f"rc{q}"))
                done(A, it, f"rc{q}")
                v.tensor_tensor(lr[:, p:p + 1], rc[:, p, 1:2], lay_now[:, 0:1], ALU.mult).then_inc(*A.step(f"lr{q}"))
                done(A, it, f"lr{q}")
                v.tensor_scalar(PR[:, p, 1, 0:kn], PR[:, p, 1, 0:kn], lr[:, p:p + 1], None, ALU.mult).then_inc(*A.step(f"a{q}"))
                done(A, it, f"a{q}")
                v.scalar_tensor_tensor(PR[:, p, 0, 0:kn], PR[:, p, 0, 0:kn], rc[:, p, 0:1], PR[:, p, 1, 0:kn],
                                       ALU.mult, ALU.add).then_inc(*A.step(f"al{q}"))

            def mixers(it, L, h):
                gla_gates(it)
                att_rope(it, L)
                gla_sums(it)
                att_max(it, 0)
                gla_decayed(it)
                gla_diagonal(it)
                for k in range(len(LEVELS)):
                    level_keys(it, k)
                    if k == 0:
                        carried_states(it)
                    else:
                        copy_level(it, k - 1)
                    if k < NT:
                        att_weights(it, k)
                    if k + 1 < NT:
                        att_max(it, k + 1)
                    if k == 1:
                        low(unit(L, U_GT + 1, h))
                    if k == 4:
                        low(unit(L, U_GT + 2, h))
                copy_level(it, len(LEVELS) - 1)
                done(A_act, it, "sq")
                v.tensor_reduce(st_t[:, 0, :], SQ2[:], AX_X, ALU.add).then_inc(*A_dve.step("ss"))
                gla_output(it)
                normed(it, A_dve, A_pool, O2, st_t, lambda c: sl_row[:])
                done(G_dve, it, "o1")
                normed(it, G_dve, G_pool, O1, st_g, lambda c: gN[:, c, :])

            with dve.Fori(0, DEPTH) as L:
                dve.wait_ge(s_lay, L * 48 + 48)
                v.tensor_copy(lay_now[:], laytab[:, bass.ds(L * 2, 2)]).then_inc(*lay_dve.step("lay"))
                done(lay_dve, L, "lay")
                v.tensor_scalar(sl_row[:], sl_row[:], lay_now[:, 1:2], None, ALU.mult).then_inc(*lay_dve.step("slw"))
                low(unit(L, 0))
                dve.wait_ge(s_wr, L * 96 + 16)
                norm_stage(n1, L, X, True)
                with dve.Fori(0, N_PB // 2) as i:
                    for u in range(2):
                        low(unit(L, U_PB + u + 1, i))
                with dve.Fori(0, 5) as g:
                    it = L * 5 + g
                    low(unit(L, U_PA + 1, g))
                    low(unit(L, U_PA + 2, g))
                    dve.wait_ge(zn_st, it * 16 + 16)
                    for t in range(NT):
                        if t < NT - 1:
                            done(pa_pe, it, f"a{t}")
                        else:
                            dve.wait_ge(w_used, unit(L, U_PA + 1, g)[0] + 3)
                        v.tensor_copy(stN[:, t, :], ps[:, t, :]).then_inc(*pa_dve.step(f"ev{t}"))
                with dve.Fori(0, NH) as h:
                    mixers(L * NH + h, L, h)
                for c in range(KD):
                    done(ab_act, L, f"h{c}")
                    v.tensor_tensor(hT_lo[:, c, :], abT[:, c, :], hT_hi[:, c, :].bitcast(F32), ALU.subtract).then_inc(*ab_dve.step(f"l{c}"))
                with dve.Fori(0, 2) as i:
                    it = L * 2 + i
                    for u in range(2):
                        low(unit(L, U_BR + u + 1, i))
                        for b in range(2):
                            n = f"{u}_{b}"
                            if b == 0:
                                done(br_pe, it, f"blk{u}")
                            else:
                                dve.wait_ge(w_used, unit(L, U_BR + u, i)[0] + 3)
                            done(br_act, it, f"sg{n}")
                            if (u, b) != (0, 0):
                                done(br_dve, it, f"ml{(2 * u + b - 1) // 2}_{(b + 1) % 2}")
                            else:
                                dve.wait_ge(br_dve.sem, br_dve.before(it, "ml1_1"))
                            for k, name, dst in ((0, "ta", BT1), (1, "tb", BT2)):
                                for hf, (t0, tn) in enumerate(HALVES):
                                    v.tensor_tensor(dst[:, t0:t0 + tn], GT[:, b, k, t0:t0 + tn], ps[:, 4 * b + 2 * k + hf, 0:tn], ALU.mult)\
                                        .then_inc(*br_dve.step(f"{name}{hf}{n}"))
                            done(br_dve, it, f"tb1{n}")
                            v.tensor_tensor(BT1[:], BT1[:], BT2[:], ALU.add).then_inc(*br_dve.step(f"m{n}"))
                            done(br_act, it, f"mh{n}")
                            blk = i * 4 + (2 * u + b)
                            v.tensor_tensor(mT_lo[:, bass.ds(blk, 1), :].rearrange("p o t -> p (o t)"), BT1[:],
                                            mT_hi[:, bass.ds(blk, 1), :].rearrange("p o t -> p (o t)").bitcast(F32), ALU.subtract)\
                                .then_inc(*br_dve.step(f"ml{n}"))
                low(unit(L, U_WO + 1))
                low(unit(L, U_WO + 2))
                for t in range(NT):
                    done(wo_act, L, f"sq{t}")
                    v.tensor_copy(Y0w[:, t, :], ps[:, t, :]).then_inc(*wo_dve.step(f"y{t}"))
                low(unit(L, U_WO + 3))
                low(unit(L, U_UP))
                dve.wait_ge(s_wr, L * 96 + 64)
                done(wo_dve, L, f"y{NT - 1}")
                for n in range(3):
                    dve.wait_ge(s_x[n], L * 32 + 32)
                norm_stage(nr, L * 2, X, True, Y0w, lambda t: None)
                with dve.Fori(0, NFF // 2) as i:
                    it = L * (NFF // 2) + i
                    for u in range(2):
                        low(unit(L, U_UP + u + 1, i))
                        if u == 0:
                            dve.wait_ge(up_dve.sem, up_dve.before(it, "pr1"))
                        dve.wait_ge(up_act.sem, up_act.before(it, f"cv1_{u}"))
                        v.tensor_copy(conv_now[:, u, :], conv_all[:, bass.ds(i * 2 + u, 1), :].rearrange("p o c -> p (o c)"))\
                            .then_inc(*up_dve.step(f"cp{u}"))
                        done(up_dve, it, f"cp{u}")
                        for gv, C in enumerate((CG, CV)):
                            nm = "gv"[gv]
                            done(up_act, it, f"c{nm}1_{u}")
                            for hf, (t0, tn) in enumerate(HALVES):
                                bank = 4 * u + 2 * gv + hf
                                left, right = C[:, u, t0 + 1:t0 + tn], C[:, u, t0:t0 + tn - 1]
                                v.scalar_tensor_tensor(left, ps[:, bank, 0:tn - 1], conv_now[:, u, 4 * gv:4 * gv + 1], left,
                                                       ALU.mult, ALU.add).then_inc(*up_dve.step(f"{nm}{hf}l{u}"))
                                done(up_dve, it, f"{nm}{hf}l{u}")
                                v.scalar_tensor_tensor(right, ps[:, bank, 1:tn], conv_now[:, u, 4 * gv + 2:4 * gv + 3], right,
                                                       ALU.mult, ALU.add).then_inc(*up_dve.step(f"{nm}{hf}r{u}"))
                        done(up_act, it, f"ge{u}")
                        done(up_dve, it, f"v1r{u}")
                        v.tensor_tensor(prod[:, bass.ds(i * 2 + u, 1), :].rearrange("p o t -> p (o t)"), CG[:, u, :], CV[:, u, :], ALU.mult)\
                            .then_inc(*up_dve.step(f"pr{u}"))

                def prod_low(n):
                    done(dn_act, L, f"ph{n}")
                    j = n % 11
                    v.tensor_tensor(PH_lo[:, n % 2], prod[:, 2 * j:2 * j + 2, :], PH_hi[:, n % 2].bitcast(F32), ALU.subtract)\
                        .then_inc(*dn_dve.step(f"pl{n}"))

                prod_low(0)
                for n in range(22):
                    low(unit(L, U_DN + n + 1), 1024)
                    if n + 1 < 22:
                        prod_low(n + 1)
                    if n == 10:
                        for t in range(NT):
                            done(dn_act, L, f"sq{t}")
                            v.tensor_copy(Y0d[:, t, :], ps[:, t, :]).then_inc(*dn_dve.step(f"y{t}"))
                for b in range(3):
                    done(pt_act, L, f"h{b}")
                    v.tensor_tensor(view(PT_lo[:], b * 512, [[1, 512]]), ps[:, 6 + b % 2, :],
                                    view(PT_hi[:], b * 512, [[1, 512]]).bitcast(F32), ALU.subtract).then_inc(*pt_dve.step(f"l{b}"))
                low(unit(L, U_PE + 1), 1024)
                dve.wait_ge(s_wr, L * 96 + 80)
                dve.wait_ge(s_xm, L * 16 + 16)
                norm_stage(nr, L * 2 + 1, XM, False, Y0d, lambda t: None)
                for j in range(4):
                    low(unit(L, U_PG + j))
                for c in range(2):
                    for t in range(NT):
                        done(pg_act, L, f"s{c}_{t}")
                        v.tensor_tensor(E[:, c, t, :], SG[:, t % 2, :], E[:, c, t, :], ALU.mult).then_inc(*pg_dve.step(f"m{c}_{t}"))
                dve.wait_ge(s_wr, L * 96 + 96)
                for t in range(NT):
                    done(fin_pool, L, f"r{t}")
                    if t:
                        done(fin_dve, L, f"x{t - 1}")
                    for c, n in ((0, "a"), (1, "b")):
                        v.scalar_tensor_tensor(TMP[:, c * 512:(c + 1) * 512], E[:, c, t, :], rsy[:, t:t + 1],
                                               wrows[:, 1, c * 512:(c + 1) * 512], ALU.mult, ALU.mult).then_inc(*fin_dve.step(f"{n}{t}"))
                    done(fin_dve, L, f"b{t}")
                    v.tensor_tensor(XM[:, t, :], XM[:, t, :], TMP[:], ALU.add).then_inc(*fin_dve.step(f"x{t}"))

        @block.gpsimd
        def _(pool):
            g = nc.gpsimd
            pool.wait_ge(const_ok, 3)

            def done(c, it, name):
                pool.wait_ge(c.sem, c.at(it, name))

            def rstd(c, it, out, ms, ss, width, m, r, n=1, col=0):
                pool.sem_inc(waited, 1)
                g.tensor_scalar(ms, ss, 1.0 / width, EPS, ALU.mult, ALU.add).then_inc(*c.step(m))
                done(c, it, m)
                g.tensor_tensor(out, ms, half_neg[:, 0:n], ALU.pow).then_inc(*c.step(r))

            def norm_stage(c, it, residual=None):
                for s in range(NT + 2):
                    r, n = s, s - 1
                    if r < NT and residual:
                        done(c["act"], it, f"sqy{r}")
                        g.tensor_tensor(msy[:, r:r + 1], ssy[:, r:r + 1], ssy[:, NT + r:NT + r + 1], ALU.add).then_inc(*c["pool"].step(f"sy{r}"))
                        done(c["pool"], it, f"sy{r}")
                        rstd(c["pool"], it, rsy[:, r:r + 1], msy[:, r:r + 1], msy[:, r:r + 1], D, f"my{r}", f"ry{r}")
                    if 0 <= n < NT:
                        done(c["act"], it, f"sqx{n}")
                        rstd(c["pool"], it, rsx[:, n:n + 1], msx[:, n:n + 1], ssx[:, n:n + 1], D, f"mx{n}", f"rs{n}")

            with pool.Fori(0, DEPTH) as L:
                norm_stage(n1, L)
                with pool.Fori(0, NH) as h:
                    it = L * NH + h
                    for c_dve, c_pool, st in ((A_dve, A_pool, st_t), (G_dve, G_pool, st_g)):
                        done(c_dve, it, "ss")
                        rstd(c_pool, it, st[:, 2, :], st[:, 1, :], st[:, 0, :], P, "ms", "rs", NT)
                norm_stage(nr, L * 2, True)
                norm_stage(nr, L * 2 + 1, True)
                for t in range(NT):
                    done(pg_act, L, f"q1_{t}")
                    g.tensor_tensor(msy[:, t:t + 1], ssy[:, t:t + 1], ssy[:, NT + t:NT + t + 1], ALU.add).then_inc(*fin_pool.step(f"s{t}"))
                    done(fin_pool, L, f"s{t}")
                    rstd(fin_pool, L, rsy[:, t:t + 1], msy[:, t:t + 1], msy[:, t:t + 1], D, f"m{t}", f"r{t}")

        @block.scalar
        def _(act):
            a = nc.scalar.activation

            def done(c, it, name):
                act.wait_ge(c.sem, c.at(it, name))

            def high(u, width=ISLOTS):
                n, half, s = u
                act.wait_ge(w_loaded[s], half * 32 + 32)
                act.wait_ge(w_used, n + 1)
                a(whi[:, s, 0:width], raw[:, s, 0:width], ACT.Copy).then_inc(w_hi, 1)

            def used(u):
                act.wait_ge(w_used, u[0] + (1 + CREDIT))

            def norm_stage(c, it, x, junk, hT_free, residual=None, extra=None):
                for s in range(NT + 2):
                    r, n, h = s, s - 1, s - 2
                    if r < NT and residual is not None:
                        residual(r)
                        if r:
                            done(c["act"], it, f"sqy{r - 1}")
                        a(JK[:], ps[:, r, :], ACT.Square, accum_out=ssy[:, NT + r:NT + r + 1]).then_inc(*c["act"].step(f"sqy{r}"))
                    if 0 <= n < NT:
                        if residual is not None:
                            done(c["dve"], it, f"rx{n}")
                        if n == 0:
                            hT_free()
                        else:
                            done(c["act"], it, f"sqx{n - 1}")
                        a(junk[:], x[:, n, :], ACT.Square, accum_out=ssx[:, n:n + 1]).then_inc(*c["act"].step(f"sqx{n}"))
                    if h >= 0:
                        for k in range(2):
                            done(c["pe"], it, f"tr{h}_{k}")
                            a(hT_hi[:, 4 * k:4 * k + 4, h * P:(h + 1) * P], ps[:, 6 + k, :].rearrange("p (k t) -> p k t", k=4), ACT.Copy)\
                                .then_inc(*c["act"].step(f"hi{h}_{k}"))
                    if extra:
                        extra(s)

            def row(dst, w, L, s):
                act.dma_start(dst, w[bass.ds(L, 1), :].partition_broadcast(P)).then_inc(s, 16)

            def load_x(dst_of, L):
                for n in range(3):
                    act.dma_start(X[:, 2 * n:2 * n + 2, :], out[n * 2 * P:(n + 1) * 2 * P, :].rearrange("(t p) d -> p t d", p=P))\
                        .then_inc(s_x[n], 16)

            def head_store(it, h, c_act, c_pe, dst, banks, row0, s):
                for k, n in ((0, 4), (1, 2)):
                    done(c_pe, it, f"tro{k}")
                    a(dst[:, 4 * k * P:(4 * k + n) * P], ps[:, banks[k], 0:n * P], ACT.Copy).then_inc(*c_act.step(f"ab{k}"))
                done(c_act, it, "ab1")
                act.dma_start(abD[bass.ds(h * P + row0, P), :], dst).then_inc(s, 16)

            def gla_gates(it):
                act.wait_ge(s_fz, it * 16 + 16)
                a(FZ[:, 0, :], FZ[:, 0, :], ACT.Silu).then_inc(*G_act.step("silu_q"))
                act.wait_ge(s_g, it * 16 + 16)
                a(gN[:], gN[:], ACT.Silu).then_inc(*G_act.step("silu_g"))
                a(LB0[:], FZ[:, 1:3, :], ACT.Sigmoid).then_inc(*G_act.step("sig"))
                done(G_act, it, "sig")
                a(FZ[:, 1:3, :], FZ[:, 1:3, :], ACT.Sigmoid, scale=-1.0).then_inc(*G_act.step("sig_neg"))
                done(G_dve, it, "fa")
                a(LB1[:], LB1[:], ACT.Ln).then_inc(*G_act.step("ln1"))
                done(G_dve, it, "fb")
                a(LB2[:], LB2[:], ACT.Ln).then_inc(*G_act.step("ln2"))

            def gla_exponentials(it):
                done(G_dve, it, "scan1")
                a(LB1[:], B[:], ACT.Exp).then_inc(*G_act.step("exp_b"))
                done(G_dve, it, "dl")
                a(LB2[:], LB2[:], ACT.Exp, scale=-1.0).then_inc(*G_act.step("exp_l"))

            def level_exponentials(it, l):
                h_ = LEVELS[l]
                nb_ = T // (2 * h_)
                keys, queries = [[T + h_, 2], [2 * h_, nb_], [1, h_]], [[T - h_, 2], [2 * h_, nb_], [1, h_]]
                buf = LB[l % 3]
                done(G_dve, it, f"D{l}")
                a(view(buf[:], 0, keys), view(buf[:], 0, keys), ACT.Exp, scale=-1.0).then_inc(*G_act.step(f"xk{l}"))
                a(view(buf[:], h_, queries), view(buf[:], h_, queries), ACT.Exp).then_inc(*G_act.step(f"xq{l}"))

            def att_exponentials(it, n):
                p, kn = n % 2, SEQ_OF[n][1]
                done(A_dve, it, f"nb{n}")
                if n >= 2:
                    done(A_pe, it, f"tra{n - 2}")
                for m in range(2):
                    a(PR[:, p, m, 0:kn], ps[:, AB[m], 0:kn], ACT.Exp, bias=nb[:, p, m:m + 1], scale=DA_DH ** -0.5,
                      accum_out=sm[:, p, m:m + 1]).then_inc(*A_act.step(f"e{n}_{m}"))

            def gate_store(it, L, h, b):
                if b % 2 == 0:
                    done(gt_pe, it, f"b{b}")
                else:
                    used(unit(L, U_GT + b // 2, h))
                act.wait_ge(zg_st, it * 64 + (16 * b + 16))
                for hf, (t0, tn) in enumerate(HALVES):
                    a(gst[:, t0:t0 + tn], ps[:, 6 + hf, 0:tn], ACT.Copy).then_inc(*gt_act.step(f"ev{b}_{hf}"))
                done(gt_act, it, f"ev{b}_1")
                act.dma_start(zT[bass.ds(h * 4 * P + (12 + b) * P, P), :], gst).then_inc(zg_st, 16)

            def mixers(it, L, h):
                gla_gates(it)
                for b in range(3):
                    done(A_pe, it, f"trq{b}")
                    a(view(qkT[:], b * 512, [[1, 512]]), ps[:, AB[b], :], ACT.Copy).then_inc(*A_act.step(f"qk{b}"))
                gla_exponentials(it)
                level_exponentials(it, 0)
                att_exponentials(it, 0)
                for b in range(3):
                    done(G_pe, it, f"trk{b}")
                    a(view(FZ[:], b * 512, [[1, 512]]), ps[:, GB[b], :], ACT.Copy).then_inc(*G_act.step(f"kht{b}"))
                high(unit(L, U_GT + 1, h))
                gate_store(it, L, h, 0)
                for k in range(len(LEVELS)):
                    if k + 1 < len(LEVELS):
                        level_exponentials(it, k + 1)
                    if k + 1 < NT:
                        att_exponentials(it, k + 1)
                    if k:
                        done(A_pe, it, f"av{k - 1}")
                        a(O2[:, k - 1, :], ps[:, AB[2], 0:P], ACT.Copy).then_inc(*A_act.step(f"oc{k - 1}"))
                    if k < NT:
                        kn = SEQ_OF[k][1]
                        done(A_pe, it, f"tra{k}")
                        a(At[:, k % 2, 0:kn], ps[:, AB[2], 0:kn], ACT.Copy).then_inc(*A_act.step(f"at{k}"))
                    if k == 2:
                        gate_store(it, L, h, 1)
                        high(unit(L, U_GT + 2, h))
                done(A_act, it, f"oc{NT - 1}")
                a(SQ2[:], O2[:], ACT.Square).then_inc(*A_act.step("sq"))
                gate_store(it, L, h, 2)
                for k, n in ((0, 4), (1, 2)):
                    done(G_pe, it, f"o{k}")
                    a(SQ1[:, 4 * k:4 * k + n, :], ps[:, GB[k], 0:n * P].rearrange("p (c v) -> p c v", v=P), ACT.Square)\
                        .then_inc(*G_act.step(f"sq{k}"))
                head_store(it, h, A_act, A_pe, SQ2.rearrange("p c v -> p (c v)"), (AB[0], AB[1]), NH * P, ab_st[1])
                gate_store(it, L, h, 3)
                head_store(it, h, G_act, G_pe, FZ[:, 1, :], (GB[2], GB[0]), 0, ab_st[0])

            act.wait_ge(const_ok, mark["exponents"])
            a(lams[:, 4:8], lams[:, 0:4], ACT.Exp).then_inc(lam_exp, 1)
            a(lbs[:, 24:40], lbs[:, 8:24], ACT.Exp).then_inc(lam_exp, 1)
            act.wait_ge(const_ok, mark["all"])

            with act.Fori(0, DEPTH) as L:
                act.wait_ge(s_out, L * 192 + 16)
                act.wait_ge(fin_dve.sem, fin_dve.before(L, f"x{NT - 1}"))
                load_x(X, L)
                row(wrows[:, 0, :], n_mix_pre, L, s_wr)
                row(gn_row[:], gnorm, L, s_lay)
                row(sl_row[:], subln, L, s_lay)
                act.dma_start(conv_all[:], conv_p[bass.ds(L, 1), :, :].rearrange("o p (u c) -> p (o u) c", c=8)).then_inc(s_lay, 16)
                high(unit(L, 0))

                act.wait_ge(s_x[0], L * 32 + 16)
                act.wait_ge(s_x[1], L * 32 + 16)
                act.wait_ge(s_x[2], L * 32 + 16)
                norm_stage(n1, L, X, JX, lambda: None)
                done(n1["dve"], L, f"hn{NT - 1}")
                act.dma_start(rope[:], rope_in.rearrange("p (a t) -> p a t", a=2)).then_inc(s_wr, 16)
                with act.Fori(0, N_PB // 2) as i:
                    it = L * (N_PB // 2) + i
                    for u in range(2):
                        w = unit(L, U_PB + u, i)
                        high(unit(L, U_PB + u + 1, i))
                        act.wait_ge(zt_st[u], it * 16 + 16)
                        for b in range(2):
                            if b == 0:
                                done(pb_pe, it, f"blk{u}")
                            else:
                                used(w)
                            for hf, (t0, tn) in enumerate(HALVES):
                                a(stT[:, u, b, t0:t0 + tn], ps[:, 4 * u + 2 * b + hf, 0:tn], ACT.Copy)\
                                    .then_inc(*pb_act.step(f"ev{u}_{b}_{hf}"))
                        done(pb_act, it, f"ev{u}_1_1")
                        act.dma_start(zT[bass.ds(i * 4 * P + u * 2 * P, 2 * P), :].rearrange("(b p) t -> p b t", p=P), stT[:, u])\
                            .then_inc(zt_st[u], 16)
                with act.Fori(0, 5) as g:
                    it = L * 5 + g
                    high(unit(L, U_PA + 1, g))
                    high(unit(L, U_PA + 2, g))
                    done(pa_dve, it, f"ev{NT - 1}")
                    act.dma_start(zN[:, bass.ds(g * 512, 512)].rearrange("(t p) c -> p t c", p=P), stN[:]).then_inc(zn_st, 16)
                for u in range(2):
                    act.wait_ge(zt_st[u], L * (16 * N_PB // 2) + 16 * (N_PB // 2 + 1))
                act.wait_ge(zn_st, L * (16 * 5) + 16 * 6)
                heads = zT.rearrange("(a h p) t -> h p a t", a=7, p=P)
                cols = zN.rearrange("(t p) (g h c) -> g h p t c", p=P, g=5, h=NH)
                with act.Fori(0, NH) as h:
                    it = L * NH + h
                    act.wait_ge(G_pe.sem, G_pe.before(it, "tro1"))
                    act.wait_ge(A_act.sem, A_act.before(it, "ab1"))
                    act.wait_ge(ab_st[0], it * 16 + 16)
                    act.dma_start(FZ[:], heads[bass.ds(h, 1), :, 0:3, :].rearrange("o p a t -> p (o a) t")).then_inc(s_fz, 16)
                    for n, (dst, s) in enumerate(((vN[:], s_v), (gN[:], s_g), (QK[:, 0], s_qk), (QK[:, 1], s_qk), (vD[:], s_vd))):
                        act.dma_start(dst, cols[n, bass.ds(h, 1)].rearrange("o p t c -> p (o t) c")).then_inc(s, 16)
                    mixers(it, L, h)
                row(wrows[:, 0, :], n_ffn_pre, L, s_wr)
                row(wrows[:, 1, :], n_mix_post, L, s_wr)
                act.wait_ge(ab_st[0], L * (16 * NH) + 16 * (NH + 1))
                act.wait_ge(ab_st[1], L * (16 * NH) + 16 * (NH + 1))
                act.dma_start(abT[:], abD.rearrange("(b p) t -> p b t", p=P)).then_inc(s_ab, 16)
                used(unit(L, U_BR - 1))
                act.wait_ge(s_ab, L * 16 + 16)
                for c in range(KD):
                    a(hT_hi[:, c, :], abT[:, c, :], ACT.Copy).then_inc(*ab_act.step(f"h{c}"))
                act.wait_ge(zg_st, L * (64 * NH) + (64 * NH + 16))
                gates = zT[12 * P:28 * P, :].rearrange("(g b p) t -> b p g t", g=2, p=P)
                with act.Fori(0, 2) as i:
                    it = L * 2 + i
                    for u in range(2):
                        for b in range(2):
                            act.wait_ge(br_dve.sem, br_dve.at(it, f"tb10_{b}") if u else br_dve.before(it, f"tb11_{b}"))
                            act.dma_start(GT[:, b], gates[bass.ds(i * 4 + (2 * u + b), 1)].rearrange("o p g t -> p (o g) t")).then_inc(s_gt[b], 16)
                        high(unit(L, U_BR + u + 1, i))
                        for b in range(2):
                            act.wait_ge(s_gt[b], it * 32 + (16 * u + 16))
                            a(GT[:, b], GT[:, b], ACT.Sigmoid).then_inc(*br_act.step(f"sg{u}_{b}"))
                            done(br_dve, it, f"m{u}_{b}")
                            a(mT_hi[:, bass.ds(i * 4 + (2 * u + b), 1), :].rearrange("p o t -> p (o t)"), BT1[:], ACT.Copy)\
                                .then_inc(*br_act.step(f"mh{u}_{b}"))
                done(ab_dve, L, f"l{KD - 1}")
                load_x(X, L)
                high(unit(L, U_WO + 1))
                high(unit(L, U_WO + 2))
                for t in range(NT):
                    if t < NT - 1:
                        done(wo_pe, L, f"a0_{t}")
                    else:
                        used(unit(L, U_WO + 1))
                    if t == 0:
                        done(br_dve, L * 2 + 1, "ml1_1")
                    else:
                        done(wo_act, L, f"sq{t - 1}")
                    a(JK[:], ps[:, t, :], ACT.Square, accum_out=ssy[:, t:t + 1]).then_inc(*wo_act.step(f"sq{t}"))
                high(unit(L, U_WO + 3))
                high(unit(L, U_UP))

                def wo_bank(t):
                    if t == 0:
                        done(wo_act, L, f"sq{NT - 1}")
                    if t < NT - 1:
                        done(wo_pe, L, f"a1_{t}")
                    else:
                        used(unit(L, U_WO + 3))

                def store_x(x):
                    def f(s):
                        if 1 <= s <= NT:
                            act.dma_start(out[(s - 1) * P:s * P, :], x[:, s - 1, :]).then_inc(s_out, 16)
                    return f

                norm_stage(nr, L * 2, X, JY, lambda: used(unit(L, U_WO + 3)), wo_bank, store_x(X))
                done(nr["dve"], L * 2, f"hn{NT - 1}")
                row(wrows[:, 1, :], n_ffn_post, L, s_wr)
                act.wait_ge(s_out, L * 192 + (16 + 96))
                with act.Fori(0, NFF // 2) as i:
                    it = L * (NFF // 2) + i
                    for u in range(2):
                        high(unit(L, U_UP + u + 1, i))
                        act.wait_ge(up_dve.sem, up_dve.before(it, f"pr{u}"))
                        done(up_dve, it, f"cp{u}")
                        for gv, C in enumerate((CG, CV)):
                            if gv == 0:
                                done(up_pe, it, f"blk{u}")
                            else:
                                used(unit(L, U_UP + u, i))
                            for hf, (t0, tn) in enumerate(HALVES):
                                a(C[:, u, t0:t0 + tn], ps[:, 4 * u + 2 * gv + hf, 0:tn], ACT.Identity,
                                  scale=conv_now[:, u, 4 * gv + 1:4 * gv + 2], bias=conv_now[:, u, 4 * gv + 3:4 * gv + 4])\
                                    .then_inc(*up_act.step(f"c{'gv'[gv]}{hf}_{u}"))
                        done(up_dve, it, f"g1r{u}")
                        a(CG[:, u, :], CG[:, u, :], ACT.Gelu_apprx_tanh).then_inc(*up_act.step(f"ge{u}"))

                def prod_high(n):
                    act.wait_ge(w_used, unit(L, U_DN + n)[0] + 1)
                    j = n % 11
                    a(PH_hi[:, n % 2], prod[:, 2 * j:2 * j + 2, :], ACT.Copy).then_inc(*dn_act.step(f"ph{n}"))

                done(up_dve, L * (NFF // 2) + (NFF // 2 - 1), "pr1")
                act.wait_ge(w_used, unit(L, U_DN)[0] + 2)
                prod_high(0)
                for n in range(22):
                    high(unit(L, U_DN + n + 1), 1024)
                    if n + 1 < 22:
                        prod_high(n + 1)
                    if n == 10:
                        for t in range(NT):
                            if t < NT - 1:
                                done(dn_pe, L, f"a0_{t}")
                            else:
                                used(unit(L, U_DN + 10))
                            if t:
                                done(dn_act, L, f"sq{t - 1}")
                            a(CG[:, 0, 0:512], ps[:, t, :], ACT.Square, accum_out=ssy[:, t:t + 1]).then_inc(*dn_act.step(f"sq{t}"))
                done(dn_dve, L, "pl21")
                act.dma_start(XM[:], out.rearrange("(t p) d -> p t d", p=P)).then_inc(s_xm, 16)
                act.dma_start(Pn[:], p_in[bass.ds(L, 1), :, :].rearrange("o (t p) c -> p (o t) c", p=P)).then_inc(s_p, 16)
                for b in range(3):
                    done(pt_pe, L, f"tr{b}")
                    a(view(PT_hi[:], b * 512, [[1, 512]]), ps[:, 6 + b % 2, :], ACT.Copy).then_inc(*pt_act.step(f"h{b}"))
                high(unit(L, U_PE + 1), 1024)

                def dn_bank(t):
                    if t < NT - 1:
                        done(dn_pe, L, f"a1_{t}")

                def e_out(c, t):
                    if t < NT - 1:
                        done(pe_pe, L, f"e{c}_{t}")
                    else:
                        used(unit(L, U_PE + c))
                    a(E[:, c, t, :], ps[:, t, :], ACT.Copy).then_inc(*pe_act.step(f"e{c}_{t}"))

                norm_stage(nr, L * 2 + 1, XM, JX, lambda: None, dn_bank, lambda s: e_out(0, s - 1) if 1 <= s <= NT else None)
                row(wrows[:, 1, :], n_ple, L, s_wr)
                high(unit(L, U_PG))
                for t in range(NT):
                    e_out(1, t)
                for j in (1, 2, 3):
                    high(unit(L, U_PG + j))
                for c in range(2):
                    for t in range(NT + 1):
                        if t < NT:
                            if t < NT - 1:
                                done(pg_pe, L, f"g{c}_{t}")
                            else:
                                used(unit(L, U_PG + 1 + 2 * c))
                            n = c * NT + t
                            if n >= 2:
                                done(pg_dve, L, f"m{(n - 2) // NT}_{(n - 2) % NT}")
                            a(SG[:, t % 2, :], ps[:, t, :], ACT.Sigmoid).then_inc(*pg_act.step(f"s{c}_{t}"))
                        if t:
                            done(pg_dve, L, f"m{c}_{t - 1}")
                            if t > 1:
                                done(pg_act, L, f"q{c}_{t - 2}")
                            elif c:
                                done(pg_act, L, f"q0_{NT - 1}")
                            else:
                                done(nr["act"], L * 2 + 1, f"sqy{NT - 1}")
                            a(JK[:], E[:, c, t - 1, :], ACT.Square, accum_out=ssy[:, c * NT + t - 1:c * NT + t]).then_inc(*pg_act.step(f"q{c}_{t - 1}"))
                for t in range(NT):
                    done(fin_dve, L, f"x{t}")
                    act.dma_start(out[t * P:(t + 1) * P, :], XM[:, t, :]).then_inc(s_out, 16)
            act.wait_ge(s_out, DEPTH * 192 + 16)



def kernel(**inputs):
    import numpy as np
    import concourse.bacc as bacc
    from concourse.bass_utils import run_bass_kernel_spmd

    i = {k: np.asarray(v) for k, v in inputs.items()}
    lay = {
        "x_in": np.concatenate([i["x_prompt"][0], i["x_sample"][0]], axis=0),
        "p_in": np.concatenate([i["p_prompt"][:, 0], i["p_sample"][:, 0]], axis=1),
        "w_in": i["w_in"],
        "lb_logits": i["hgrn_lb_logits"].reshape(DEPTH, 2, NH, P).transpose(3, 2, 1, 0).reshape(P, -1),
        "gnorm": i["hgrn_gnorm"],
        "lam_in": i["diff_lambda"].reshape(1, -1),
        "subln": i["diff_subln"],
        "w_a": i["w_branch_a"], "w_b": i["w_branch_b"], "w_out": i["w_out"],
        "n_mix_pre": i["norm_mix_pre"], "n_mix_post": i["norm_mix_post"],
        "w_up": i["w_up"],
        "conv_p": np.concatenate([i["conv_w"], i["conv_b"][:, None]], axis=1).reshape(DEPTH, 4, 2, NFF, P)
        .transpose(0, 4, 3, 2, 1).reshape(DEPTH, P, NFF * 8),
        "w_down": i["w_down"],
        "n_ffn_pre": i["norm_ffn_pre"], "n_ffn_post": i["norm_ffn_post"],
        "w_ple": i["w_ple"], "w_ple_gate": i["w_ple_gate"], "n_ple": i["norm_ple"],
    }
    lay["ident_in"] = np.eye(P, dtype=np.float32)
    masks = np.zeros((P, 2, len(LEVELS), 64), np.float32)
    for l, h in enumerate(LEVELS):
        for j in range(64):
            block = j // h * 2 * h
            masks[block:block + h, 0, l, j] = 1
            masks[block + h:block + 2 * h, 1, l, j] = 1
    lay["masks_in"] = masks.reshape(P, -1)
    inv = (1.0 / (10000.0 ** (np.arange(0, DA_DH, 2) / DA_DH))).astype(np.float32)
    pos = np.concatenate([np.arange(TP), np.arange(TS)]).astype(np.float32)
    ang = (pos[:, None] * inv[None, :]).astype(np.float32)
    cos, sin = np.cos(ang), np.sin(ang)
    rope = np.stack([np.concatenate([cos, cos] * 2, 1), np.concatenate([-sin, sin] * 2, 1)])
    lay["rope_in"] = rope.reshape(2, NT, P, P).transpose(2, 0, 1, 3).reshape(P, -1).astype(np.float32)

    nc = bacc.Bacc("TRN2", target_bir_lowering=False, num_devices=1)
    arrays, args = {}, {}
    for name, arr in lay.items():
        arr = np.ascontiguousarray(arr)
        arrays[name + "_dram"] = arr
        args[name] = nc.dram_tensor(name + "_dram", arr.shape, mybir.dt.from_np(arr.dtype), kind="ExternalInput").ap()
    args["out"] = nc.dram_tensor("out_dram", (T, D), F32, kind="ExternalOutput").ap()
    build(nc, **args)
    y = run_bass_kernel_spmd(nc, [arrays], core_ids=[0]).results[0]["out_dram"]
    return y[None, :TP], y[None, TP:]
```

```python
import math
from contextlib import ExitStack

import concourse.bass as bass
from concourse import mybir

ALU = mybir.AluOpType
ACT = mybir.ActivationFunctionType
F32 = mybir.dt.float32
F32R = mybir.dt.float32r
U8 = mybir.dt.uint8
AX_X = mybir.AxisListType.X

P = 128
DEPTH = 2
TP, TS = 256, 512
T = TP + TS
NT = T // P
D = 1024
KD = D // P
HW = 512
NH = 4
DA_DH = 64
PLE = 256
FF = 2816
NFF = FF // P
EPS = 1e-6
LB_FLOOR = 1e-30
LN_SPLIT = 2.0 ** -60
HALVES = ((0, TP), (TP, TS))
LEVELS = (64, 32, 16, 8, 4, 2, 1)
STATES = ((0, 0), (0, 2), (0, 3), (0, 4), (1, 1), (1, 5), (1, 4), (1, 3))
CARRIES = ((0, 0, 1), (0, 1, 3), (0, 2, 4), (0, 3, 5), (1, 4, 0), (1, 5, 4), (1, 6, 3), (1, 7, 2))
SEQ_OF = [(0, TP)] * (TP // P) + [(TP, TS)] * (TS // P)
ISLOTS = 2048

GROUPS = ((0, 1), (2, 4), (5, 6), (3, 7))
HEAD_U = len(GROUPS)
GATE_U = 0
SIDE_U = HEAD_U + GATE_U
N_IN = HEAD_U * NH + 2 * NH
FIRST = (3, 0, 1, 2)
ZROWS = 6
SLOTS = (2, 2, 2, 1, 0, 1, 1, 1, 1, 1, 0, 0, 1, 1, 2)
SLOTS_LAST = (2, 2, 2, 2, 2, 2, 2, 2, 2, 2, 2, 2, 2, 2, 4)
U_BR = 24
U_WO = 28
U_UP = 32
U_DN = 54
U_PE = 76
U_PG = 78
N_UNITS = 82
CREDIT = 2


def lambda_init(l):
    return 0.8 - 0.6 * math.exp(-0.3 * l)


class Steps:

    def __init__(self, sem, names, credit=0):
        self.sem, self.names, self.n, self.credit = sem, list(names), len(names), credit
        self.index = {s: i for i, s in enumerate(self.names)}
        assert len(self.index) == self.n
        self.next = 0

    def step(self, name):
        assert self.names[self.next] == name, (self.names[self.next], name)
        self.next = (self.next + 1) % self.n
        return self.sem, 1

    def at(self, it, name):
        return it * self.n + (self.index[name] + 1 + self.credit)

    def before(self, it, name):
        return it * self.n + (self.index[name] + 1 + self.credit - self.n)

    def last(self, it):
        return self.at(it, self.names[-1])


def view(ap, offset, dims):
    return bass.AP(tensor=ap.tensor, offset=ap.offset + offset, ap=[list(ap.ap[0])] + [list(d) for d in dims])


def norm_names(engine, residual):
    out = []
    for s in range(NT + 2):
        r, n, h = s, s - 1, s - 2
        if r < NT and residual:
            out += {"act": [f"sqy{r}"], "dve": [f"ra{r}", f"rb{r}", f"rx{r}"],
                    "pool": [f"sy{r}", f"my{r}", f"ry{r}"], "pe": []}[engine]
        if 0 <= n < NT:
            out += {"act": [f"sqx{n}"], "dve": [f"hn{n}"], "pool": [f"mx{n}", f"rs{n}"],
                    "pe": [f"tr{n}_0", f"tr{n}_1"]}[engine]
        if h >= 0:
            out += {"act": [f"hi{h}_0", f"hi{h}_1"], "dve": [f"lo{h}_0", f"lo{h}_1"], "pool": [], "pe": []}[engine]
    return out


def slot_work(slots, s):
    start, end = sum(slots[:s]), sum(slots[:s + 1])
    before = sum(slots[:s - 1]) if s else 0
    out = []
    for half in range(sum(slots) // 2):
        done_at = 2 * half + 2
        if start < done_at < end or before < done_at == start:
            out.append(half)
    return range(start, end), out, [q // 4 for q in range(start, end) if q % 4 == 1]


def gla_names():
    act = ["silu_q", "sig", "sig_neg", "ln1", "ln2", "exp_b", "xk0", "xq0", "exp_l", "silu_g", "kht0", "kht1", "kht2"]
    dve = ["lb", "qs", "k0", "k1", "f0", "f1", "fa", "fb", "g", "scan0", "scan1", "D0"]
    dve += ["dec", "qh", "dl", "kh", "D1", "gw", "at0", "at1"]
    pe = ["trk0", "trk1", "trk2", "diag", "ds"]
    n = len(LEVELS)
    for l in range(n):
        act += [f"xk{l}", f"xq{l}"] if l else []
        dve += [f"mk{l}", f"mq{l}"] + ([f"D{l + 2}"] if l + 2 < n else []) + (["s0", "s1", "s2", "s3", "s4", "s5"] if l == 0 else [])
        dve += [f"cp{l - 1}_0", f"cp{l - 1}_1"] if l else []
        pe += [f"lv{l}_0", f"lv{l}_1"]
    dve += [f"cp{n - 1}_0", f"cp{n - 1}_1", "o0", "o1", "ss"] + [f"on{c}" for c in range(NT)] + ["ab0", "ab1"]
    act += ["sq0", "sq1"]
    pe += ["o0", "o1", "tro0", "tro1"]
    return act, dve, pe


def att_names():
    act, dve, pe = [], ["cqk", "sqk", "radd"], []
    act += ["e0_0", "e0_1"]
    dve += ["mx0", "nb0"]
    pe += ["sc0"]
    for k in range(NT + 1):
        if k < NT:
            dve += [f"rc{k}", f"lr{k}", f"a{k}", f"al{k}"]
        if k + 1 < NT:
            pe += [f"sc{k + 1}"]
            dve += [f"mx{k + 1}", f"nb{k + 1}"]
        pe += ([f"av{k - 1}"] if k else []) + ([f"tra{k}"] if k < NT else [])
        act += ([f"e{k + 1}_0", f"e{k + 1}_1"] if k + 1 < NT else []) + ([f"oc{k - 1}"] if k else []) + ([f"at{k}"] if k < NT else [])
    pe += ["tro0", "tro1"]
    act += ["sq", "ab0", "ab1"]
    dve += ["ss"] + [f"on{c}" for c in range(NT)]
    return act, dve, pe


def build(nc, x_in, p_in, w_in, lb_logits, gnorm, lam_in, subln, w_a, w_b, w_out, n_mix_pre, n_mix_post,
          w_up, conv_p, w_down, n_ffn_pre, n_ffn_post, w_ple, w_ple_gate, n_ple, ident_in, masks_in,
          rope_in, out):
    with ExitStack() as ctx:
        place = [(nc.sbuf_base + 31) // 32 * 32]

        def put(name, shape, dt, offset=None):
            size = mybir.dt.size(dt)
            for s in shape[1:]:
                size *= s
            if offset is None:
                offset = place[0]
                place[0] += (size + 31) // 32 * 32
            return nc.alloc_sbuf_tensor_at(name, shape, dt, offset=offset), offset, offset + (size + 31) // 32 * 32

        def keep(name, shape, dt=F32):
            return put(name, shape, dt)[0]

        ident = keep("ident", [P, P])
        masks = keep("masks", [P, 2 * len(LEVELS), 64], U8)
        rmask = keep("rmask", [P, T], U8)
        lbl = keep("lbl", [P, NH * 2 * DEPTH])
        lbtab = keep("lbtab", [P, DEPTH * NH * 4])
        lb_now = keep("lb_now", [P, 4])
        lbs = keep("lbs", [P, 64])
        laytab = keep("laytab", [P, DEPTH * 2])
        lay_now = keep("lay_now", [P, 2])
        lams = keep("lams", [P, 16])
        conv_all = keep("conv_all", [P, NFF, 8])
        conv_now = keep("conv_now", [P, 2, 8])
        gn_col = keep("gn_col", [P, 1])
        sl_row = keep("sl_row", [P, P])
        ssx = keep("ssx", [P, NT])
        rsx = keep("rsx", [P, NT])
        ssy = keep("ssy", [P, 2 * NT])
        rsy = keep("rsy", [P, NT])
        msx = keep("msx", [P, NT])
        msy = keep("msy", [P, NT])
        half_neg = keep("half_neg", [P, NT])
        decay = keep("decay", [P, 2, NT])
        st_g = keep("st_g", [P, 4, NT])
        st_t = keep("st_t", [P, 4, NT])
        mx = keep("mx", [P, 2, 2])
        nb = keep("nb", [P, 2, 2])
        sm = keep("sm", [P, 2, 2])
        rc = keep("rc", [P, 2, 2])
        lr = keep("lr", [P, 2])
        wrows, wr_off, _ = put("wrows", [P, 2, D], F32)
        rope = put("rope", [P, 2, T], F32, wr_off)[0]
        hn = keep("hn", [P, D])
        raw = keep("raw", [P, 2, ISLOTS])
        whi = keep("whi", [P, 2, ISLOTS], F32R)
        wlo = keep("wlo", [P, 2, ISLOTS], F32R)
        X, x_off, _ = put("X", [P, NT, D], F32)
        hT_hi, h_off, _ = put("hT_hi", [P, KD, T], F32R)
        hT_lo, _, h_end = put("hT_lo", [P, KD, T], F32R)
        m_off = place[0]
        prod, _, m_end = put("prod", [P, NFF, T], F32)
        assert place[0] <= nc.sbuf_usable_end, (place[0], nc.sbuf_usable_end)

        def stack(start, end, items):
            got, at = [], start
            for name, shape, dt in items:
                t, _, at = put(name, shape, dt, at)
                got.append(t)
            assert at <= end, (at, end)
            return got

        abT = put("abT", [P, 2 * NH, T], F32, x_off)[0]
        Qb, Kb, B, LB0, LB1, QH, AT, vN, gT, S, FZ, vD = stack(m_off, m_end, [
            ("Qb", [P, T], F32), ("Kb", [P, 2, T], F32), ("B", [P, 2, T], F32), ("LB0", [P, 2, T], F32),
            ("LB1", [P, 2, T], F32), ("QH", [P, 2, T], F32), ("AT", [P, NT, P], F32), ("vN", [P, NT, P], F32),
            ("gT", [P, T], F32), ("S", [P, 8, P], F32), ("FZ", [P, 3, T], F32),
            ("vD", [P, NT, P], F32)])
        LB2 = put("LB2", [P, 2, T], F32, m_end - 2 * T * 4)[0]
        khT = FZ[:, 0:2, :].rearrange("p a (c k) -> p (a c) k", k=P)
        O1, SQ1 = (Kb[:, k, :].rearrange("p (c v) -> p c v", v=P) for k in range(2))
        ab1 = QH[:, 0, :]
        QK, QKs, PR, At = stack(x_off, h_off, [
            ("QK", [P, 2, T], F32), ("QKs", [P, 2, T], F32), ("PR", [P, 2, 2, TS], F32), ("At", [P, 2, TS], F32)])
        O2, SQ2 = (QKs[:, k, :].rearrange("p (c v) -> p c v", v=P) for k in range(2))
        ab2 = PR.rearrange("p a m t -> p (a m t)")[:, 0:T]
        gst = hn
        mT_hi, mT_lo, GT, BT1, BT2 = stack(m_off, m_end, [
            ("mT_hi", [P, KD, T], F32R), ("mT_lo", [P, KD, T], F32R), ("GT", [P, 2, 2, T], F32),
            ("BT1", [P, T], F32), ("BT2", [P, T], F32)])
        Y0w = put("Y0w", [P, NT, 512], F32, m_off + 2 * KD * T * 4)[0]
        TMP = put("TMP", [P, D], F32, m_off + 2 * KD * T * 4 + NT * 512 * 4)[0]
        CG, CV, Y0d = stack(x_off, h_off, [("CG", [P, 2, T], F32), ("CV", [P, 2, T], F32), ("Y0d", [P, NT, 512], F32)])
        PH_hi, PH_lo = stack(h_off, h_end, [("PH_hi", [P, 2, 2, T], F32R), ("PH_lo", [P, 2, 2, T], F32R)])
        XM, PT_hi, PT_lo, Pn, SG = stack(m_off, m_off + 2 * KD * T * 4, [
            ("XM", [P, NT, D], F32), ("PT_hi", [P, 2, T], F32R), ("PT_lo", [P, 2, T], F32R),
            ("Pn", [P, NT, PLE], F32), ("SG", [P, 2, 512], F32)])
        E = put("E", [P, 2, NT, 512], F32, x_off)[0]
        LB = (LB0, LB1, LB2)
        GB, AB = (0, 1, 2), (3, 4, 5)
        JK = put("JK", [P, 512], F32, m_end - 2048)[0]
        JX = put("JX", [P, D], F32, m_off + 2 * KD * T * 4)[0]

        ps = ctx.enter_context(nc.psum_tensor("ps", [P, 8, 512], F32))
        zT = nc.dram_tensor("zT", [(ZROWS * NH + 4 * NH) * P, T], F32, kind="Internal").ap()
        abD = nc.dram_tensor("abD", [2 * NH * P, T], F32, kind="Internal").ap()
        zN = nc.dram_tensor("zN", [T, NH * 2 * P], F32, kind="Internal").ap()

        def sem(name):
            return ctx.enter_context(nc.semaphore(name))

        const_ld = sem("constants_loaded")
        const_ok = sem("constants_ready")
        lam_exp = sem("lambda_exponentials")
        waited = sem("waited")
        w_loaded = [sem("unit_loaded_slot0"), sem("unit_loaded_slot1")]
        w_hi = sem("unit_high_part")
        w_lo = sem("unit_low_part")
        w_used = sem("unit_used")
        s_x = [sem(f"x_tiles_loaded_{n}") for n in range(3)]
        s_x0 = sem("first_x_loaded")
        s_xm = sem("x_loaded_for_ple")
        s_wr = sem("rows_loaded")
        s_lay = sem("layer_constants_loaded")
        s_out = sem("x_stored")
        s_p = sem("p_loaded")
        z_st = sem("projection_stored")
        z_mid = sem("projection_first_half")
        z_out = sem("projection_out_of_psum")
        ab_st = [sem("gla_head_stored"), sem("att_head_stored")]
        s_ab = sem("heads_loaded")
        s_fz, s_v, s_g, s_qk, s_vd = (sem(n) for n in ("gla_qf_loaded", "gla_v_loaded", "gla_g_loaded", "att_qk_loaded", "att_v_loaded"))
        s_gt = [sem("gates_loaded_0"), sem("gates_loaded_1")]

        def steps(name, names, credit=False):
            return Steps(sem(name), names, len(names) if credit else 0)

        lay_dve = steps("layer_dve", ["lay", "slw"])
        n1 = {e: steps(f"norm1_{e}", norm_names(e, False)) for e in ("act", "dve", "pool", "pe")}
        nr = {e: steps(f"resnorm_{e}", norm_names(e, True)) for e in ("act", "dve", "pool", "pe")}
        ga, gd, gp = gla_names()
        G_act, G_dve, G_pe = steps("gla_act", ga, True), steps("gla_dve", gd, True), steps("gla_pe", gp, True)
        G_pool = steps("gla_pool", ["ms", "rs"])
        ta, td, tp = att_names()
        A_act, A_dve, A_pe = steps("att_act", ta, True), steps("att_dve", td, True), steps("att_pe", tp, True)
        A_pool = steps("att_pool", ["ms", "rs"])
        ab_act = steps("ab_act", [f"h{c}" for c in range(KD)])
        ab_dve = steps("ab_dve", [f"l{c}" for c in range(KD)])
        br_pe = steps("br_pe", ["blk0", "blk1"])
        br_act = steps("br_act", [f"{k}{u}_{b}" for u in range(2) for b in range(2) for k in ("sg", "mh")])
        br_dve = steps("br_dve", [f"{k}{u}_{b}" for u in range(2) for b in range(2) for k in ("ta0", "ta1", "tb0", "tb1", "m", "ml")], True)
        wo_pe = steps("wo_pe", [f"a{c}_{t}" for c in range(2) for t in range(NT - 1)])
        wo_act = steps("wo_act", [f"sq{t}" for t in range(NT)])
        wo_dve = steps("wo_dve", [f"y{t}" for t in range(NT)])
        up_pe = steps("up_pe", ["blk0", "blk1"])
        up_act = steps("up_act", [f"{k}{u}" for u in range(2) for k in ("cg0_", "cg1_", "cv0_", "cv1_", "ge")], True)
        up_dve = steps("up_dve", [f"{k}{u}" for u in range(2) for k in
                                  ("cp", "g0l", "g0r", "g1l", "g1r", "v0l", "v0r", "v1l", "v1r", "pr")], True)
        dn_pe = steps("dn_pe", [f"a{c}_{t}" for c in range(2) for t in range(NT - 1)])
        dn_act = steps("dn_act", [f"ph{j}" for j in range(12)] + [f"sq{t}" for t in range(NT)] + [f"ph{j}" for j in range(12, 22)])
        dn_dve = steps("dn_dve", [f"pl{j}" for j in range(12)] + [f"y{t}" for t in range(NT)] + [f"pl{j}" for j in range(12, 22)])
        pt_pe = steps("pt_pe", ["tr0", "tr1", "tr2"])
        pt_act = steps("pt_act", ["h0", "h1", "h2"])
        pt_dve = steps("pt_dve", ["l0", "l1", "l2"])
        pe_pe = steps("ple_pe", [f"e{c}_{t}" for c in range(2) for t in range(NT - 1)])
        pe_act = steps("ple_act", [f"e{c}_{t}" for c in range(2) for t in range(NT)])
        pg_pe = steps("gate_pe", [f"g{c}_{t}" for c in range(2) for t in range(NT - 1)])
        pg_act = steps("gate_act", [x for c in range(2) for t in range(NT + 1)
                                    for x in ([f"s{c}_{t}"] if t < NT else []) + ([f"q{c}_{t - 1}"] if t else [])])
        pg_dve = steps("gate_dve", [f"m{c}_{t}" for c in range(2) for t in range(NT)])
        fin_pool = steps("fin_pool", [f"{k}{t}" for t in range(NT) for k in ("s", "m", "r")])
        fin_dve = steps("fin_dve", [f"{k}{t}" for t in range(NT) for k in ("a", "b", "x")], True)

        def unit(L, j, i=None, each=2):
            n, half = L * N_UNITS + j, L * (N_UNITS // 2) + j // 2
            return (n, half, j % 2) if i is None else (n + i * each, half + i * (each // 2), j % 2)

        def side_unit(L, h, u):
            first = HEAD_U + (SIDE_U * (NH - 1) if h is None else 0)
            e = L * N_IN + (first + u)
            return (unit(L, first + u), e) if h is None else (unit(L, first + u, h, SIDE_U), e + h * SIDE_U)

        def heads_stored(L, h):
            return (L * (NH - 1) + (NH - 1)) * 16 + 16 if h is None else (L * (NH - 1) + h) * 16 + 16

        block = ctx.enter_context(nc.Block())

        @block.sync
        def _(sp):
            for dst, src in ((ident[:], ident_in), (X[:, 0, 0:len(LEVELS) * P], masks_in), (lbl[:], lb_logits)):
                sp.dma_start(dst, src).then_inc(const_ld, 16)
            sp.dma_start(hn[:, 0:2 * DEPTH * 2 * DA_DH], lam_in.partition_broadcast(P)).then_inc(const_ld, 16)
            sp.dma_start(XM[:], x_in.rearrange("(t p) d -> p t d", p=P)).then_inc(s_x0, 16)
            sp.dma_start(out, x_in).then_inc(s_out, 16)
            for s in (G_act, G_dve, G_pe, A_act, A_dve, A_pe, br_dve, up_act, up_dve, fin_dve):
                sp.sem_inc(s.sem, s.credit)
            for s in (w_lo, w_used):
                sp.sem_inc(s, CREDIT)
            for s in (z_st, *ab_st):
                sp.sem_inc(s, 16)

            def load(u, parts, width=ISLOTS):
                n, _, s = u
                sp.wait_ge(w_lo, n + 1)
                sp.sem_inc(waited, 1)
                at = 0
                for src in parts:
                    cols = width // len(parts)
                    sp.dma_start(raw[:, s, at:at + cols].rearrange("p (k n) -> p k n", n=src.shape[-1]), src)\
                        .then_inc(w_loaded[s], 16 * 2 // len(parts))
                    at += cols

            def rows(w, L, k0, nk, c0, nc_):
                return w[bass.ds(L, 1), k0 * P:(k0 + nk) * P, bass.ds(c0, nc_)].rearrange("o (k p) n -> p (o k) n", p=P)

            with sp.Fori(0, DEPTH) as L:
                for j, u in enumerate(FIRST):
                    load(unit(L, j), [rows(w_in, L, 0, KD, g * HW, P) for g in GROUPS[u]])
                with sp.Fori(0, NH - 1) as h:
                    for u, groups in enumerate(GROUPS):
                        load(side_unit(L, h, u)[0], [rows(w_in, L, 0, KD, h * P + (P + g * HW), P) for g in groups])
                    for u in range(GATE_U):
                        load(side_unit(L, h, HEAD_U + u)[0], [rows(w_in, L, 0, KD, h * (GATE_U * 256) + (8 * HW + u * 256), 256)])
                for u in range(2 * NH - GATE_U * (NH - 1)):
                    load(side_unit(L, None, u)[0], [rows(w_in, L, 0, KD, 8 * HW + (NH - 1) * GATE_U * 256 + u * 256, 256)])
                with sp.Fori(0, 2) as i:
                    for u in range(2):
                        load(unit(L, U_BR + u, i), [rows(w, L, 0, 4, i * 512 + u * 256, 256) for w in (w_a, w_b)])
                with sp.Fori(0, 2) as i:
                    for u in range(2):
                        load(unit(L, U_WO + u, i), [rows(w_out, L, 4 * u, 4, i * 512, 512)])
                with sp.Fori(0, NFF // 2) as i:
                    for u in range(2):
                        load(unit(L, U_UP + u, i), [rows(w_up, L, 0, KD, i * 256 + (u * P + half), P) for half in (0, FF)])
                for c in range(2):
                    for j in range(11):
                        load(unit(L, U_DN + c * 11 + j), [rows(w_down, L, 2 * j, 2, c * 512, 512)], 1024)
                for c in range(2):
                    load(unit(L, U_PE + c), [rows(w_ple, L, 0, 2, c * 512, 512)], 1024)
                for c in range(2):
                    for u in range(2):
                        load(unit(L, U_PG + 2 * c + u), [rows(w_ple_gate, L, 4 * u, 4, c * 512, 512)])

        @block.tensor
        def _(pe):
            mm = nc.tensor.matmul
            pe.wait_ge(const_ld, 64)
            PASSES = ((0, 0), (0, 1), (1, 0))
            hT, mT, PH, PT, W = (hT_hi, hT_lo), (mT_hi, mT_lo), (PH_hi, PH_lo), (PT_hi, PT_lo), (whi, wlo)

            def unit_ready(u):
                pe.wait_ge(w_lo, u[0] + (1 + CREDIT))

            def feature_block(rhs, s, chunks, banks, ready=None):
                n = len(chunks) * 3
                i = 0
                for w0, k in chunks:
                    if ready:
                        ready(k)
                    for a, b in PASSES:
                        for (t0, tn), bank in zip(HALVES, banks):
                            ins = mm(ps[:, bank, 0:tn], W[b][:, s, w0:w0 + P], rhs[a][:, k, t0:t0 + tn],
                                     start=(i == 0), stop=(i == n - 1))
                        i += 1
                return ins

            def token_chunks(lhs, s, chunks, first, last, counter, names, free=None):
                for i, (w, k) in enumerate(chunks):
                    for t in range(NT):
                        if free and first and i == 0:
                            free(t)
                        for q, (a, b) in enumerate(PASSES):
                            end = last and i == len(chunks) - 1 and q == 2
                            ins = mm(ps[:, t, :], lhs[a][:, k, t * P:(t + 1) * P] if not callable(k) else k(a, t),
                                     W[b][:, s, w * 512:(w + 1) * 512], start=(first and i == 0 and q == 0), stop=end)
                        if end and t < NT - 1:
                            ins.then_inc(*counter.step(names[t]))
                ins.then_inc(w_used, 1)

            def token_tiles(lhs, units, counter, names, free, after=None):
                for t in range(NT):
                    if free:
                        free(t)
                    for u, w in enumerate(units):
                        if t == 0:
                            unit_ready(w)
                        for k in range(4):
                            for q, (a, b) in enumerate(PASSES):
                                ins = mm(ps[:, t, :], lhs[a][:, 4 * u + k, t * P:(t + 1) * P], W[b][:, w[2], k * 512:(k + 1) * 512],
                                         start=(u == 0 and k == 0 and q == 0), stop=(u == 1 and k == 3 and q == 2))
                        if t == NT - 1:
                            ins.then_inc(w_used, 1)
                    if t < NT - 1:
                        ins.then_inc(*counter.step(names[t]))
                    if after:
                        after(t)

            def norm_transposes(c, it, ahead=None, after=None, tiles=range(NT)):
                for t in tiles:
                    if ahead and t == 0:
                        ahead(0)
                    if ahead and t + 1 < NT:
                        ahead(t + 1)
                    pe.wait_ge(c["dve"].sem, c["dve"].at(it, f"hn{t}"))
                    for h in range(2):
                        if t:
                            pe.wait_ge(c["dve"].sem, c["dve"].at(it, f"lo{t - 1}_{h}"))
                        for k in range(4):
                            ins = nc.tensor.transpose(ps[:, 6 + h, k * P:(k + 1) * P],
                                                      hn[:, (4 * h + k) * P:(4 * h + k + 1) * P], ident[:])
                        ins.then_inc(*c["pe"].step(f"tr{t}_{h}"))
                    if after and t:
                        after(t - 1)
                if after:
                    after(NT - 1)

            def gla_keys(it):
                pe.wait_ge(G_dve.sem, G_dve.at(it, "kh"))
                for b in range(3):
                    for i in range(4):
                        d, c = divmod(4 * b + i, NT)
                        ins = nc.tensor.transpose(ps[:, GB[b], i * P:(i + 1) * P], LB2[:, d, c * P:(c + 1) * P], ident[:])
                    ins.then_inc(*G_pe.step(f"trk{b}"))
                pe.wait_ge(G_act.sem, G_act.at(it, "kht1"))
                for c in range(NT):
                    o = ps[:, GB[c // 4], (c % 4) * P:(c % 4 + 1) * P]
                    mm(o, Kb[:, 0, c * P:(c + 1) * P], Qb[:, c * P:(c + 1) * P], start=True, stop=False)
                    ins = mm(o, Kb[:, 1, c * P:(c + 1) * P], Qb[:, c * P:(c + 1) * P], start=False, stop=True)
                ins.then_inc(*G_pe.step("diag"))
                pe.wait_ge(G_act.sem, G_act.at(it, "kht2"))
                pe.wait_ge(s_v, it * 16 + 16)
                pe.wait_ge(G_dve.sem, G_dve.at(it, "at0"))
                for n, (d, c) in enumerate(STATES):
                    ins = mm(ps[:, GB[2 - 2 * (n // 4)], (n % 4) * P:(n % 4 + 1) * P], khT[:, d * NT + c, :], vN[:, c, :],
                             start=True, stop=True)
                ins.then_inc(*G_pe.step("ds"))

            def gla_level(it, l):
                h, buf = LEVELS[l], LB[l % 3]
                pe.wait_ge(G_dve.sem, G_dve.at(it, f"mq{l}"))
                for d in range(2):
                    n = 2 * l + d
                    pe.wait_ge(G_dve.sem, G_dve.at(it, f"cp{(n - 3) // 2}_{(n - 3) % 2}" if n >= 3 else "s1"))
                    for c in range(NT):
                        ins = mm(ps[:, GB[(n + 1) % 3], c * 64:(c + 1) * 64], buf[:, d, c * P:(c + 1) * P],
                                 view(buf[:], d * T + c * P + (0 if d else h), [[2 * h, 64 // h], [1, h]]),
                                 start=True, stop=True)
                    ins.then_inc(*G_pe.step(f"lv{l}_{d}"))

            def gla_out(it):
                pe.wait_ge(G_dve.sem, G_dve.at(it, f"cp{len(LEVELS) - 1}_1"))
                for c in range(NT):
                    o = ps[:, GB[c // 4], (c % 4) * P:(c % 4 + 1) * P]
                    carried = [(d, n) for d, n, cc in CARRIES if cc == c]
                    mm(o, AT[:, c, :], vN[:, c, :], start=True, stop=False)
                    for i, (d, n) in enumerate(carried):
                        ins = mm(o, QH[:, d, c * P:(c + 1) * P], S[:, n, :], start=False, stop=(i == len(carried) - 1))
                    if c in (3, 5):
                        ins.then_inc(*G_pe.step(f"o{c // 4}"))

            def out_transposes(dve_steps, pe_steps, it, o, banks):
                for c in range(NT):
                    if c in (0, 4):
                        pe.wait_ge(dve_steps.sem, dve_steps.at(it, f"on{3 if c == 0 else 5}"))
                    ins = nc.tensor.transpose(ps[:, banks[c // 4], (c % 4) * P:(c % 4 + 1) * P], o[:, c, :], ident[:])
                    if c in (3, 5):
                        ins.then_inc(*pe_steps.step(f"tro{c // 4}"))

            def att_scores(it, q):
                k0, kn = SEQ_OF[q]
                if q == 0:
                    pe.wait_ge(A_dve.sem, A_dve.at(it, "radd"))
                else:
                    pe.wait_ge(A_act.sem, A_act.at(it, f"e{q - 1}_1"))
                for m in range(2):
                    rows_ = slice(m * DA_DH, (m + 1) * DA_DH)
                    ins = mm(ps[:, AB[m], 0:kn], QK[rows_, 0, q * P:(q + 1) * P], QK[rows_, 1, k0:k0 + kn], start=True, stop=True)
                ins.then_inc(*A_pe.step(f"sc{q}"))

            def att_turn_weights(it, q):
                pe.wait_ge(A_dve.sem, A_dve.at(it, f"al{q}"))
                if q:
                    pe.wait_ge(A_act.sem, A_act.at(it, f"oc{q - 1}"))
                for j in range(SEQ_OF[q][1] // P):
                    ins = nc.tensor.transpose(ps[:, AB[2], j * P:(j + 1) * P], PR[:, q % 2, 0, j * P:(j + 1) * P], ident[:])
                ins.then_inc(*A_pe.step(f"tra{q}"))

            def att_values(it, q):
                k0, kn = SEQ_OF[q]
                pe.wait_ge(A_act.sem, A_act.at(it, f"at{q}"))
                if q == 0:
                    pe.wait_ge(s_vd, it * 16 + 16)
                for j in range(kn // P):
                    ins = mm(ps[:, AB[2], 0:P], At[:, q % 2, j * P:(j + 1) * P], vD[:, k0 // P + j, :],
                             start=(j == 0), stop=(j == kn // P - 1))
                ins.then_inc(*A_pe.step(f"av{q}"))

            def project(w, e, q, token, banks, gate=False):
                if q == 0:
                    unit_ready(w)
                b, half = divmod(q, 2)
                if token:
                    for t in ((0, 1), (2, 3), (4,), (5,))[q]:
                        o = ps[:, (banks[0][0], banks[0][1], banks[1][0])[t // 2], (t % 2) * 256:(t % 2 + 1) * 256]
                        for k in range(KD):
                            for i, (x, y) in enumerate(PASSES):
                                ins = mm(o, hT[x][:, k, t * P:(t + 1) * P], view(W[y][:], w[2] * ISLOTS + k * P, [[1024, 2], [1, P]]),
                                         start=(k == 0 and i == 0), stop=(k == KD - 1 and i == 2))
                else:
                    for k in range(4 * half, 4 * half + 4):
                        for i, (x, y) in enumerate(PASSES):
                            for (t0, tn), bank in zip(HALVES, banks[b]):
                                w0 = k * 256 + b * P if gate else b * 1024 + k * P
                                ins = mm(ps[:, bank, 0:tn], W[y][:, w[2], w0:w0 + P],
                                         hT[x][:, k, t0:t0 + tn], start=(k == 0 and i == 0), stop=(k == KD - 1 and i == 2))
                if half:
                    ins.then_inc(z_mid if b == 0 else w_used, 1)

            def mixers(it, L, h, slots):
                def side(s):
                    for n in slot_work(slots, s)[0]:
                        w, e = side_unit(L, h, n // 4)
                        token = h is not None and n // 4 == HEAD_U - 1
                        if n % 2 == 0:
                            pe.wait_ge(z_out, e * 4 + (1 if token and n % 4 else n % 4))
                        project(w, e, n % 4, token, ((6, 7), (6, 7)), h is None or n // 4 >= HEAD_U)

                side(0)
                side(1)
                side(2)
                att_scores(it, 0)
                side(3)
                gla_keys(it)
                side(4)
                for k in range(len(LEVELS)):
                    if k + 1 < NT:
                        att_scores(it, k + 1)
                    gla_level(it, k)
                    if k:
                        att_values(it, k - 1)
                    side(5 + k)
                    if k < NT:
                        att_turn_weights(it, k)
                side(12)
                gla_out(it)
                side(13)
                out_transposes(A_dve, A_pe, it, O2, (AB[0], AB[1]))
                side(14)
                out_transposes(G_dve, G_pe, it, O1, (GB[2], GB[0]))

            with pe.Fori(0, DEPTH) as L:
                def first_quarters(t):
                    if t in (1, 3, 4, 5):
                        pe.wait_ge(n1["dve"].sem, n1["dve"].at(L, f"lo{t}_1"))
                        project(unit(L, 0), L * N_IN, (1, 3, 4, 5).index(t), True, ((0, 1), (2, 3)))

                norm_transposes(n1, L, after=first_quarters)
                for u in range(1, HEAD_U):
                    b0 = 4 * (u % 2)
                    for q in range(4):
                        if u >= 2 and q % 2 == 0:
                            pe.wait_ge(z_out, L * (4 * N_IN) + (4 * (u - 2) + q + 2))
                        project(unit(L, u), L * N_IN + u, q, False, ((b0, b0 + 1), (b0 + 2, b0 + 3)))
                with pe.Fori(0, NH - 1) as h:
                    mixers(L * NH + h, L, h, SLOTS)
                mixers(L * NH + (NH - 1), L, None, SLOTS_LAST)
                with pe.Fori(0, 2) as i:
                    it = L * 2 + i
                    for u in range(2):
                        w = unit(L, U_BR + u, i)
                        unit_ready(w)
                        for b in range(2):
                            pe.wait_ge(br_dve.sem, br_dve.at(it, f"tb10_{b}") if u else br_dve.before(it, f"tb11_{b}"))
                            split = (lambda k: pe.wait_ge(ab_dve.sem, ab_dve.at(L, f"l{k}"))) if (u, b) == (0, 0) else None
                            feature_block(hT, w[2], [(k * 256 + b * P, k) for k in range(4)], (4 * b, 4 * b + 1), split)
                            ins = feature_block(hT, w[2], [(1024 + k * 256 + b * P, 4 + k) for k in range(4)], (4 * b + 2, 4 * b + 3), split)
                            ins.then_inc(*(br_pe.step(f"blk{u}") if b == 0 else (w_used, 1)))
                pe.wait_ge(br_dve.sem, br_dve.last(L * 2 + 1))
                for u in range(2):
                    w = unit(L, U_WO + u)
                    unit_ready(w)
                    token_chunks(mT, w[2], [(k, 4 * u + k) for k in range(4)], u == 0, u == 1, wo_pe, [f"a0_{t}" for t in range(NT - 1)])
                token_tiles(mT, [unit(L, U_WO + 2 + u) for u in range(2)], wo_pe, [f"a1_{t}" for t in range(NT - 1)],
                            lambda t: pe.wait_ge(wo_dve.sem, wo_dve.at(L, f"y{t}")),
                            lambda t: norm_transposes(nr, L * 2, tiles=(t - 3,)) if t >= 3 else None)
                norm_transposes(nr, L * 2, tiles=range(3, NT))
                pe.wait_ge(nr["dve"].sem, nr["dve"].last(L * 2))
                pe.sem_inc(waited, 1)
                with pe.Fori(0, NFF // 2) as i:
                    it = L * (NFF // 2) + i
                    for u in range(2):
                        w = unit(L, U_UP + u, i)
                        unit_ready(w)
                        for b in range(2):
                            pe.wait_ge(up_dve.sem, up_dve.before(it, f"{'gv'[b]}1r{u}"))
                            ins = feature_block(hT, w[2], [(b * 1024 + k * P, k) for k in range(KD)],
                                                (4 * u + 2 * b, 4 * u + 2 * b + 1))
                            ins.then_inc(*(up_pe.step(f"blk{u}") if b == 0 else (w_used, 1)))
                pe.wait_ge(up_dve.sem, up_dve.last(L * (NFF // 2) + (NFF // 2 - 1)))
                for c in range(2):
                    for j in range(11):
                        n = 11 * c + j
                        w = unit(L, U_DN + n)
                        unit_ready(w)
                        pe.wait_ge(dn_dve.sem, dn_dve.at(L, f"pl{n}"))
                        token_chunks(PH, w[2], [(k, (lambda a, t, k=k: PH[a][:, n % 2, k, t * P:(t + 1) * P])) for k in range(2)],
                                     j == 0, j == 10, dn_pe, [f"a{c}_{t}" for t in range(NT - 1)],
                                     (lambda t: pe.wait_ge(dn_dve.sem, dn_dve.at(L, f"y{t}"))) if c else None)
                pe.wait_ge(s_p, L * 16 + 16)
                for b in range(3):
                    if b == 2:
                        pe.wait_ge(pt_dve.sem, pt_dve.at(L, "l0"))
                    for i in range(4):
                        k, t = divmod(4 * b + i, NT)
                        ins = nc.tensor.transpose(ps[:, 6 + b % 2, i * P:(i + 1) * P], Pn[:, t, k * P:(k + 1) * P], ident[:])
                    ins.then_inc(*pt_pe.step(f"tr{b}"))
                pe.wait_ge(pt_dve.sem, pt_dve.last(L))
                def e_tile(c, t):
                    if c:
                        pe.wait_ge(pe_act.sem, pe_act.at(L, f"e0_{t}"))
                    else:
                        pe.wait_ge(nr["dve"].sem, nr["dve"].at(L * 2 + 1, f"ra{t}"))
                    for k in range(2):
                        for q, (a, b) in enumerate(PASSES):
                            ins = mm(ps[:, t, :], PT[a][:, k, t * P:(t + 1) * P], W[b][:, (U_PE + c) % 2, k * 512:(k + 1) * 512],
                                     start=(k == 0 and q == 0), stop=(k == 1 and q == 2))
                    ins.then_inc(*(pe_pe.step(f"e{c}_{t}") if t < NT - 1 else (w_used, 1)))

                unit_ready(unit(L, U_PE))
                norm_transposes(nr, L * 2 + 1, lambda t: e_tile(0, t))
                unit_ready(unit(L, U_PE + 1))
                for t in range(NT):
                    e_tile(1, t)
                pe.wait_ge(nr["dve"].sem, nr["dve"].last(L * 2 + 1))
                for u in range(2):
                    w = unit(L, U_PG + u)
                    unit_ready(w)
                    token_chunks(hT, w[2], [(k, 4 * u + k) for k in range(4)], u == 0, u == 1, pg_pe, [f"g0_{t}" for t in range(NT - 1)],
                                 lambda t: pe.wait_ge(pe_act.sem, pe_act.at(L, f"e1_{t}")))
                token_tiles(hT, [unit(L, U_PG + 2 + u) for u in range(2)], pg_pe, [f"g1_{t}" for t in range(NT - 1)],
                            lambda t: pe.wait_ge(pg_act.sem, pg_act.at(L, f"s0_{t}")))

        mark = {}

        @block.vector
        def _(dve):
            v = nc.vector
            count = [0]

            def link(ins, name=None):
                count[0] += 1
                ins.then_inc(const_ok, 1)
                dve.wait_ge(const_ok, count[0])
                if name:
                    mark[name] = count[0]

            def done(c, it, name):
                dve.wait_ge(c.sem, c.at(it, name))

            link(v.memset(rmask[:], 1))
            link(v.memset(view(rmask[:], 0, [[P, NT]]), 0))
            link(v.memset(half_neg[:], -0.5))
            dve.wait_ge(const_ld, 64)
            link(v.tensor_copy(masks[:].rearrange("p a j -> p (a j)"), X[:, 0, 0:len(LEVELS) * P]))
            link(v.tensor_tensor(view(hn[:], 512, [[128, 2], [64, 2], [1, 64]]), view(hn[:], 0, [[256, 2], [128, 2], [1, 64]]),
                                 view(hn[:], 64, [[256, 2], [128, 2], [1, 64]]), ALU.mult))
            link(v.tensor_reduce(lams[:, 0:4], view(hn[:], 512, [[64, 4], [1, 64]]), AX_X, ALU.add))
            l0, l1 = view(lbl[:], 0, [[2, 8]]), view(lbl[:], 1, [[2, 8]])
            link(v.tensor_tensor(lbs[:, 0:8], l0, l1, ALU.max))
            link(v.tensor_tensor(view(lbs[:], 8, [[2, 8], [1, 2]]), view(lbl[:], 0, [[2, 8], [1, 2]]),
                                 view(lbs[:], 0, [[1, 8], [0, 2]]), ALU.subtract), "exponents")
            dve.wait_ge(lam_exp, 2)
            e0, e1 = view(lbs[:], 24, [[2, 8]]), view(lbs[:], 25, [[2, 8]])
            link(v.tensor_tensor(lbs[:, 40:48], e0, e1, ALU.add))
            link(v.reciprocal(lbs[:, 48:56], lbs[:, 40:48]))
            link(v.tensor_tensor(view(lbs[:], 8, [[2, 8], [1, 2]]), view(lbs[:], 24, [[2, 8], [1, 2]]),
                                 view(lbs[:], 48, [[1, 8], [0, 2]]), ALU.mult))
            p0, p1 = view(lbs[:], 8, [[2, 8]]), view(lbs[:], 9, [[2, 8]])
            link(v.tensor_tensor(lbs[:, 40:48], p0, p1, ALU.add))
            link(v.tensor_tensor(lbs[:, 56:64], lbs[:, 40:48], p0, ALU.subtract))
            link(v.tensor_tensor(lbs[:, 48:56], p0, p0, ALU.subtract))
            for l in range(DEPTH):
                lb = lbs[:, 48 + 8 * l:56 + 8 * l]
                link(v.tensor_scalar(view(lbtab[:], 16 * l, [[2, 8]]), lb, -1.0, 1.0, ALU.mult, ALU.add))
                link(v.tensor_scalar(view(lbtab[:], 16 * l + 1, [[2, 8]]), lb, LB_FLOOR, None, ALU.max))
                link(v.tensor_tensor(lams[:, 8 + l:9 + l], lams[:, 5 + 2 * l:6 + 2 * l], lams[:, 4 + 2 * l:5 + 2 * l], ALU.subtract))
                link(v.tensor_scalar(laytab[:, 2 * l:2 * l + 1], lams[:, 8 + l:9 + l], -lambda_init(l), None, ALU.add))
                link(v.memset(laytab[:, 2 * l + 1:2 * l + 2], 1.0 - lambda_init(l)), "all")

            def low(u, width=ISLOTS):
                n, _, s = u
                dve.wait_ge(w_hi, n + 1)
                v.tensor_tensor(wlo[:, s, 0:width], raw[:, s, 0:width], whi[:, s, 0:width].bitcast(F32), ALU.subtract)\
                    .then_inc(w_lo, 1)

            def norm_stage(c, it, x, weight, residual=None, bank_ready=None, extra=None):
                for s in range(NT + 2):
                    r, n, h = s, s - 1, s - 2
                    if r < NT and residual is not None:
                        bank_ready(r)
                        done(c["pool"], it, f"ry{r}")
                        if r:
                            done(c["dve"], it, f"rx{r - 1}")
                        v.scalar_tensor_tensor(TMP[:, 512:D], ps[:, r, :], rsy[:, r:r + 1], wrows[:, 1, 512:D], ALU.mult, ALU.mult)\
                            .then_inc(*c["dve"].step(f"ra{r}"))
                        v.scalar_tensor_tensor(TMP[:, 0:512], residual[:, r, :], rsy[:, r:r + 1], wrows[:, 1, 0:512], ALU.mult, ALU.mult)\
                            .then_inc(*c["dve"].step(f"rb{r}"))
                        done(c["dve"], it, f"rb{r}")
                        v.tensor_tensor(x[:, r, :], x[:, r, :], TMP[:], ALU.add).then_inc(*c["dve"].step(f"rx{r}"))
                    if 0 <= n < NT:
                        done(c["pool"], it, f"rs{n}")
                        if n:
                            done(c["pe"], it, f"tr{n - 1}_1")
                        if weight:
                            v.scalar_tensor_tensor(hn[:], x[:, n, :], rsx[:, n:n + 1], wrows[:, 0, :], ALU.mult, ALU.mult)\
                                .then_inc(*c["dve"].step(f"hn{n}"))
                        else:
                            v.tensor_scalar(hn[:], x[:, n, :], rsx[:, n:n + 1], None, ALU.mult).then_inc(*c["dve"].step(f"hn{n}"))
                    if h >= 0:
                        for k in range(2):
                            done(c["act"], it, f"hi{h}_{k}")
                            v.tensor_tensor(hT_lo[:, 4 * k:4 * k + 4, h * P:(h + 1) * P],
                                            ps[:, 6 + k, :].rearrange("p (k t) -> p k t", k=4),
                                            hT_hi[:, 4 * k:4 * k + 4, h * P:(h + 1) * P].bitcast(F32), ALU.subtract)\
                                .then_inc(*c["dve"].step(f"lo{h}_{k}"))
                    if extra:
                        extra(s)


            def gla_gates(it):
                G = G_dve
                dve.wait_ge(G_pe.sem, G_pe.before(it, "tro1"))
                v.tensor_copy(lb_now[:], lbtab[:, bass.ds(it * 4, 4)]).then_inc(*G.step("lb"))
                done(G_act, it, "silu_q")
                v.tensor_scalar(Qb[:], FZ[:, 0, :], float(P) ** -0.5, None, ALU.mult).then_inc(*G.step("qs"))
                done(G_act, it, "sig_neg")
                done(G, it, "lb")
                for d in range(2):
                    v.tensor_scalar(Kb[:, d, :], FZ[:, 1 + d, :], lb_now[:, 2 * d:2 * d + 1], None, ALU.mult).then_inc(*G.step(f"k{d}"))
                for d in range(2):
                    v.tensor_scalar(LB0[:, d, :], LB0[:, d, :], lb_now[:, 2 * d:2 * d + 1], lb_now[:, 2 * d + 1:2 * d + 2],
                                    ALU.mult, ALU.add).then_inc(*G.step(f"f{d}"))
                done(G, it, "f1")
                v.tensor_scalar(LB1[:], LB0[:], LN_SPLIT, None, ALU.max).then_inc(*G.step("fa"))
                v.tensor_scalar(LB2[:], LB0[:], 1.0 / LN_SPLIT, 1.0, ALU.mult, ALU.min).then_inc(*G.step("fb"))

            def gla_sums(it):
                G = G_dve
                done(G_act, it, "ln2")
                done(G, it, "fb")
                v.tensor_tensor(LB0[:], LB1[:], LB2[:], ALU.add).then_inc(*G.step("g"))
                done(G, it, "g")
                v.tensor_tensor_scan(B[:, 0, :], rmask[:], LB0[:, 0, :], 0.0, ALU.mult, ALU.add).then_inc(*G.step("scan0"))
                v.tensor_tensor_scan(B[:, 1, ::-1], rmask[:], LB0[:, 1, ::-1], 0.0, ALU.mult, ALU.add).then_inc(*G.step("scan1"))
                done(G, it, "scan1")
                differences(it, 0)

            def differences(it, l):
                h, out = LEVELS[l], LB[l % 3]
                nb_ = T // (2 * h)
                full = [[T, 2], [2 * h, nb_], [1, 2 * h]]
                v.tensor_tensor(view(out[:], 0, full), view(B[:], 0, full),
                                view(B[:], h - 1, [[T + 1, 2], [2 * h, nb_], [0, 2 * h]]), ALU.subtract).then_inc(*G_dve.step(f"D{l}"))

            def gla_decayed(it, L, h):
                G = G_dve
                done(G_act, it, "exp_b")
                ends = [[T - P + 1, 2], [P, NT]]
                v.tensor_copy(decay[:], view(LB1[:], P - 1, ends)).then_inc(*G.step("dec"))
                dve.wait_ge(ab_st[0], heads_stored(L, h))
                v.tensor_tensor(QH[:], view(Qb[:], 0, [[0, 2], [1, T]]), LB1[:], ALU.mult).then_inc(*G.step("qh"))
                v.tensor_tensor(view(LB2[:], 0, [[T, 2], [P, NT], [1, P]]), view(B[:], 0, [[T, 2], [P, NT], [1, P]]),
                                view(B[:], P - 1, ends + [[0, P]]), ALU.subtract).then_inc(*G.step("dl"))
                done(G_act, it, "exp_l")
                v.tensor_tensor(LB2[:], LB2[:], Kb[:], ALU.mult).then_inc(*G.step("kh"))
                done(G, it, "qh")
                differences(it, 1)

            def gla_diagonal(it):
                done(G_act, it, "silu_g")
                v.tensor_scalar(gT[:], gT[:], gn_col[:], None, ALU.mult).then_inc(*G_dve.step("gw"))
                done(G_pe, it, "diag")
                for k, n in ((0, 4), (1, 2)):
                    v.tensor_tensor(AT[:, 4 * k:4 * k + n, :], ps[:, GB[k], 0:n * P].rearrange("p (c t) -> p c t", t=P),
                                    view(ident[:], 0, [[0, n], [1, P]]), ALU.mult).then_inc(*G_dve.step(f"at{k}"))

            def level_keys(it, l):
                G, h = G_dve, LEVELS[l]
                nb_ = T // (2 * h)
                keys, queries = [[T + h, 2], [2 * h, nb_], [1, h]], [[T - h, 2], [2 * h, nb_], [1, h]]
                buf = LB[l % 3]
                done(G_act, it, f"xk{l}")
                v.tensor_tensor(view(buf[:], 0, keys), view(buf[:], 0, keys), view(Kb[:], 0, keys), ALU.mult).then_inc(*G.step(f"mk{l}"))
                done(G_act, it, f"xq{l}")
                v.tensor_tensor(view(buf[:], h, queries), view(buf[:], h, queries),
                                view(Qb[:], h, [[-h, 2], [2 * h, nb_], [1, h]]), ALU.mult).then_inc(*G.step(f"mq{l}"))
                if l + 2 < len(LEVELS):
                    if l == 0:
                        done(G_pe, it, "trk2")
                        done(G, it, "kh")
                    else:
                        done(G_pe, it, f"lv{l - 1}_1")
                    differences(it, l + 2)

            def carried_states(it):
                G = G_dve
                done(G_pe, it, "ds")
                for k in range(2):
                    v.tensor_copy(S[:, 4 * k:4 * k + 4, :], ps[:, GB[2 - 2 * k], :].rearrange("p (n v) -> p n v", v=P)).then_inc(*G.step(f"s{k}"))
                done(G, it, "s1")
                for i, (n, d, c) in enumerate(((2, 0, 3), (3, 0, 4), (6, 1, 4), (7, 1, 3))):
                    v.scalar_tensor_tensor(S[:, n, :], S[:, n - 1, :], decay[:, d, c:c + 1], S[:, n, :], ALU.mult, ALU.add)\
                        .then_inc(*G.step(f"s{2 + i}"))
                    done(G, it, f"s{2 + i}")

            def copy_level(it, l):
                G, h = G_dve, LEVELS[l]
                for d in range(2):
                    done(G_pe, it, f"lv{l}_{d}")
                    done(G, it, f"cp{l}_0" if d else f"cp{l - 1}_1" if l else "at1")
                    dve.sem_inc(waited, 1)
                    v.copy_predicated(view(AT[:], 0 if d else h, [[P, NT], [2 * h, 64 // h], [1, h]]),
                                      view(masks[:], (d * len(LEVELS) + l) * 64, [[0, NT], [h, 64 // h], [1, h]]),
                                      view(ps[:], GB[(2 * l + d + 1) % 3] * 512, [[64, NT], [h, 64 // h], [1, h]]))\
                        .then_inc(*G.step(f"cp{l}_{d}"))

            def gla_output(it):
                for k, n in ((0, 4), (1, 2)):
                    done(G_act, it, f"sq{k}")
                    v.tensor_copy(O1[:, 4 * k:4 * k + n, :],
                                  ps[:, GB[k], 0:n * P].rearrange("p (c v) -> p c v", v=P)).then_inc(*G_dve.step(f"o{k}"))
                v.tensor_reduce(st_g[:, 0, :], SQ1[:], AX_X, ALU.add).then_inc(*G_dve.step("ss"))

            def att_rope(it, L):
                A = A_dve
                dve.wait_ge(s_qk, it * 80 + 80)
                dve.wait_ge(s_wr, L * 96 + 32)
                for src, tab, n in ((QK, 0, "cqk"), (QKs, T, "sqk")):
                    v.tensor_tensor(src[:], src[:], view(rope[:], tab, [[0, 2], [1, T]]), ALU.mult).then_inc(*A.step(n))
                done(A, it, "sqk")
                v.tensor_tensor(QK[:], QK[:], QKs[:], ALU.add).then_inc(*A.step("radd"))

            def att_max(it, n):
                A, p = A_dve, n % 2
                done(A_pe, it, f"sc{n}")
                v.tensor_reduce(mx[:, p, :], ps[:, AB[0]:AB[0] + 2, 0:SEQ_OF[n][1]], AX_X, ALU.max, negate=True).then_inc(*A.step(f"mx{n}"))
                done(A, it, f"mx{n}")
                v.tensor_scalar(nb[:, p, :], mx[:, p, :], DA_DH ** -0.5, None, ALU.mult).then_inc(*A.step(f"nb{n}"))

            def att_weights(it, q):
                A, p, kn = A_dve, q % 2, SEQ_OF[q][1]
                done(A_act, it, f"e{q}_1")
                v.reciprocal(rc[:, p, :], sm[:, p, :]).then_inc(*A.step(f"rc{q}"))
                done(A, it, f"rc{q}")
                v.tensor_tensor(lr[:, p:p + 1], rc[:, p, 1:2], lay_now[:, 0:1], ALU.mult).then_inc(*A.step(f"lr{q}"))
                done(A, it, f"lr{q}")
                v.tensor_scalar(PR[:, p, 1, 0:kn], PR[:, p, 1, 0:kn], lr[:, p:p + 1], None, ALU.mult).then_inc(*A.step(f"a{q}"))
                done(A, it, f"a{q}")
                v.scalar_tensor_tensor(PR[:, p, 0, 0:kn], PR[:, p, 0, 0:kn], rc[:, p, 0:1], PR[:, p, 1, 0:kn],
                                       ALU.mult, ALU.add).then_inc(*A.step(f"al{q}"))

            def mixers(it, L, h, slots):
                def side(s):
                    for u in slot_work(slots, s)[2]:
                        low(side_unit(L, h, u + 1)[0])

                gla_gates(it)
                side(0)
                att_rope(it, L)
                side(1)
                gla_sums(it)
                side(2)
                gla_decayed(it, L, h)
                att_max(it, 0)
                side(3)
                gla_diagonal(it)
                side(4)
                for k in range(len(LEVELS)):
                    level_keys(it, k)
                    if k == 0:
                        carried_states(it)
                    else:
                        copy_level(it, k - 1)
                    if k < NT:
                        att_weights(it, k)
                    if k + 1 < NT:
                        att_max(it, k + 1)
                    side(5 + k)
                copy_level(it, len(LEVELS) - 1)
                done(A_act, it, "sq")
                v.tensor_reduce(st_t[:, 0, :], SQ2, AX_X, ALU.add).then_inc(*A_dve.step("ss"))
                side(12)
                gla_output(it)
                done(A_pool, it, "rs")
                for c in range(NT):
                    v.scalar_tensor_tensor(O2[:, c, :], O2[:, c, :], st_t[:, 2, c:c + 1], sl_row[:], ALU.mult, ALU.mult)\
                        .then_inc(*A_dve.step(f"on{c}"))
                side(13)
                done(G_pool, it, "rs")
                done(G_dve, it, "o1")
                for c in range(NT):
                    v.tensor_scalar(O1[:, c, :], O1[:, c, :], st_g[:, 2, c:c + 1], None, ALU.mult).then_inc(*G_dve.step(f"on{c}"))
                side(14)
                if h is None:
                    done(A_pe, it, "tro1")
                for k, n in ((0, 4), (1, 2)):
                    done(G_pe, it, f"tro{k}")
                    cols = slice(4 * k * P, (4 * k + n) * P)
                    v.tensor_tensor((abT[:, NH - 1, :] if h is None else ab1)[:, cols], ps[:, GB[2 - 2 * k], 0:n * P], gT[:, cols], ALU.mult).then_inc(*G_dve.step(f"ab{k}"))

            with dve.Fori(0, DEPTH) as L:
                dve.wait_ge(s_x0, 16)
                dve.wait_ge(s_wr, L * 96 + 16)
                norm_stage(n1, L, XM, True, extra=lambda s: low(unit(L, 0)) if s == 0 else None)
                dve.wait_ge(s_lay, L * 48 + 48)
                v.tensor_copy(lay_now[:], laytab[:, bass.ds(L * 2, 2)]).then_inc(*lay_dve.step("lay"))
                done(lay_dve, L, "lay")
                v.tensor_scalar(sl_row[:], sl_row[:], lay_now[:, 1:2], None, ALU.mult).then_inc(*lay_dve.step("slw"))
                for u in range(HEAD_U):
                    low(unit(L, u + 1))
                with dve.Fori(0, NH - 1) as h:
                    mixers(L * NH + h, L, h, SLOTS)
                mixers(L * NH + (NH - 1), L, None, SLOTS_LAST)
                for c in range(KD):
                    done(ab_act, L, f"h{c}")
                    v.tensor_tensor(hT_lo[:, c, :], abT[:, c, :], hT_hi[:, c, :].bitcast(F32), ALU.subtract).then_inc(*ab_dve.step(f"l{c}"))
                with dve.Fori(0, 2) as i:
                    it = L * 2 + i
                    for u in range(2):
                        low(unit(L, U_BR + u + 1, i))
                        for b in range(2):
                            n = f"{u}_{b}"
                            if b == 0:
                                done(br_pe, it, f"blk{u}")
                            else:
                                dve.wait_ge(w_used, unit(L, U_BR + u, i)[0] + 3)
                            done(br_act, it, f"sg{n}")
                            if (u, b) != (0, 0):
                                done(br_dve, it, f"ml{(2 * u + b - 1) // 2}_{(b + 1) % 2}")
                            else:
                                dve.wait_ge(br_dve.sem, br_dve.before(it, "ml1_1"))
                            for k, name, dst in ((0, "ta", BT1), (1, "tb", BT2)):
                                for hf, (t0, tn) in enumerate(HALVES):
                                    v.tensor_tensor(dst[:, t0:t0 + tn], GT[:, b, k, t0:t0 + tn], ps[:, 4 * b + 2 * k + hf, 0:tn], ALU.mult)\
                                        .then_inc(*br_dve.step(f"{name}{hf}{n}"))
                            done(br_dve, it, f"tb1{n}")
                            v.tensor_tensor(BT1[:], BT1[:], BT2[:], ALU.add).then_inc(*br_dve.step(f"m{n}"))
                            done(br_act, it, f"mh{n}")
                            blk = i * 4 + (2 * u + b)
                            v.tensor_tensor(mT_lo[:, bass.ds(blk, 1), :].rearrange("p o t -> p (o t)"), BT1[:],
                                            mT_hi[:, bass.ds(blk, 1), :].rearrange("p o t -> p (o t)").bitcast(F32), ALU.subtract)\
                                .then_inc(*br_dve.step(f"ml{n}"))
                low(unit(L, U_WO + 1))
                low(unit(L, U_WO + 2))
                for t in range(NT):
                    done(wo_act, L, f"sq{t}")
                    v.tensor_copy(Y0w[:, t, :], ps[:, t, :]).then_inc(*wo_dve.step(f"y{t}"))
                low(unit(L, U_WO + 3))
                dve.wait_ge(s_wr, L * 96 + 64)
                done(wo_dve, L, f"y{NT - 1}")
                for n in range(3):
                    dve.wait_ge(s_x[n], L * 16 + 16)
                norm_stage(nr, L * 2, X, True, Y0w, lambda t: None, lambda s: low(unit(L, U_UP)) if s == NT else None)
                with dve.Fori(0, NFF // 2) as i:
                    it = L * (NFF // 2) + i
                    for u in range(2):
                        low(unit(L, U_UP + u + 1, i))
                        if u == 0:
                            dve.wait_ge(up_dve.sem, up_dve.before(it, "pr1"))
                        dve.wait_ge(up_act.sem, up_act.before(it, f"cv1_{u}"))
                        v.tensor_copy(conv_now[:, u, :], conv_all[:, bass.ds(i * 2 + u, 1), :].rearrange("p o c -> p (o c)"))\
                            .then_inc(*up_dve.step(f"cp{u}"))
                        done(up_dve, it, f"cp{u}")
                        for gv, C in enumerate((CG, CV)):
                            nm = "gv"[gv]
                            done(up_act, it, f"c{nm}1_{u}")
                            for hf, (t0, tn) in enumerate(HALVES):
                                bank = 4 * u + 2 * gv + hf
                                left, right = C[:, u, t0 + 1:t0 + tn], C[:, u, t0:t0 + tn - 1]
                                v.scalar_tensor_tensor(left, ps[:, bank, 0:tn - 1], conv_now[:, u, 4 * gv:4 * gv + 1], left,
                                                       ALU.mult, ALU.add).then_inc(*up_dve.step(f"{nm}{hf}l{u}"))
                                done(up_dve, it, f"{nm}{hf}l{u}")
                                v.scalar_tensor_tensor(right, ps[:, bank, 1:tn], conv_now[:, u, 4 * gv + 2:4 * gv + 3], right,
                                                       ALU.mult, ALU.add).then_inc(*up_dve.step(f"{nm}{hf}r{u}"))
                        done(up_act, it, f"ge{u}")
                        done(up_dve, it, f"v1r{u}")
                        v.tensor_tensor(prod[:, bass.ds(i * 2 + u, 1), :].rearrange("p o t -> p (o t)"), CG[:, u, :], CV[:, u, :], ALU.mult)\
                            .then_inc(*up_dve.step(f"pr{u}"))

                def prod_low(n):
                    done(dn_act, L, f"ph{n}")
                    j = n % 11
                    v.tensor_tensor(PH_lo[:, n % 2], prod[:, 2 * j:2 * j + 2, :], PH_hi[:, n % 2].bitcast(F32), ALU.subtract)\
                        .then_inc(*dn_dve.step(f"pl{n}"))

                prod_low(0)
                for n in range(22):
                    low(unit(L, U_DN + n + 1), 1024)
                    if n + 1 < 22:
                        prod_low(n + 1)
                    if n == 10:
                        for t in range(NT):
                            done(dn_act, L, f"sq{t}")
                            v.tensor_copy(Y0d[:, t, :], ps[:, t, :]).then_inc(*dn_dve.step(f"y{t}"))
                for b in range(3):
                    done(pt_act, L, f"h{b}")
                    v.tensor_tensor(view(PT_lo[:], b * 512, [[1, 512]]), ps[:, 6 + b % 2, :],
                                    view(PT_hi[:], b * 512, [[1, 512]]).bitcast(F32), ALU.subtract).then_inc(*pt_dve.step(f"l{b}"))
                low(unit(L, U_PE + 1), 1024)
                dve.wait_ge(s_wr, L * 96 + 80)
                dve.wait_ge(s_xm, L * 16 + 16)
                norm_stage(nr, L * 2 + 1, XM, False, Y0d, lambda t: None)
                for j in range(4):
                    low(unit(L, U_PG + j))
                for t in range(NT):
                    done(pg_act, L, f"s0_{t}")
                    v.tensor_tensor(E[:, 0, t, :], SG[:, t % 2, :], E[:, 0, t, :], ALU.mult).then_inc(*pg_dve.step(f"m0_{t}"))
                dve.wait_ge(s_wr, L * 96 + 96)
                for s in range(NT + 1):
                    if s < NT:
                        done(pg_act, L, f"s1_{s}")
                        v.tensor_tensor(E[:, 1, s, :], SG[:, s % 2, :], E[:, 1, s, :], ALU.mult).then_inc(*pg_dve.step(f"m1_{s}"))
                    if s:
                        t = s - 1
                        done(fin_pool, L, f"r{t}")
                        if t:
                            done(fin_dve, L, f"x{t - 1}")
                        for c, n in ((0, "a"), (1, "b")):
                            v.scalar_tensor_tensor(TMP[:, c * 512:(c + 1) * 512], E[:, c, t, :], rsy[:, t:t + 1],
                                                   wrows[:, 1, c * 512:(c + 1) * 512], ALU.mult, ALU.mult).then_inc(*fin_dve.step(f"{n}{t}"))
                        done(fin_dve, L, f"b{t}")
                        v.tensor_tensor(XM[:, t, :], XM[:, t, :], TMP[:], ALU.add).then_inc(*fin_dve.step(f"x{t}"))

        @block.gpsimd
        def _(pool):
            g = nc.gpsimd
            pool.wait_ge(const_ok, 3)

            def done(c, it, name):
                pool.wait_ge(c.sem, c.at(it, name))

            def rstd(c, it, out, ms, ss, width, m, r, n=1, col=0):
                pool.sem_inc(waited, 1)
                g.tensor_scalar(ms, ss, 1.0 / width, EPS, ALU.mult, ALU.add).then_inc(*c.step(m))
                done(c, it, m)
                g.tensor_tensor(out, ms, half_neg[:, 0:n], ALU.pow).then_inc(*c.step(r))

            def norm_stage(c, it, residual=None):
                for s in range(NT + 2):
                    r, n = s, s - 1
                    if r < NT and residual:
                        done(c["act"], it, f"sqy{r}")
                        g.tensor_tensor(msy[:, r:r + 1], ssy[:, r:r + 1], ssy[:, NT + r:NT + r + 1], ALU.add).then_inc(*c["pool"].step(f"sy{r}"))
                        done(c["pool"], it, f"sy{r}")
                        rstd(c["pool"], it, rsy[:, r:r + 1], msy[:, r:r + 1], msy[:, r:r + 1], D, f"my{r}", f"ry{r}")
                    if 0 <= n < NT:
                        done(c["act"], it, f"sqx{n}")
                        rstd(c["pool"], it, rsx[:, n:n + 1], msx[:, n:n + 1], ssx[:, n:n + 1], D, f"mx{n}", f"rs{n}")

            with pool.Fori(0, DEPTH) as L:
                norm_stage(n1, L)
                with pool.Fori(0, NH) as h:
                    it = L * NH + h
                    for c_dve, c_pool, st in ((A_dve, A_pool, st_t), (G_dve, G_pool, st_g)):
                        done(c_dve, it, "ss")
                        rstd(c_pool, it, st[:, 2, :], st[:, 1, :], st[:, 0, :], P, "ms", "rs", NT)
                norm_stage(nr, L * 2, True)
                norm_stage(nr, L * 2 + 1, True)
                for t in range(NT):
                    done(pg_act, L, f"q1_{t}")
                    g.tensor_tensor(msy[:, t:t + 1], ssy[:, t:t + 1], ssy[:, NT + t:NT + t + 1], ALU.add).then_inc(*fin_pool.step(f"s{t}"))
                    done(fin_pool, L, f"s{t}")
                    rstd(fin_pool, L, rsy[:, t:t + 1], msy[:, t:t + 1], msy[:, t:t + 1], D, f"m{t}", f"r{t}")

        @block.scalar
        def _(act):
            a = nc.scalar.activation

            def done(c, it, name):
                act.wait_ge(c.sem, c.at(it, name))

            def high(u, width=ISLOTS):
                n, half, s = u
                act.wait_ge(w_loaded[s], half * 32 + 32)
                act.wait_ge(w_used, n + 1)
                a(whi[:, s, 0:width], raw[:, s, 0:width], ACT.Copy).then_inc(w_hi, 1)

            def used(u):
                act.wait_ge(w_used, u[0] + (1 + CREDIT))

            def norm_stage(c, it, x, junk, residual=None, extra=None, x_ready=None):
                for s in range(NT + 2):
                    r, n, h = s, s - 1, s - 2
                    if r < NT and residual is not None:
                        residual(r)
                        if r:
                            done(c["act"], it, f"sqy{r - 1}")
                        a(JK[:], ps[:, r, :], ACT.Square, accum_out=ssy[:, NT + r:NT + r + 1]).then_inc(*c["act"].step(f"sqy{r}"))
                    if 0 <= n < NT:
                        if residual is not None:
                            done(c["dve"], it, f"rx{n}")
                        else:
                            x_ready(n)
                        if n:
                            done(c["act"], it, f"sqx{n - 1}")
                        a(junk(n), x[:, n, :], ACT.Square, accum_out=ssx[:, n:n + 1]).then_inc(*c["act"].step(f"sqx{n}"))
                    if h >= 0:
                        for k in range(2):
                            done(c["pe"], it, f"tr{h}_{k}")
                            a(hT_hi[:, 4 * k:4 * k + 4, h * P:(h + 1) * P], ps[:, 6 + k, :].rearrange("p (k t) -> p k t", k=4), ACT.Copy)\
                                .then_inc(*c["act"].step(f"hi{h}_{k}"))
                    if extra:
                        extra(s)

            def row(dst, w, L, s):
                act.dma_start(dst, w[bass.ds(L, 1), :].partition_broadcast(P)).then_inc(s, 16)

            def load_x(dst_of, L):
                for n in range(3):
                    act.dma_start(X[:, 2 * n:2 * n + 2, :], out[n * 2 * P:(n + 1) * 2 * P, :].rearrange("(t p) d -> p t d", p=P))\
                        .then_inc(s_x[n], 16)

            def gla_gates(it):
                act.wait_ge(s_fz, it * 16 + 16)
                a(FZ[:, 0, :], FZ[:, 0, :], ACT.Silu).then_inc(*G_act.step("silu_q"))
                a(LB0[:], FZ[:, 1:3, :], ACT.Sigmoid).then_inc(*G_act.step("sig"))
                done(G_act, it, "sig")
                a(FZ[:, 1:3, :], FZ[:, 1:3, :], ACT.Sigmoid, scale=-1.0).then_inc(*G_act.step("sig_neg"))

            def gla_logarithms(it):
                done(G_dve, it, "fa")
                a(LB1[:], LB1[:], ACT.Ln).then_inc(*G_act.step("ln1"))
                done(G_dve, it, "fb")
                a(LB2[:], LB2[:], ACT.Ln).then_inc(*G_act.step("ln2"))

            def level_exponentials(it, l):
                h_ = LEVELS[l]
                nb_ = T // (2 * h_)
                keys, queries = [[T + h_, 2], [2 * h_, nb_], [1, h_]], [[T - h_, 2], [2 * h_, nb_], [1, h_]]
                buf = LB[l % 3]
                done(G_dve, it, f"D{l}")
                a(view(buf[:], 0, keys), view(buf[:], 0, keys), ACT.Exp, scale=-1.0).then_inc(*G_act.step(f"xk{l}"))
                a(view(buf[:], h_, queries), view(buf[:], h_, queries), ACT.Exp).then_inc(*G_act.step(f"xq{l}"))

            def att_exponentials(it, n):
                p, kn = n % 2, SEQ_OF[n][1]
                done(A_dve, it, f"nb{n}")
                if n >= 2:
                    done(A_pe, it, f"tra{n - 2}")
                for m in range(2):
                    a(PR[:, p, m, 0:kn], ps[:, AB[m], 0:kn], ACT.Exp, bias=nb[:, p, m:m + 1], scale=DA_DH ** -0.5,
                      accum_out=sm[:, p, m:m + 1]).then_inc(*A_act.step(f"e{n}_{m}"))

            def project_out(w, e, b, token, banks, dst):
                if b == 0:
                    act.wait_ge(z_mid, e + 1)
                else:
                    used(w)
                act.wait_ge(z_st, e * 32 + (16 * b + 16))
                if token:
                    places = ((banks[0], 0, 512), (banks[1], 0, 512)) if b == 0 else ((banks[0], 0, 256), (banks[0], 256, 256))
                else:
                    places = ((banks[0], 0, TP), (banks[1], 0, TS))
                at = 0
                for bank, c0, cn in places:
                    a(gst[:, at:at + cn], ps[:, bank, c0:c0 + cn], ACT.Copy).then_inc(z_out, 1)
                    at += cn
                act.wait_ge(z_out, e * 4 + (2 * b + 2))
                src = gst[:, 0:at]
                act.dma_start(dst, src.rearrange("p (t c) -> p t c", c=2 * P) if token else src).then_inc(z_st, 16)

            def head_place(h, u, b):
                if u == HEAD_U - 1:
                    return zN[4 * b * P:(6 if b else 4) * P, bass.ds(h * (2 * P), 2 * P)].rearrange("(t p) c -> p t c", p=P)
                return zT[bass.ds(h * (ZROWS * P) + (2 * u + b) * P, P), :]

            def load_qf(head):
                act.dma_start(FZ[:], zT[bass.ds(head * (ZROWS * P), 3 * P), :].rearrange("(n p) t -> p n t", p=P)).then_inc(s_fz, 16)

            def load_g(head):
                act.dma_start(gT[:], zT[bass.ds(head * (ZROWS * P) + 3 * P, P), :]).then_inc(s_g, 16)

            def load_qk(head, turned):
                src = zT[bass.ds(head * (ZROWS * P) + 4 * P, 2 * P), :].rearrange("(n p) t -> p n t", p=P)
                if not turned:
                    act.dma_start(QK[:], src).then_inc(s_qk, 16)
                else:
                    half = DA_DH // 2
                    for n in range(4):
                        act.dma_start(QKs[n * half:(n + 1) * half], src[(n ^ 1) * half:((n ^ 1) + 1) * half]).then_inc(s_qk, 16)

            def load_v(head):
                for dst, c0, s in ((vN, 0, s_v), (vD, P, s_vd)):
                    act.dma_start(dst[:], zN[:, bass.ds(head * (2 * P) + c0, P)].rearrange("(t p) c -> p t c", p=P)).then_inc(s, 16)

            def load_ab(first, n):
                act.dma_start(abT[:, first:first + n, :], abD[first * P:(first + n) * P, :].rearrange("(b p) t -> p b t", p=P)).then_inc(s_ab, 16)

            def mixers(it, L, h, slots):
                head = NH - 1 if h is None else h

                def side(s):
                    _, halves, split = slot_work(slots, s)
                    for n in halves:
                        u, b = divmod(n, 2)
                        w, e = side_unit(L, h, u)
                        if h is None:
                            row0 = (ZROWS * NH + 2 * GATE_U * (NH - 1) + n) * P
                            dst = zT[row0:row0 + P, :]
                        elif u < HEAD_U:
                            dst = head_place(h + 1, u, b)
                        else:
                            dst = zT[bass.ds(h * (2 * GATE_U * P) + (ZROWS * NH + n - 2 * HEAD_U) * P, P), :]
                        project_out(w, e, b, h is not None and u == HEAD_U - 1, (6, 7), dst)
                    for u in split:
                        high(side_unit(L, h, u + 1)[0])

                gla_gates(it)
                side(1)
                side(0)
                gla_logarithms(it)
                side(2)
                done(G_dve, it, "scan1")
                a(LB1[:], B[:], ACT.Exp).then_inc(*G_act.step("exp_b"))
                level_exponentials(it, 0)
                side(3)
                done(G_dve, it, "dl")
                a(LB2[:], LB2[:], ACT.Exp, scale=-1.0).then_inc(*G_act.step("exp_l"))
                act.wait_ge(s_g, it * 16 + 16)
                a(gT[:], gT[:], ACT.Silu).then_inc(*G_act.step("silu_g"))
                act.wait_ge(ab_st[1], heads_stored(L, h))
                att_exponentials(it, 0)
                for b in range(3):
                    done(G_pe, it, f"trk{b}")
                    a(view(FZ[:], b * 512, [[1, 512]]), ps[:, GB[b], :], ACT.Copy).then_inc(*G_act.step(f"kht{b}"))
                side(4)
                for k in range(len(LEVELS)):
                    if k + 1 < len(LEVELS):
                        level_exponentials(it, k + 1)
                    if k + 1 < NT:
                        att_exponentials(it, k + 1)
                    if k:
                        done(A_pe, it, f"av{k - 1}")
                        a(O2[:, k - 1, :], ps[:, AB[2], 0:P], ACT.Copy).then_inc(*A_act.step(f"oc{k - 1}"))
                    side(5 + k)
                    if h is not None and k == 3:
                        done(G_pe, it, "ds")
                        act.wait_ge(z_st, side_unit(L, h, 1)[1] * 32 + 32)
                        load_qf(h + 1)
                    if h is None and k == 6:
                        load_ab(0, 2)
                    if h is not None and k == 6:
                        act.wait_ge(z_st, side_unit(L, h, 2)[1] * 32 + 48)
                        load_qk(h + 1, False)
                    if k < NT:
                        kn = SEQ_OF[k][1]
                        done(A_pe, it, f"tra{k}")
                        a(At[:, k % 2, 0:kn], ps[:, AB[2], 0:kn], ACT.Copy).then_inc(*A_act.step(f"at{k}"))
                done(A_act, it, f"oc{NT - 1}")
                a(SQ2, O2, ACT.Square).then_inc(*A_act.step("sq"))
                side(12)
                for k, n in ((0, 4), (1, 2)):
                    done(G_pe, it, f"o{k}")
                    a(SQ1[:, 4 * k:4 * k + n, :], ps[:, GB[k], 0:n * P].rearrange("p (c v) -> p c v", v=P), ACT.Square)\
                        .then_inc(*G_act.step(f"sq{k}"))
                side(13)
                for k, n in ((0, 4), (1, 2)):
                    done(A_pe, it, f"tro{k}")
                    a((abT[:, 2 * NH - 1, :] if h is None else ab2)[:, 4 * k * P:(4 * k + n) * P], ps[:, AB[k], 0:n * P], ACT.Copy).then_inc(*A_act.step(f"ab{k}"))
                if h is None:
                    load_ab(2, 1)
                    load_ab(NH, NH - 1)
                else:
                    done(A_act, it, "ab1")
                    act.dma_start(abD[bass.ds(head * P + NH * P, P), :], ab2).then_inc(ab_st[1], 16)
                    load_qk(h + 1, True)
                side(14)
                side(15)
                done(G_dve, it, "ab1")
                if h is not None:
                    act.dma_start(abD[bass.ds(head * P, P), :], ab1).then_inc(ab_st[0], 16)
                    load_g(h + 1)
                    act.wait_ge(z_st, side_unit(L, h, 3)[1] * 32 + 48)
                    load_v(h + 1)

            act.wait_ge(const_ok, mark["exponents"])
            a(lams[:, 4:8], lams[:, 0:4], ACT.Exp).then_inc(lam_exp, 1)
            a(lbs[:, 24:40], lbs[:, 8:24], ACT.Exp).then_inc(lam_exp, 1)
            act.wait_ge(const_ok, mark["all"])

            with act.Fori(0, DEPTH) as L:
                row(wrows[:, 0, :], n_mix_pre, L, s_wr)
                act.dma_start(gn_col[:], gnorm[bass.ds(L, 1), :].rearrange("o p -> p o")).then_inc(s_lay, 16)
                row(sl_row[:], subln, L, s_lay)
                act.dma_start(conv_all[:], conv_p[bass.ds(L, 1), :, :].rearrange("o p (u c) -> p (o u) c", c=8)).then_inc(s_lay, 16)
                act.wait_ge(s_x0, 16)
                norm_stage(n1, L, XM, lambda n: JX[:], extra=lambda s: high(unit(L, 0)) if s == 0 else None,
                           x_ready=lambda n: act.wait_ge(fin_dve.sem, fin_dve.before(L, f"x{n}")))
                done(n1["dve"], L, f"hn{NT - 1}")
                act.dma_start(rope[:], rope_in.rearrange("p (a t) -> p a t", a=2)).then_inc(s_wr, 16)
                for u in range(HEAD_U):
                    high(unit(L, u + 1))
                    for b in range(2):
                        project_out(unit(L, u), L * N_IN + u, b, u == 0, (4 * (u % 2) + 2 * b, 4 * (u % 2) + 2 * b + 1),
                                    head_place(0, FIRST[u], b))
                act.wait_ge(s_out, L * 192 + 16)
                act.wait_ge(z_st, L * (32 * N_IN) + (16 + 32 * HEAD_U))
                load_qf(0)
                load_g(0)
                load_qk(0, False)
                load_qk(0, True)
                load_v(0)
                with act.Fori(0, NH - 1) as h:
                    mixers(L * NH + h, L, h, SLOTS)
                mixers(L * NH + (NH - 1), L, None, SLOTS_LAST)
                row(wrows[:, 0, :], n_ffn_pre, L, s_wr)
                row(wrows[:, 1, :], n_mix_post, L, s_wr)
                used(unit(L, U_BR - 1))
                act.wait_ge(s_ab, L * 48 + 48)
                for c in range(KD):
                    a(hT_hi[:, c, :], abT[:, c, :], ACT.Copy).then_inc(*ab_act.step(f"h{c}"))
                act.wait_ge(z_st, L * (32 * N_IN) + (32 * N_IN + 16))
                gates = zT[ZROWS * NH * P:, :].rearrange("(g b p) t -> b p g t", g=2, p=P)
                with act.Fori(0, 2) as i:
                    it = L * 2 + i
                    for u in range(2):
                        for b in range(2):
                            act.wait_ge(br_dve.sem, br_dve.at(it, f"tb10_{b}") if u else br_dve.before(it, f"tb11_{b}"))
                            act.dma_start(GT[:, b], gates[bass.ds(i * 4 + (2 * u + b), 1)].rearrange("o p g t -> p (o g) t")).then_inc(s_gt[b], 16)
                        high(unit(L, U_BR + u + 1, i))
                        for b in range(2):
                            act.wait_ge(s_gt[b], it * 32 + (16 * u + 16))
                            a(GT[:, b], GT[:, b], ACT.Sigmoid).then_inc(*br_act.step(f"sg{u}_{b}"))
                            done(br_dve, it, f"m{u}_{b}")
                            a(mT_hi[:, bass.ds(i * 4 + (2 * u + b), 1), :].rearrange("p o t -> p (o t)"), BT1[:], ACT.Copy)\
                                .then_inc(*br_act.step(f"mh{u}_{b}"))
                done(ab_dve, L, f"l{KD - 1}")
                act.wait_ge(s_out, L * 192 + 16)
                load_x(X, L)
                high(unit(L, U_WO + 1))
                high(unit(L, U_WO + 2))
                for t in range(NT):
                    if t < NT - 1:
                        done(wo_pe, L, f"a0_{t}")
                    else:
                        used(unit(L, U_WO + 1))
                    if t == 0:
                        done(br_dve, L * 2 + 1, "ml1_1")
                    else:
                        done(wo_act, L, f"sq{t - 1}")
                    a(JK[:], ps[:, t, :], ACT.Square, accum_out=ssy[:, t:t + 1]).then_inc(*wo_act.step(f"sq{t}"))
                high(unit(L, U_WO + 3))

                def wo_bank(t):
                    if t == 0:
                        done(wo_act, L, f"sq{NT - 1}")
                    if t < NT - 1:
                        done(wo_pe, L, f"a1_{t}")
                    else:
                        used(unit(L, U_WO + 3))

                def store_x(x):
                    def f(s):
                        if 1 <= s <= NT:
                            act.dma_start(out[(s - 1) * P:s * P, :], x[:, s - 1, :]).then_inc(s_out, 16)
                        if s == NT - 1:
                            high(unit(L, U_UP))
                    return f

                norm_stage(nr, L * 2, X, lambda n: view(ps[:], (n - 1 if n else 6) * 512, [[1, D]]), wo_bank, store_x(X))
                done(nr["dve"], L * 2, f"hn{NT - 1}")
                row(wrows[:, 1, :], n_ffn_post, L, s_wr)
                act.wait_ge(s_out, L * 192 + (16 + 96))
                with act.Fori(0, NFF // 2) as i:
                    it = L * (NFF // 2) + i
                    for u in range(2):
                        high(unit(L, U_UP + u + 1, i))
                        act.wait_ge(up_dve.sem, up_dve.before(it, f"pr{u}"))
                        done(up_dve, it, f"cp{u}")
                        for gv, C in enumerate((CG, CV)):
                            if gv == 0:
                                done(up_pe, it, f"blk{u}")
                            else:
                                used(unit(L, U_UP + u, i))
                            for hf, (t0, tn) in enumerate(HALVES):
                                a(C[:, u, t0:t0 + tn], ps[:, 4 * u + 2 * gv + hf, 0:tn], ACT.Identity,
                                  scale=conv_now[:, u, 4 * gv + 1:4 * gv + 2], bias=conv_now[:, u, 4 * gv + 3:4 * gv + 4])\
                                    .then_inc(*up_act.step(f"c{'gv'[gv]}{hf}_{u}"))
                        done(up_dve, it, f"g1r{u}")
                        a(CG[:, u, :], CG[:, u, :], ACT.Gelu_apprx_tanh).then_inc(*up_act.step(f"ge{u}"))

                def prod_high(n):
                    act.wait_ge(w_used, unit(L, U_DN + n)[0] + 1)
                    j = n % 11
                    a(PH_hi[:, n % 2], prod[:, 2 * j:2 * j + 2, :], ACT.Copy).then_inc(*dn_act.step(f"ph{n}"))

                done(up_dve, L * (NFF // 2) + (NFF // 2 - 1), "pr1")
                act.wait_ge(w_used, unit(L, U_DN)[0] + 2)
                prod_high(0)
                for n in range(22):
                    high(unit(L, U_DN + n + 1), 1024)
                    if n + 1 < 22:
                        prod_high(n + 1)
                    if n == 10:
                        for t in range(NT):
                            if t < NT - 1:
                                done(dn_pe, L, f"a0_{t}")
                            else:
                                used(unit(L, U_DN + 10))
                            if t:
                                done(dn_act, L, f"sq{t - 1}")
                            a(CG[:, 0, 0:512], ps[:, t, :], ACT.Square, accum_out=ssy[:, t:t + 1]).then_inc(*dn_act.step(f"sq{t}"))
                done(dn_dve, L, "pl21")
                act.dma_start(XM[:], out.rearrange("(t p) d -> p t d", p=P)).then_inc(s_xm, 16)
                act.dma_start(Pn[:], p_in[bass.ds(L, 1), :, :].rearrange("o (t p) c -> p (o t) c", p=P)).then_inc(s_p, 16)
                for b in range(3):
                    done(pt_pe, L, f"tr{b}")
                    a(view(PT_hi[:], b * 512, [[1, 512]]), ps[:, 6 + b % 2, :], ACT.Copy).then_inc(*pt_act.step(f"h{b}"))
                high(unit(L, U_PE + 1), 1024)

                def dn_bank(t):
                    if t < NT - 1:
                        done(dn_pe, L, f"a1_{t}")

                def e_out(c, t):
                    if t < NT - 1:
                        done(pe_pe, L, f"e{c}_{t}")
                    else:
                        used(unit(L, U_PE + c))
                    a(E[:, c, t, :], ps[:, t, :], ACT.Copy).then_inc(*pe_act.step(f"e{c}_{t}"))

                norm_stage(nr, L * 2 + 1, XM, lambda n: JX[:], dn_bank, lambda s: e_out(0, s - 1) if 1 <= s <= NT else None)
                row(wrows[:, 1, :], n_ple, L, s_wr)
                high(unit(L, U_PG))
                for t in range(NT):
                    e_out(1, t)
                for j in (1, 2, 3):
                    high(unit(L, U_PG + j))

                def store_last(t):
                    done(fin_dve, L, f"x{t}")
                    act.dma_start(out[t * P:(t + 1) * P, :], XM[:, t, :]).then_inc(s_out, 16)

                for c in range(2):
                    for t in range(NT + 1):
                        if t < NT:
                            if t < NT - 1:
                                done(pg_pe, L, f"g{c}_{t}")
                            else:
                                used(unit(L, U_PG + 1 + 2 * c))
                            n = c * NT + t
                            if n >= 2:
                                done(pg_dve, L, f"m{(n - 2) // NT}_{(n - 2) % NT}")
                            a(SG[:, t % 2, :], ps[:, t, :], ACT.Sigmoid).then_inc(*pg_act.step(f"s{c}_{t}"))
                        if t:
                            done(pg_dve, L, f"m{c}_{t - 1}")
                            if t > 1:
                                done(pg_act, L, f"q{c}_{t - 2}")
                            elif c:
                                done(pg_act, L, f"q0_{NT - 1}")
                            else:
                                done(nr["act"], L * 2 + 1, f"sqy{NT - 1}")
                            a(JK[:], E[:, c, t - 1, :], ACT.Square, accum_out=ssy[:, c * NT + t - 1:c * NT + t]).then_inc(*pg_act.step(f"q{c}_{t - 1}"))
                            if c and t > 1:
                                store_last(t - 2)
                store_last(NT - 1)
            act.wait_ge(s_out, DEPTH * 192 + 16)



def kernel(**inputs):
    import numpy as np
    import concourse.bacc as bacc
    from concourse.bass_utils import run_bass_kernel_spmd

    i = {k: np.asarray(v) for k, v in inputs.items()}
    lay = {
        "x_in": np.concatenate([i["x_prompt"][0], i["x_sample"][0]], axis=0),
        "p_in": np.concatenate([i["p_prompt"][:, 0], i["p_sample"][:, 0]], axis=1),
        "w_in": i["w_in"],
        "lb_logits": i["hgrn_lb_logits"].reshape(DEPTH, 2, NH, P).transpose(3, 2, 1, 0).reshape(P, -1),
        "gnorm": i["hgrn_gnorm"],
        "lam_in": i["diff_lambda"].reshape(1, -1),
        "subln": i["diff_subln"],
        "w_a": i["w_branch_a"], "w_b": i["w_branch_b"], "w_out": i["w_out"],
        "n_mix_pre": i["norm_mix_pre"], "n_mix_post": i["norm_mix_post"],
        "w_up": i["w_up"],
        "conv_p": np.concatenate([i["conv_w"], i["conv_b"][:, None]], axis=1).reshape(DEPTH, 4, 2, NFF, P)
        .transpose(0, 4, 3, 2, 1).reshape(DEPTH, P, NFF * 8),
        "w_down": i["w_down"],
        "n_ffn_pre": i["norm_ffn_pre"], "n_ffn_post": i["norm_ffn_post"],
        "w_ple": i["w_ple"], "w_ple_gate": i["w_ple_gate"], "n_ple": i["norm_ple"],
    }
    lay["ident_in"] = np.eye(P, dtype=np.float32)
    masks = np.zeros((P, 2, len(LEVELS), 64), np.float32)
    for l, h in enumerate(LEVELS):
        for j in range(64):
            block = j // h * 2 * h
            masks[block:block + h, 0, l, j] = 1
            masks[block + h:block + 2 * h, 1, l, j] = 1
    lay["masks_in"] = masks.reshape(P, -1)
    inv = (1.0 / (10000.0 ** (np.arange(0, DA_DH, 2) / DA_DH))).astype(np.float32)
    pos = np.concatenate([np.arange(TP), np.arange(TS)]).astype(np.float32)
    ang = (pos[:, None] * inv[None, :]).astype(np.float32)
    cos, sin = np.cos(ang), np.sin(ang)
    lay["rope_in"] = np.stack([np.concatenate([cos, cos] * 2, 1).T, np.concatenate([-sin, sin] * 2, 1).T], 1).reshape(P, -1)

    nc = bacc.Bacc("TRN2", target_bir_lowering=False, num_devices=1)
    arrays, args = {}, {}
    for name, arr in lay.items():
        arr = np.ascontiguousarray(arr)
        arrays[name + "_dram"] = arr
        args[name] = nc.dram_tensor(name + "_dram", arr.shape, mybir.dt.from_np(arr.dtype), kind="ExternalInput").ap()
    args["out"] = nc.dram_tensor("out_dram", (T, D), F32, kind="ExternalOutput").ap()
    build(nc, **args)
    y = run_bass_kernel_spmd(nc, [arrays], core_ids=[0]).results[0]["out_dram"]
    return y[None, :TP], y[None, TP:]
```
